# Optimizing a Trainium2 kernel written in Bass

```python
import jax, jax.numpy as jnp
from jax import lax
import numpy as np

D_MODEL = 2048
BATCH = 1
SEQ = 512
DEPTH = 1

D_RNN = 2048
RNN_BLOCKS = 16
RNN_BLOCK = D_RNN // RNN_BLOCKS
RNN_CONV = 4
LRU_C = 8.0
D_CONV = 2048
CONF_WIDTH = 31
MEM_LEN = 256
XA_HEADS = 4
XA_HEAD_DIM = D_MODEL // XA_HEADS
N_KEYS = 128
N_EXPERTS = N_KEYS * N_KEYS
PEER_HEADS = 8
PEER_KEY_DIM = 128
PEER_HALF = PEER_KEY_DIM // 2
PEER_TOPK = 16
PEER_HK = PEER_HEADS * PEER_TOPK
PEER_TOKEN_BLOCK = 128
DN_ALPHA = (2 * DEPTH) ** 0.25
DN_BETA = (8 * DEPTH) ** -0.25
LN_EPS = 1e-5
IN_WIDTH = 2 * D_RNN + 2 * D_CONV + 2 * D_MODEL
IN_SPLITS = (D_RNN, 2 * D_RNN, 2 * D_RNN + D_CONV, 2 * D_RNN + 2 * D_CONV, 2 * D_RNN + 2 * D_CONV + D_MODEL)

kernel_name = 'hybrid_rglru_conformer_peer_deepnorm'

def _layer_norm(x, g, b):
    xf = x.astype(jnp.float32)
    mu = jnp.mean(xf, axis=-1, keepdims=True)
    var = jnp.mean(jnp.square(xf - mu), axis=-1, keepdims=True)
    y = (xf - mu) * lax.rsqrt(var + LN_EPS)
    return (y * g + b).astype(x.dtype)

def _causal_dwconv(x, w, b):
    k = w.shape[0]
    y = lax.conv_general_dilated(x, w[:, None, :].astype(x.dtype), window_strides=(1,), padding=[(k - 1, 0)],
                                 dimension_numbers=('NWC', 'WIO', 'NWC'), feature_group_count=x.shape[-1])
    return y + b

def _rg_lru(xr, w_a, b_a, w_x, b_x, lam):
    bsz, seq, _ = xr.shape
    xb = xr.reshape(bsz, seq, RNN_BLOCKS, RNN_BLOCK)
    r = jax.nn.sigmoid(jnp.einsum('bshi,hij->bshj', xb, w_a).reshape(bsz, seq, D_RNN) + b_a)
    i = jax.nn.sigmoid(jnp.einsum('bshi,hij->bshj', xb, w_x).reshape(bsz, seq, D_RNN) + b_x)
    log_a = (-LRU_C * r.astype(jnp.float32)) * jax.nn.softplus(-lam.astype(jnp.float32))
    a = jnp.exp(log_a)
    u = jnp.sqrt(-jnp.expm1(2.0 * log_a)) * (i * xr).astype(jnp.float32)

    def combine(left, right):
        a_l, b_l = left
        a_r, b_r = right
        return a_l * a_r, a_r * b_l + b_r

    _, h = lax.associative_scan(combine, (a, u), axis=1)
    return h.astype(xr.dtype)

def _hybrid_mixer(x, w_in, b_in, rnn_conv_w, rnn_conv_b, rnn_w_a, rnn_b_a, rnn_w_x, rnn_b_x, rnn_lambda,
                  w_rnn_out, conf_dw_w, conf_dw_b, conf_ln_g, conf_ln_b, w_conf_out, b_conf_out, w_mix_out):
    proj = x @ w_in + b_in
    xr, gr, ca, cg, g_rnn, g_conf = jnp.split(proj, IN_SPLITS, axis=-1)
    xr = _causal_dwconv(xr, rnn_conv_w, rnn_conv_b)
    h = _rg_lru(xr, rnn_w_a, rnn_b_a, rnn_w_x, rnn_b_x, rnn_lambda)
    y_rnn = (h * jax.nn.gelu(gr)) @ w_rnn_out
    c = ca * jax.nn.sigmoid(cg)
    c = _causal_dwconv(c, conf_dw_w, conf_dw_b)
    c = jax.nn.silu(_layer_norm(c, conf_ln_g, conf_ln_b))
    y_conf = c @ w_conf_out + b_conf_out
    merged = jax.nn.sigmoid(g_rnn) * y_rnn + jax.nn.sigmoid(g_conf) * y_conf
    return merged @ w_mix_out

def _memory_cross_attention(x, mem, w_q, w_k, w_v, w_o):
    bsz, seq, _ = x.shape
    m = mem.shape[1]
    q = (x @ w_q).reshape(bsz, seq, XA_HEADS, XA_HEAD_DIM)
    k = (mem @ w_k).reshape(bsz, m, XA_HEADS, XA_HEAD_DIM)
    v = (mem @ w_v).reshape(bsz, m, XA_HEADS, XA_HEAD_DIM)
    s = jnp.einsum('bshd,bmhd->bhsm', q, k).astype(jnp.float32) * (XA_HEAD_DIM ** -0.5)
    p = jax.nn.softmax(s, axis=-1).astype(x.dtype)
    o = jnp.einsum('bhsm,bmhd->bshd', p, v).reshape(bsz, seq, D_MODEL)
    return o @ w_o

def _peer(x, w_q, sub_keys, expert_u, expert_v):
    bsz, seq, d = x.shape
    t = bsz * seq
    xt = x.reshape(t, d)
    q = (xt @ w_q).reshape(t, PEER_HEADS, 2, PEER_HALF).astype(jnp.float32)
    s = jnp.einsum('thcd,ckd->thck', q, sub_keys.astype(jnp.float32))
    s_top, i_top = lax.top_k(s, PEER_TOPK)
    cand = (s_top[:, :, 0, :, None] + s_top[:, :, 1, None, :]).reshape(t, PEER_HEADS, PEER_TOPK * PEER_TOPK)
    best, pos = lax.top_k(cand, PEER_TOPK)
    e1 = jnp.take_along_axis(i_top[:, :, 0], pos // PEER_TOPK, axis=-1)
    e2 = jnp.take_along_axis(i_top[:, :, 1], pos % PEER_TOPK, axis=-1)
    experts = (e1 * N_KEYS + e2).reshape(t, PEER_HK)
    gates = jax.nn.softmax(best, axis=-1).reshape(t, PEER_HK).astype(x.dtype)
    nb = t // PEER_TOKEN_BLOCK

    def token_block(args):
        xb, eb, gb = args
        u = expert_u[eb]
        v = expert_v[eb]
        act = jax.nn.gelu(jnp.einsum('td,tkd->tk', xb, u)) * gb
        return jnp.einsum('tk,tkd->td', act, v)

    out = lax.map(token_block, (xt.reshape(nb, PEER_TOKEN_BLOCK, d),
                                experts.reshape(nb, PEER_TOKEN_BLOCK, PEER_HK),
                                gates.reshape(nb, PEER_TOKEN_BLOCK, PEER_HK)))
    return out.reshape(bsz, seq, d)

def setup_inputs(seed: int = 0) -> dict:
    key = jax.random.key(seed)
    keys = iter(jax.random.split(key, 40))
    f32 = jnp.float32

    def nrm(shape, scale):
        return jax.random.normal(next(keys), (DEPTH,) + shape, f32) * scale

    def gain(n):
        return 1.0 + nrm((n,), 0.01)

    lam_u = jax.random.uniform(next(keys), (DEPTH, D_RNN), f32, minval=0.9, maxval=0.999)
    lam_p = lam_u ** (1.0 / LRU_C)
    rnn_lambda = jnp.log(lam_p) - jnp.log1p(-lam_p)
    return {
        'x': jax.random.normal(next(keys), (BATCH, SEQ, D_MODEL), f32),
        'mem': jax.random.normal(next(keys), (BATCH, MEM_LEN, D_MODEL), f32),
        'w_in': nrm((D_MODEL, IN_WIDTH), D_MODEL ** -0.5),
        'b_in': nrm((IN_WIDTH,), 0.01),
        'rnn_conv_w': nrm((RNN_CONV, D_RNN), RNN_CONV ** -0.5),
        'rnn_conv_b': nrm((D_RNN,), 0.01),
        'rnn_w_a': nrm((RNN_BLOCKS, RNN_BLOCK, RNN_BLOCK), RNN_BLOCK ** -0.5),
        'rnn_b_a': nrm((D_RNN,), 0.01),
        'rnn_w_x': nrm((RNN_BLOCKS, RNN_BLOCK, RNN_BLOCK), RNN_BLOCK ** -0.5),
        'rnn_b_x': nrm((D_RNN,), 0.01),
        'rnn_lambda': rnn_lambda,
        'w_rnn_out': nrm((D_RNN, D_MODEL), D_RNN ** -0.5 * DN_BETA),
        'conf_dw_w': nrm((CONF_WIDTH, D_CONV), CONF_WIDTH ** -0.5),
        'conf_dw_b': nrm((D_CONV,), 0.01),
        'conf_ln_g': gain(D_CONV),
        'conf_ln_b': nrm((D_CONV,), 0.01),
        'w_conf_out': nrm((D_CONV, D_MODEL), D_CONV ** -0.5 * DN_BETA),
        'b_conf_out': nrm((D_MODEL,), 0.01),
        'w_mix_out': nrm((D_MODEL, D_MODEL), D_MODEL ** -0.5 * DN_BETA),
        'ln1_g': gain(D_MODEL),
        'ln1_b': nrm((D_MODEL,), 0.01),
        'xa_w_q': nrm((D_MODEL, D_MODEL), D_MODEL ** -0.5),
        'xa_w_k': nrm((D_MODEL, D_MODEL), D_MODEL ** -0.5),
        'xa_w_v': nrm((D_MODEL, D_MODEL), D_MODEL ** -0.5 * DN_BETA),
        'xa_w_o': nrm((D_MODEL, D_MODEL), D_MODEL ** -0.5 * DN_BETA),
        'ln2_g': gain(D_MODEL),
        'ln2_b': nrm((D_MODEL,), 0.01),
        'peer_w_q': nrm((D_MODEL, PEER_HEADS * PEER_KEY_DIM), D_MODEL ** -0.5),
        'peer_sub_keys': nrm((2, N_KEYS, PEER_HALF), PEER_HALF ** -0.5),
        'peer_u': nrm((N_EXPERTS, D_MODEL), D_MODEL ** -0.5),
        'peer_v': nrm((N_EXPERTS, D_MODEL), DN_BETA),
        'ln3_g': gain(D_MODEL),
        'ln3_b': nrm((D_MODEL,), 0.01),
    }

def reference(x, mem, w_in, b_in, rnn_conv_w, rnn_conv_b, rnn_w_a, rnn_b_a, rnn_w_x, rnn_b_x, rnn_lambda,
              w_rnn_out, conf_dw_w, conf_dw_b, conf_ln_g, conf_ln_b, w_conf_out, b_conf_out, w_mix_out,
              ln1_g, ln1_b, xa_w_q, xa_w_k, xa_w_v, xa_w_o, ln2_g, ln2_b,
              peer_w_q, peer_sub_keys, peer_u, peer_v, ln3_g, ln3_b):
    for l in range(DEPTH):
        mix = _hybrid_mixer(x, w_in[l], b_in[l], rnn_conv_w[l], rnn_conv_b[l], rnn_w_a[l], rnn_b_a[l],
                            rnn_w_x[l], rnn_b_x[l], rnn_lambda[l], w_rnn_out[l], conf_dw_w[l], conf_dw_b[l],
                            conf_ln_g[l], conf_ln_b[l], w_conf_out[l], b_conf_out[l], w_mix_out[l])
        x = _layer_norm(DN_ALPHA * x + mix, ln1_g[l], ln1_b[l])
        xa = _memory_cross_attention(x, mem, xa_w_q[l], xa_w_k[l], xa_w_v[l], xa_w_o[l])
        x = _layer_norm(DN_ALPHA * x + xa, ln2_g[l], ln2_b[l])
        ff = _peer(x, peer_w_q[l], peer_sub_keys[l], peer_u[l], peer_v[l])
        x = _layer_norm(DN_ALPHA * x + ff, ln3_g[l], ln3_b[l])
    return x


_drawn_inputs = setup_inputs


def setup_inputs(seed=0):
    import zlib

    import numpy as np

    out = dict(_drawn_inputs(seed))
    spreads = {}
    factors = {'b_in': 2.978,
     'rnn_conv_b': 2.891,
     'rnn_b_a': 194.875,
     'rnn_b_x': 136.234,
     'conf_dw_b': 5.005,
     'conf_ln_g': 17.062,
     'conf_ln_b': 21.237,
     'b_conf_out': 11.308,
     'ln3_g': 189.479,
     'ln3_b': 181.701}
    for name, (base, spread) in spreads.items():
        noise = np.random.default_rng([zlib.crc32(name.encode()), seed]).standard_normal(out[name].shape)
        drawn = base * np.exp(spread * noise) if base else spread * noise
        out[name] = __import__('jax').numpy.asarray(drawn.astype(out[name].dtype))
    for name, factor in factors.items():
        out[name] = (out[name] * factor).astype(out[name].dtype)
    return out
```

```python
from contextlib import ExitStack

import concourse.bass as bass
from concourse import mybir

F32 = mybir.dt.float32
F32R = mybir.dt.float32r
U32 = mybir.dt.uint32
ACT = mybir.ActivationFunctionType
ALU = mybir.AluOpType
AX_X = mybir.AxisListType.X

P = 128
D = 2048
T = 512
KC = D // P
HALF = KC // 2
WH = HALF * P
M = 256
RNN_K, CONF_K = 4, 31
HEADS, HD = 4, 512
HC = HD // P
PH, NK, TOPK = 8, 128, 16
HK = PH * TOPK
TT = T // P
ALPHA = 2.0 ** 0.25
EPS = 1e-5
GELU_C = 0.7978845608028654
RING = 8

COLS = {}
_at = 0
for _name, _n in (("b_in", 6 * KC), ("rnn_w", RNN_K * KC), ("rnn_b", KC), ("b_a", KC), ("b_x", KC), ("lam", KC),
                  ("conf_w", CONF_K * KC), ("conf_b", KC), ("conf_g", KC), ("conf_be", KC), ("b_out", KC),
                  ("g1", KC), ("be1", KC), ("g2", KC), ("be2", KC)):
    COLS[_name] = _at
    _at += _n
NCOLS = _at

STAGE_CHUNKS = (("kv", 2 * KC), ("glu", 2 * KC), ("conf", 2 * KC), ("lru", 2 * KC), ("rnn", 2 * KC),
                ("mix", KC), ("att", KC), ("xo", KC), ("pq", PH))
BASE = {}
_at = 0
for _name, _n in STAGE_CHUNKS:
    BASE[_name] = 2 * _at
    _at += _n
HALVES = 2 * _at
AHEAD_LOAD, AHEAD_SPLIT = 4, 2


class Steps:

    def __init__(self, sem, names):
        self.sem, self.names, self.at = sem, names.split(), 0

    def one(self, name):
        assert self.names[self.at % len(self.names)] == name, (name, self.names[self.at % len(self.names)])
        self.at += 1
        return 1

    def now(self, name, i=0):
        return i * len(self.names) + (len(self.names) + self.names.index(name) + 1)

    def before(self, name, i=0):
        return i * len(self.names) + (self.names.index(name) + 1)

    def all(self, n):
        return (n + 1) * len(self.names)


def build(nc, wstream, x_t, mem_t, vecs, gates_w, ident_d, keys_t, peer_u, peer_v, ln3, out, debug=None):
    top = ExitStack()
    with top:
        def sb(name, shape, dt=F32, ctx=top):
            return ctx.enter_context(nc.sbuf_tensor(name, shape, dt))

        def sem(name, ctx=top):
            return ctx.enter_context(nc.semaphore(name))

        psum = top.enter_context(nc.psum_tensor("psum", [P, 8, 512], F32))
        vec = sb("vec", [P, NCOLS])
        hb_in = sb("hb_in", [P, 6 * KC])
        hb_ax = sb("hb_ax", [P, 2 * KC])
        nsp = sb("nsp", [P, KC])
        hcw = sb("hcw", [P, CONF_K * KC])
        ident = sb("ident", [P, P])
        ones = sb("ones", [P, P])
        zeros = sb("zeros", [P, WH])
        kv_d = nc.dram_tensor("kv_scratch", (2 * KC, P, M), F32).ap()
        conf_d = nc.dram_tensor("conf_scratch", (KC, P, T), F32).ap()
        x2_d = nc.dram_tensor("x2_scratch", (TT, P, D), F32).ap()

        loaded = [sem(f"weights_loaded{i}") for i in range(4)]
        hi_made = sem("weights_hi_made")
        split = sem("weights_split")
        raw_free = sem("weights_raw_free")
        used = sem("weights_used")
        alone = sem("wait_passed")

        def hold(eng, s, value):
            eng.wait_ge(s, value)
            eng.sem_inc(alone, 1)

        res = sb("res", [P, KC * T])
        wctx = top.enter_context(ExitStack())
        w_raw = [sb(f"w_raw{i}", [P, WH], ctx=wctx) for i in range(2)]
        w_hi = [sb(f"w_hi{i}", [P, WH], F32R, ctx=wctx) for i in range(2)]
        w_lo = [sb(f"w_lo{i}", [P, WH], F32R, ctx=wctx) for i in range(2)]
        stream = wstream.rearrange("h p n -> h p n")

        def load_half(sp, g, s):
            hold(sp, raw_free, g + 1)
            sp.dma_start(w_raw[s % 2][:, :], stream[bass.ds(g, 1)].rearrange("a p n -> (a p) n")).then_inc(loaded[s], 16)

        def split_half(pool, g, round_, s):
            hold(pool, loaded[s], round_ * 16 + 16)
            hold(pool, used, g + 1)
            pool.tensor_tensor(w_hi[s % 2][:, :], w_raw[s % 2][:, :], zeros[:, :], ALU.add).then_inc(hi_made, 1)
            pool.wait_ge(hi_made, g + 1)
            pool.tensor_tensor(w_lo[s % 2][:, :], w_raw[s % 2][:, :], w_hi[s % 2][:, :].bitcast(F32),
                               ALU.subtract).then_inc(split, 1)
            pool.wait_ge(split, g + 1)
            pool.sem_inc(raw_free, 1)

        def loads(sp, name, n_chunks):
            first, last = BASE[name] + AHEAD_LOAD, min(BASE[name] + 2 * n_chunks + AHEAD_LOAD, HALVES)
            with sp.Fori(0, (last - first) // 4) as i:
                for s in range(4):
                    load_half(sp, i * 4 + (first + s), s)

        def splits(pool, name, n_chunks):
            first, last = BASE[name] + AHEAD_SPLIT, min(BASE[name] + 2 * n_chunks + AHEAD_SPLIT, HALVES)
            n = (last - first) // 4
            with pool.Fori(0, n) as i:
                for s in range(4):
                    slot = (AHEAD_SPLIT + s) % 4
                    split_half(pool, i * 4 + (first + s), i + (first + s) // 4, slot)
            for g in range(first + 4 * n, last):
                split_half(pool, g, g // 4, g % 4)

        def gemm(pe, bank, act_hi, act_lo, g, n=T, done=None):
            for half in range(2):
                pe.wait_ge(split, g + (half + 1))
                for k in range(HALF):
                    kk = half * HALF + k
                    wh, wl = (w[half][:, k * P:(k + 1) * P] for w in (w_hi, w_lo))
                    xh, xl = (a[:, kk * n:(kk + 1) * n] for a in (act_hi, act_lo))
                    pe.matmul(psum[:, bank, 0:n], wh, xh, start=(kk == 0), stop=False)
                    pe.matmul(psum[:, bank, 0:n], wh, xl, start=False, stop=False)
                    last = pe.matmul(psum[:, bank, 0:n], wl, xh, start=False, stop=(kk == KC - 1))
                last.then_inc(used, 1)

        def gemm_done(eng, g):
            eng.wait_ge(used, g + 4)

        def chunk(t, c, n=T):
            return t[:, bass.ts(c, n)]

        def col(name, c, k=0, t=None):
            return (vec if t is None else t)[:, bass.ds(c + ((COLS[name] if t is None else 0) + k), 1)]

        a_hi = sb("a_hi", [P, KC * T], F32R, ctx=wctx)
        a_lo = sb("a_lo", [P, KC * T], F32R, ctx=wctx)
        x_hi = sb("x_hi", [P, KC * T], F32R, ctx=wctx)
        x_lo = sb("x_lo", [P, KC * T], F32R, ctx=wctx)
        tile = [res[:, k * T:(k + 1) * T] for k in range(KC)]

        const_in, c_d, c_a, c_p = sem("const_in"), sem("c_dve"), sem("c_act"), sem("c_pool")
        mem_in = sem("mem_in")
        with nc.Block() as block:
            @block.sync
            def _(sp):
                sp.dma_start(vec[:, :], vecs).then_inc(const_in, 16)
                sp.dma_start(ident[:, :], ident_d).then_inc(const_in, 16)
                sp.dma_start(res[:, 0:KC * M], mem_t).then_inc(mem_in, 16)
                sp.wait_ge(raw_free, 2)
                for g in range(2):
                    sp.dma_start(w_raw[g][:, :], stream[g]).then_inc(loaded[g], 16)
                for g in range(2, AHEAD_LOAD):
                    sp.wait_ge(raw_free, g + 1)
                    sp.dma_start(w_raw[g % 2][:, :], stream[g]).then_inc(loaded[g], 16)

            @block.gpsimd
            def _(pool):
                pool.sem_inc(raw_free, 2)
                pool.memset(zeros[:, :], 0.0).then_inc(c_p, 1)
                pool.memset(ones[:, :], 1.0 / D).then_inc(c_p, 1)
                pool.wait_ge(c_p, 2)
                for g in range(AHEAD_SPLIT):
                    split_half(pool, g, 0, g)

            @block.tensor
            def _(pe):
                pe.sem_inc(used, 2)

            @block.scalar
            def _(act):
                act.wait_ge(c_d, 1)
                act.activation(tile[8][:, 0:KC], tile[9][:, 0:KC], ACT.Exp, scale=-1.0).then_inc(c_a, 1)
                act.wait_ge(c_d, 3)
                act.activation(tile[11][:, 0:KC], tile[10][:, 0:KC], ACT.Ln).then_inc(c_a, 1)
                act.wait_ge(mem_in, 16)
                act.activation(x_hi[:, 0:KC * M], res[:, 0:KC * M], ACT.Copy).then_inc(c_a, 1)

            @block.vector
            def _(dve):
                n = 0

                def done(ins):
                    nonlocal n
                    n += 1
                    ins.then_inc(c_d, 1)
                    dve.wait_ge(c_d, n)

                dve.wait_ge(const_in, 32)
                lam = vec[:, COLS["lam"]:COLS["lam"] + KC]
                e, ab, w, lw, t1 = (tile[k][:, 0:KC] for k in (8, 9, 10, 11, 12))
                t2, t3, t4 = (tile[k][:, 0:KC] for k in (13, 14, 15))
                done(dve.scalar_tensor_tensor(ab, lam, -1.0, lam, ALU.mult, ALU.max))
                dve.wait_ge(c_a, 1)
                done(dve.tensor_scalar(w, e, 1.0, None, ALU.add))
                done(dve.tensor_scalar(t1, w, -1.0, None, ALU.add))
                done(dve.tensor_scalar(t2, t1, 0.0, None, ALU.is_equal))
                done(dve.tensor_tensor(t1, t1, t2, ALU.add))
                done(dve.reciprocal(t3, t1))
                dve.wait_ge(c_a, 2)
                done(dve.tensor_tensor(lw, lw, t2, ALU.add))
                done(dve.tensor_tensor(lw, lw, t3, ALU.mult))
                done(dve.tensor_tensor(lw, lw, e, ALU.mult))
                done(dve.tensor_scalar(t4, lam, -1.0, 0.0, ALU.mult, ALU.max))
                done(dve.tensor_tensor(lw, lw, t4, ALU.add))
                done(dve.tensor_scalar(nsp[:, :], lw, -4.0, None, ALU.mult))
                done(dve.tensor_scalar(hb_in[:, :], vec[:, 0:6 * KC], 0.5, None, ALU.mult))
                done(dve.tensor_scalar(hb_ax[:, :], vec[:, COLS["b_a"]:COLS["b_a"] + 2 * KC], 0.5, None, ALU.mult))
                done(dve.tensor_scalar(hcw[:, :], vec[:, COLS["conf_w"]:COLS["conf_w"] + CONF_K * KC], 0.5, None,
                                       ALU.mult))
                dve.wait_ge(c_a, 3)
                done(dve.tensor_tensor(x_lo[:, 0:KC * M], res[:, 0:KC * M], x_hi[:, 0:KC * M].bitcast(F32),
                                       ALU.subtract))

        with ExitStack() as ctx:
            kv_out = sem("kv_out", ctx)
            A = Steps(sem("kv_evacuated", ctx), "copy0 copy1")
            sent = [sem(f"kv_sent{i}", ctx) for i in range(2)]
            with nc.Block() as block:
                @block.sync
                def _(sp):
                    loads(sp, "kv", 2 * KC)

                @block.gpsimd
                def _(pool):
                    splits(pool, "kv", 2 * KC)

                @block.tensor
                def _(pe):
                    with pe.Fori(0, KC) as i:
                        for b in range(2):
                            pe.wait_ge(A.sem, A.before(f"copy{b}", i))
                            gemm(pe, b, x_hi, x_lo, i * 4 + (BASE["kv"] + 2 * b), M)

                @block.scalar
                def _(act):
                    act.sem_inc(A.sem, 2)
                    for b in range(2):
                        act.sem_inc(sent[b], 16)
                    with act.Fori(0, KC) as i:
                        for b in range(2):
                            act.wait_ge(sent[b], i * 16 + 16)
                            gemm_done(act, i * 4 + (BASE["kv"] + 2 * b))
                            act.activation(tile[8 + b][:, 0:M], psum[:, b, 0:M], ACT.Copy)\
                               .then_inc(A.sem, A.one(f"copy{b}"))
                            hold(act, A.sem, A.now(f"copy{b}", i))
                            act.dma_start(kv_d[bass.ds(i * 2 + b, 1)].rearrange("a p n -> (a p) n"),
                                          tile[8 + b][:, 0:M]).then_inc(sent[b], 16)
                    for b in range(2):
                        act.wait_ge(sent[b], (KC + 1) * 16)

        def split_x(read_scale, from_dram):
            with ExitStack() as ctx:
                arrived = sem("x_arrived", ctx)
                hi_done = sem("x_hi_done", ctx)
                lo_done = sem("x_lo_done", ctx)
                with nc.Block() as block:
                    @block.sync
                    def _(sp):
                        if from_dram:
                            sp.dma_start(res[:, :], x_t).then_inc(arrived, 16)

                    Q = KC * T // 4
                    @block.scalar
                    def _(act):
                        if from_dram:
                            act.wait_ge(arrived, 16)
                        for q in range(4):
                            act.activation(x_hi[:, q * Q:(q + 1) * Q], res[:, q * Q:(q + 1) * Q], ACT.Copy,
                                           scale=read_scale).then_inc(hi_done, 1)

                    @block.vector
                    def _(dve):
                        for q in range(4):
                            dve.wait_ge(hi_done, q + 1)
                            dve.scalar_tensor_tensor(x_lo[:, q * Q:(q + 1) * Q], res[:, q * Q:(q + 1) * Q],
                                                     read_scale, x_hi[:, q * Q:(q + 1) * Q].bitcast(F32),
                                                     ALU.mult, ALU.subtract).then_inc(lo_done, 1)
                        dve.wait_ge(lo_done, 4)

        split_x(1.0, True)

        with ExitStack() as ctx0:
            total = sb("total", [P, T], ctx=wctx)
            PAD = CONF_K - 1
            with ExitStack() as ctx:
                th = sb("glu_th", [P, T], ctx=ctx)
                cab = sb("glu_ca", [P, T], ctx=ctx)
                xp = sb("glu_padded", [P, PAD + T], ctx=ctx)
                odd = sb("glu_odd", [P, T], ctx=ctx)
                A = Steps(sem("glu_act", ctx), "th ca")
                V = Steps(sem("glu_dve", ctx), "glu " + " ".join(f"tap{k}" for k in range(CONF_K)) + " join total")
                setup = sem("glu_setup", ctx)
                with nc.Block() as block:
                    @block.sync
                    def _(sp):
                        loads(sp, "glu", 2 * KC)

                    @block.gpsimd
                    def _(pool):
                        splits(pool, "glu", 2 * KC)

                    @block.tensor
                    def _(pe):
                        with pe.Fori(0, KC) as c:
                            pe.wait_ge(A.sem, A.before("th", c))
                            gemm(pe, 0, x_hi, x_lo, c * 4 + BASE["glu"])
                            pe.wait_ge(A.sem, A.before("ca", c))
                            gemm(pe, 1, x_hi, x_lo, c * 4 + (BASE["glu"] + 2))

                    @block.scalar
                    def _(act):
                        act.sem_inc(A.sem, len(A.names))
                        with act.Fori(0, KC) as c:
                            hold(act, V.sem, V.before("glu", c))
                            gemm_done_alone = hold(act, used, c * 4 + (BASE["glu"] + 4))
                            act.activation(th[:, :], psum[:, 0, :], ACT.Tanh, bias=col("", c, 3 * KC, hb_in),
                                           scale=0.5).then_inc(A.sem, A.one("th"))
                            hold(act, used, c * 4 + (BASE["glu"] + 6))
                            act.activation(cab[:, :], psum[:, 1, :], ACT.Identity, bias=col("b_in", c, 2 * KC))\
                               .then_inc(A.sem, A.one("ca"))

                    @block.vector
                    def _(dve):
                        dve.sem_inc(V.sem, len(V.names))
                        dve.memset(xp[:, 0:PAD], 0.0).then_inc(setup, 1)
                        dve.memset(total[:, :], 0.0).then_inc(setup, 1)
                        dve.wait_ge(setup, 2)
                        with dve.Fori(0, KC) as c:
                            even = chunk(res, c)
                            dve.wait_ge(V.sem, V.before("join", c))
                            dve.wait_ge(A.sem, A.now("ca", c))
                            dve.scalar_tensor_tensor(xp[:, PAD:PAD + T], th[:, :], 1.0, cab[:, :], ALU.add, ALU.mult)\
                               .then_inc(V.sem, V.one("glu"))
                            dve.wait_ge(V.sem, V.now("glu", c))
                            for k in range(CONF_K):
                                acc = odd[:, :] if k % 2 else even
                                tap = col("", c, k * KC, hcw)
                                if k == 0:
                                    ins = dve.tensor_scalar(acc, xp[:, 0:T], tap, col("conf_b", c), ALU.mult, ALU.add)
                                elif k == 1:
                                    ins = dve.tensor_scalar(acc, xp[:, 1:1 + T], tap, None, ALU.mult)
                                else:
                                    dve.wait_ge(V.sem, V.now(f"tap{k - 2}", c))
                                    ins = dve.scalar_tensor_tensor(acc, xp[:, k:k + T], tap, acc, ALU.mult, ALU.add)
                                ins.then_inc(V.sem, V.one(f"tap{k}"))
                            dve.wait_ge(V.sem, V.now(f"tap{CONF_K - 1}", c))
                            dve.tensor_tensor(even, even, odd[:, :], ALU.add).then_inc(V.sem, V.one("join"))
                            dve.wait_ge(V.sem, V.now("join", c))
                            dve.tensor_tensor(total[:, :], total[:, :], even, ALU.add).then_inc(V.sem, V.one("total"))
                        dve.wait_ge(V.sem, V.all(KC))

        mean = sb("mean", [P, T], ctx=wctx)
        rstd = sb("rstd", [P, T], ctx=wctx)
        tile_in = sb("tile_in", [P, T], ctx=wctx)

        def layer_norm(name, g_name, b_name, silu, transposed=False):
            with ExitStack() as ctx:
                s = lambda n: sem(f"{name}_{n}", ctx)
                sq = [sb(f"{name}_sq{i}", [P, T], ctx=ctx) for i in range(1)]
                y = sb(f"{name}_y", [P, T], ctx=ctx)
                z = tile_in
                pe_sem, act_sem, dve_sem = s("pe"), s("act"), s("dve")
                A = Steps(s("square"), "sq")
                V = Steps(s("centre"), "sub add")
                if silu:
                    A3, V3 = Steps(s("act3"), "tanh hi"), Steps(s("dve3"), "scale affine gate lo")
                elif transposed:
                    A3, V3 = Steps(s("act3"), "hi out"), Steps(s("dve3"), "scale affine lo")
                else:
                    A3, V3 = Steps(s("act3"), "hi"), Steps(s("dve3"), "scale affine lo")
                T3 = Steps(s("pe3"), "turn")
                sent = s("sent")
                with nc.Block() as block:
                    @block.tensor
                    def _(pe):
                        pe.matmul(psum[:, 6, :], ones[:, :], total[:, :], start=True, stop=True).then_inc(pe_sem, 1)
                        pe.wait_ge(dve_sem, 2)
                        pe.matmul(psum[:, 7, :], ones[:, :], total[:, :], start=True, stop=True).then_inc(pe_sem, 1)
                        if transposed:
                            with pe.Fori(0, KC) as c:
                                pe.wait_ge(V3.sem, V3.now("affine", c))
                                pe.wait_ge(A3.sem, A3.before("out", c))
                                for t in range(TT):
                                    ins = pe.transpose(psum[:, 5, t * P:(t + 1) * P], y[:, t * P:(t + 1) * P], ident[:, :])
                                ins.then_inc(T3.sem, T3.one("turn"))

                    @block.scalar
                    def _(act):
                        act.sem_inc(A.sem, 1)
                        act.sem_inc(A3.sem, len(A3.names))
                        with act.Fori(0, KC) as c:
                            hold(act, V.sem, V.now("sub", c))
                            hold(act, V.sem, V.before("add", c))
                            act.activation(sq[0][:, :], chunk(res, c), ACT.Square).then_inc(A.sem, A.one("sq"))
                        act.wait_ge(dve_sem, 3)
                        act.activation(rstd[:, :], rstd[:, :], ACT.Sqrt).then_inc(act_sem, 1)
                        if transposed:
                            act.sem_inc(sent, 16)
                        with act.Fori(0, KC) as c:
                            if silu:
                                hold(act, V3.sem, V3.now("affine", c))
                                act.activation(z[:, :], y[:, :], ACT.Tanh, scale=0.5).then_inc(A3.sem, A3.one("tanh"))
                                hold(act, V3.sem, V3.now("gate", c))
                                act.activation(chunk(a_hi, c), y[:, :], ACT.Copy, scale=0.5)\
                                   .then_inc(A3.sem, A3.one("hi"))
                            else:
                                hold(act, V3.sem, V3.now("affine", c))
                                act.activation(chunk(a_hi, c), y[:, :], ACT.Copy).then_inc(A3.sem, A3.one("hi"))
                            if transposed:
                                hold(act, sent, c * 16 + 16)
                                act.wait_ge(pe_sem, 2)
                                act.wait_ge(T3.sem, c + 1)
                                act.activation(z[:, :], psum[:, 5, :], ACT.Copy).then_inc(A3.sem, A3.one("out"))
                                hold(act, A3.sem, A3.now("out", c))
                                act.dma_start(x2_d[:, :, bass.ts(c, P)].rearrange("t p n -> p t n"),
                                              z[:, :].rearrange("p (t n) -> p t n", t=TT)).then_inc(sent, 16)
                        if transposed:
                            act.wait_ge(sent, (KC + 1) * 16)

                    @block.vector
                    def _(dve):
                        dve.sem_inc(V.sem, 2)
                        dve.sem_inc(V3.sem, len(V3.names))
                        dve.wait_ge(pe_sem, 1)
                        dve.tensor_copy(mean[:, :], psum[:, 6, :]).then_inc(dve_sem, 1)
                        dve.memset(total[:, :], 0.0).then_inc(act_sem, 1)
                        dve.wait_ge(dve_sem, 1)
                        dve.wait_ge(act_sem, 1)
                        with dve.Fori(0, KC) as c:
                            dve.tensor_tensor(chunk(res, c), chunk(res, c), mean[:, :], ALU.subtract)\
                               .then_inc(V.sem, V.one("sub"))
                            dve.wait_ge(A.sem, A.now("sq", c))
                            dve.wait_ge(V.sem, V.before("add", c))
                            dve.tensor_tensor(total[:, :], total[:, :], sq[0][:, :], ALU.add)\
                               .then_inc(V.sem, V.one("add"))
                        dve.wait_ge(V.sem, V.all(KC))
                        dve.sem_inc(dve_sem, 1)
                        dve.wait_ge(pe_sem, 2)
                        dve.tensor_scalar(rstd[:, :], psum[:, 7, :], EPS, None, ALU.add).then_inc(dve_sem, 1)
                        dve.wait_ge(act_sem, 2)
                        dve.reciprocal(rstd[:, :], rstd[:, :]).then_inc(dve_sem, 1)
                        dve.wait_ge(dve_sem, 4)
                        with dve.Fori(0, KC) as c:
                            r = chunk(res, c)
                            dve.tensor_tensor(r, r, rstd[:, :], ALU.mult).then_inc(V3.sem, V3.one("scale"))
                            dve.wait_ge(V3.sem, V3.now("scale", c))
                            dve.wait_ge(V3.sem, V3.before("lo", c))
                            dve.wait_ge(A3.sem, A3.before("hi", c))
                            if transposed:
                                dve.wait_ge(A3.sem, A3.before("out", c))
                            dve.tensor_scalar(y[:, :], r, col(g_name, c), col(b_name, c), ALU.mult, ALU.add)\
                               .then_inc(V3.sem, V3.one("affine"))
                            if silu:
                                dve.wait_ge(V3.sem, V3.now("affine", c))
                                dve.wait_ge(A3.sem, A3.now("tanh", c))
                                dve.scalar_tensor_tensor(y[:, :], z[:, :], 1.0, y[:, :], ALU.add, ALU.mult)\
                                   .then_inc(V3.sem, V3.one("gate"))
                                dve.wait_ge(V3.sem, V3.now("gate", c))
                                half = 0.5
                            else:
                                half = 1.0
                            dve.wait_ge(A3.sem, A3.now("hi", c))
                            dve.wait_ge(V3.sem, V3.now("affine", c))
                            dve.scalar_tensor_tensor(chunk(a_lo, c), y[:, :], half, chunk(a_hi, c).bitcast(F32),
                                                     ALU.mult, ALU.subtract).then_inc(V3.sem, V3.one("lo"))
                        dve.wait_ge(V3.sem, V3.all(KC))

        layer_norm("conf_ln", "conf_g", "conf_be", True)

        def gated_out(name, gate_col, add_conf):
            with ExitStack() as ctx:
                th = sb(f"{name}_th", [P, T], ctx=ctx)
                yb = sb(f"{name}_y", [P, T], ctx=ctx)
                A = Steps(sem(f"{name}_act", ctx), "th y")
                V = Steps(sem(f"{name}_dve", ctx), "gate join")
                moved = sem(f"{name}_moved", ctx)
                with nc.Block() as block:
                    @block.sync
                    def _(sp):
                        loads(sp, name, 2 * KC)

                    @block.gpsimd
                    def _(pool):
                        splits(pool, name, 2 * KC)

                    @block.tensor
                    def _(pe):
                        with pe.Fori(0, KC) as c:
                            pe.wait_ge(A.sem, A.before("th", c))
                            gemm(pe, 0, x_hi, x_lo, c * 4 + BASE[name])
                            pe.wait_ge(A.sem, A.before("y", c))
                            gemm(pe, 1, a_hi, a_lo, c * 4 + (BASE[name] + 2))

                    @block.scalar
                    def _(act):
                        act.sem_inc(A.sem, 2)
                        if not add_conf:
                            act.sem_inc(moved, 16)
                        with act.Fori(0, KC) as c:
                            hold(act, V.sem, V.before("join", c))
                            if add_conf:
                                act.dma_start(tile_in[:, :], conf_d[bass.ds(c, 1)].rearrange("a p n -> (a p) n"))\
                                   .then_inc(moved, 16)
                            hold(act, used, c * 4 + (BASE[name] + 4))
                            act.activation(th[:, :], psum[:, 0, :], ACT.Tanh, bias=col("", c, gate_col * KC, hb_in),
                                           scale=0.5).then_inc(A.sem, A.one("th"))
                            hold(act, used, c * 4 + (BASE[name] + 6))
                            if add_conf:
                                act.activation(yb[:, :], psum[:, 1, :], ACT.Copy).then_inc(A.sem, A.one("y"))
                            else:
                                act.activation(yb[:, :], psum[:, 1, :], ACT.Identity, bias=col("b_out", c))\
                                   .then_inc(A.sem, A.one("y"))
                                hold(act, V.sem, V.now("join", c))
                                act.dma_start(conf_d[bass.ds(c, 1)].rearrange("a p n -> (a p) n"), tile_in[:, :])\
                                   .then_inc(moved, 16)
                        act.wait_ge(moved, (KC if add_conf else KC + 1) * 16)

                    @block.vector
                    def _(dve):
                        dve.sem_inc(V.sem, 2)
                        with dve.Fori(0, KC) as c:
                            dve.wait_ge(A.sem, A.now("y", c))
                            dve.wait_ge(moved, c * 16 + 16)
                            if add_conf:
                                dve.scalar_tensor_tensor(yb[:, :], th[:, :], 1.0, yb[:, :], ALU.add, ALU.mult)\
                                   .then_inc(V.sem, V.one("gate"))
                                dve.wait_ge(V.sem, V.now("gate", c))
                                dve.tensor_tensor(chunk(res, c), yb[:, :], tile_in[:, :], ALU.add)\
                                   .then_inc(V.sem, V.one("join"))
                            else:
                                dve.scalar_tensor_tensor(tile_in[:, :], th[:, :], 1.0, yb[:, :], ALU.add, ALU.mult)\
                                   .then_inc(V.sem, V.one("gate"))
                                dve.wait_ge(V.sem, V.now("gate", c))
                                dve.sem_inc(V.sem, V.one("join"))
                        dve.wait_ge(V.sem, V.all(KC))

        gated_out("conf", 5, False)

        with ExitStack() as ctx:
            (g, q, xc, tr, ti, la, av, tv, den, rden, m2, u, h, gt, r, sqv) = tile
            xp = sb("lru_padded", [P, RNN_K - 1 + T], ctx=ctx)
            gw = sb("lru_gates", [P, 2 * P], ctx=ctx)
            A = Steps(sem("lru_act", ctx), "xr gr thr thi exp tanh gelu sqrt hi")
            V = Steps(sem("lru_dve", ctx), "c0 c1 c2 c3 g2 g3 g4 la ix den rden m2 gate u h r lo")
            E = Steps(sem("lru_pe", ctx), "gates")
            gates_in = sem("lru_gates_in", ctx)
            setup = sem("lru_setup", ctx)
            with nc.Block() as block:
                @block.sync
                def _(sp):
                    first = BASE["lru"] + AHEAD_LOAD
                    with sp.Fori(0, KC) as c:
                        hold(sp, E.sem, c + 1)
                        sp.dma_start(gw[:, :], gates_w[bass.ds(c, 1)].rearrange("a p n -> (a p) n"))\
                          .then_inc(gates_in, 16)
                        for s in range(4):
                            load_half(sp, c * 4 + (first + s), s)

                @block.gpsimd
                def _(pool):
                    splits(pool, "lru", 2 * KC)

                @block.tensor
                def _(pe):
                    pe.sem_inc(E.sem, 1)
                    with pe.Fori(0, KC) as c:
                        pe.wait_ge(A.sem, A.before("xr", c))
                        gemm(pe, 0, x_hi, x_lo, c * 4 + BASE["lru"])
                        pe.wait_ge(A.sem, A.before("gr", c))
                        gemm(pe, 1, x_hi, x_lo, c * 4 + (BASE["lru"] + 2))
                        pe.wait_ge(gates_in, c * 16 + 16)
                        pe.wait_ge(V.sem, V.now("c3", c))
                        pe.wait_ge(A.sem, A.before("thi", c))
                        for j in range(2):
                            ins = pe.matmul(psum[:, 2 + j, :], gw[:, j * P:(j + 1) * P], xc, start=True, stop=True)
                        ins.then_inc(E.sem, E.one("gates"))

                @block.scalar
                def _(act):
                    act.sem_inc(A.sem, len(A.names))
                    with act.Fori(0, KC) as c:
                        hold(act, used, c * 4 + (BASE["lru"] + 4))
                        hold(act, V.sem, V.before("c3", c))
                        act.activation(xp[:, 3:3 + T], psum[:, 0, :], ACT.Identity, bias=col("b_in", c))\
                           .then_inc(A.sem, A.one("xr"))
                        hold(act, used, c * 4 + (BASE["lru"] + 6))
                        hold(act, V.sem, V.before("gate", c))
                        act.activation(g, psum[:, 1, :], ACT.Identity, bias=col("b_in", c, KC))\
                           .then_inc(A.sem, A.one("gr"))
                        hold(act, E.sem, c + 2)
                        hold(act, V.sem, V.before("lo", c))
                        act.activation(tr, psum[:, 2, :], ACT.Tanh, bias=col("", c, 0, hb_ax), scale=0.5)\
                           .then_inc(A.sem, A.one("thr"))
                        act.activation(ti, psum[:, 3, :], ACT.Tanh, bias=col("", c, KC, hb_ax), scale=0.5)\
                           .then_inc(A.sem, A.one("thi"))
                        act.wait_ge(V.sem, V.now("la", c))
                        act.activation(av, la, ACT.Exp).then_inc(A.sem, A.one("exp"))
                        act.activation(tv, la, ACT.Tanh).then_inc(A.sem, A.one("tanh"))
                        act.activation(gt, q, ACT.Tanh, scale=GELU_C).then_inc(A.sem, A.one("gelu"))
                        act.wait_ge(V.sem, V.now("m2", c))
                        act.activation(sqv, m2, ACT.Sqrt).then_inc(A.sem, A.one("sqrt"))
                        hold(act, V.sem, V.now("r", c))
                        act.activation(chunk(a_hi, c), r, ACT.Copy).then_inc(A.sem, A.one("hi"))

                @block.vector
                def _(dve):
                    dve.sem_inc(V.sem, len(V.names))
                    dve.memset(xp[:, 0:3], 0.0).then_inc(setup, 1)
                    dve.wait_ge(setup, 1)
                    with dve.Fori(0, KC) as c:
                        def after(name):
                            dve.wait_ge(V.sem, V.now(name, c))

                        def step(name, ins):
                            ins.then_inc(V.sem, V.one(name))

                        dve.wait_ge(A.sem, A.now("xr", c))
                        dve.wait_ge(V.sem, V.before("lo", c))
                        step("c0", dve.tensor_scalar(xc, xp[:, 0:T], col("rnn_w", c), col("rnn_b", c), ALU.mult, ALU.add))
                        for k in range(1, RNN_K):
                            after(f"c{k - 1}")
                            step(f"c{k}", dve.scalar_tensor_tensor(xc, xp[:, k:k + T], col("rnn_w", c, k * KC), xc,
                                                                   ALU.mult, ALU.add))
                        dve.wait_ge(A.sem, A.now("gr", c))
                        step("g2", dve.tensor_tensor(q, g, g, ALU.mult))
                        after("g2")
                        step("g3", dve.tensor_scalar(q, q, 0.044715, 1.0, ALU.mult, ALU.add))
                        after("g3")
                        step("g4", dve.tensor_tensor(q, q, g, ALU.mult))
                        dve.wait_ge(A.sem, A.now("thi", c))
                        step("la", dve.tensor_scalar(la, tr, 1.0, col("", c, 0, nsp), ALU.add, ALU.mult))
                        after("la")
                        step("ix", dve.scalar_tensor_tensor(tr, ti, 1.0, xc, ALU.add, ALU.mult))
                        dve.wait_ge(A.sem, A.now("tanh", c))
                        step("den", dve.tensor_scalar(den, tv, -1.0, 1.0, ALU.mult, ALU.add))
                        after("den")
                        step("rden", dve.reciprocal(rden, den))
                        after("rden")
                        step("m2", dve.scalar_tensor_tensor(m2, tv, -2.0, rden, ALU.mult, ALU.mult))
                        dve.wait_ge(A.sem, A.now("gelu", c))
                        step("gate", dve.scalar_tensor_tensor(gt, gt, 1.0, g, ALU.add, ALU.mult))
                        dve.wait_ge(A.sem, A.now("sqrt", c))
                        after("ix")
                        step("u", dve.scalar_tensor_tensor(u, tr, 0.5, sqv, ALU.mult, ALU.mult))
                        after("u")
                        step("h", dve.tensor_tensor_scan(h, av, u, 0.0, ALU.mult, ALU.add))
                        after("h")
                        after("gate")
                        step("r", dve.scalar_tensor_tensor(r, gt, 0.5, h, ALU.mult, ALU.mult))
                        dve.wait_ge(A.sem, A.now("hi", c))
                        after("r")
                        step("lo", dve.tensor_tensor(chunk(a_lo, c), r, chunk(a_hi, c).bitcast(F32), ALU.subtract))
                    dve.wait_ge(V.sem, V.all(KC))

        gated_out("rnn", 4, True)
        split_x(0.5, False)

        def project(name, act_hi, act_lo, from_x):
            with ExitStack() as ctx:
                xr = [sb(f"{name}_x{b}", [P, T], ctx=ctx) for b in range(2)]
                V = Steps(sem(f"{name}_dve", ctx), "res0 lo0 total0 res1 lo1 total1")
                x_in = [sem(f"{name}_in{b}", ctx) for b in range(2)]
                setup = sem(f"{name}_setup", ctx)
                with nc.Block() as block:
                    @block.sync
                    def _(sp):
                        loads(sp, name, KC)

                    @block.gpsimd
                    def _(pool):
                        splits(pool, name, KC)

                    @block.tensor
                    def _(pe):
                        with pe.Fori(0, KC // 2) as i:
                            for b in range(2):
                                pe.wait_ge(V.sem, V.before(f"res{b}", i))
                                gemm(pe, b, act_hi, act_lo, i * 4 + (BASE[name] + 2 * b))

                    @block.scalar
                    def _(act):
                        if from_x:
                            with act.Fori(0, KC // 2) as i:
                                for b in range(2):
                                    hold(act, V.sem, V.before(f"res{b}", i))
                                    act.dma_start(xr[b][:, :], x_t[:, bass.ds(i * (2 * T) + b * T, T)])\
                                       .then_inc(x_in[b], 16)

                    @block.vector
                    def _(dve):
                        dve.sem_inc(V.sem, 6)
                        dve.memset(total[:, :], 0.0).then_inc(setup, 1)
                        dve.wait_ge(setup, 1)
                        with dve.Fori(0, KC // 2) as i:
                            for b in range(2):
                                at = bass.ds(i * (2 * T) + b * T, T)
                                dve.wait_ge(used, i * 4 + (BASE[name] + 2 * b + 4))
                                if from_x:
                                    dve.wait_ge(x_in[b], i * 16 + 16)
                                    src = xr[b][:, :]
                                else:
                                    src = a_hi[:, at].bitcast(F32)
                                dve.scalar_tensor_tensor(res[:, at], src, ALPHA, psum[:, b, :], ALU.mult, ALU.add)\
                                   .then_inc(V.sem, V.one(f"res{b}"))
                                dve.wait_ge(V.sem, V.now(f"res{b}", i))
                                if from_x:
                                    dve.sem_inc(V.sem, V.one(f"lo{b}"))
                                else:
                                    dve.scalar_tensor_tensor(res[:, at], a_lo[:, at].bitcast(F32), ALPHA, res[:, at],
                                                             ALU.mult, ALU.add).then_inc(V.sem, V.one(f"lo{b}"))
                                    dve.wait_ge(V.sem, V.now(f"lo{b}", i))
                                dve.tensor_tensor(total[:, :], total[:, :], res[:, at], ALU.add)\
                                   .then_inc(V.sem, V.one(f"total{b}"))
                                dve.wait_ge(V.sem, V.now(f"total{b}", i))

        project("mix", x_hi, x_lo, True)
        layer_norm("ln1", "g1", "be1", False)

        with ExitStack() as ctx:
            def part(at, n):
                return res[:, at:at + n]

            qh, kh, vt, pr, pt, vtok = (part(0, 2048), part(2048, 1024), part(3072, 1024), part(4096, 1024),
                                        part(5120, 1024), part(6144, 1024))
            stat = sb("att_stat", [P, 4 * TT], ctx=ctx)
            A = Steps(sem("att_act", ctx), "q0 q1 q2 q3 v0 v1 e0 e1 e2 e3 p0 p1 o0 o1 o2 o3")
            V = Steps(sem("att_dve", ctx), "m0 n0 m1 n1 m2 n2 m3 n3 r0 s0 r1 s1 r2 s2 r3 s3 lo0 lo1 lo2 lo3")
            E = Steps(sem("att_pe", ctx), "v s01 s23 p o0 o1 o2 o3")
            kv_in = sem("att_kv_in", ctx)
            with nc.Block() as block:
                @block.sync
                def _(sp):
                    first = BASE["att"] + AHEAD_LOAD
                    with sp.Fori(0, HEADS) as h:
                        hold(sp, E.sem, E.before("s23", h))
                        sp.dma_start(kh.rearrange("p (c n) -> p c n", c=HC),
                                     kv_d[bass.ds(h * HC, HC)].rearrange("c p n -> p c n")).then_inc(kv_in, 16)
                        sp.dma_start(vt.rearrange("p (c n) -> p c n", c=HC),
                                     kv_d[bass.ds(h * HC + KC, HC)].rearrange("c p n -> p c n")).then_inc(kv_in, 16)
                        for s in range(2 * HC):
                            load_half(sp, h * (2 * HC) + (first + s), s % 4)

                @block.gpsimd
                def _(pool):
                    splits(pool, "att", KC)

                @block.tensor
                def _(pe):
                    pe.sem_inc(E.sem, len(E.names))
                    with pe.Fori(0, HEADS) as h:
                        for c in range(HC):
                            pe.wait_ge(A.sem, A.now(f"q{c - 2}", h) if c >= 2 else A.before(f"o{c + 2}", h))
                            if c < 2:
                                pe.wait_ge(V.sem, V.before(f"lo{c + 2}", h))
                            gemm(pe, c % 2, a_hi, a_lo, h * (2 * HC) + (BASE["att"] + 2 * c))
                        pe.wait_ge(kv_in, h * 32 + 32)
                        pe.wait_ge(A.sem, A.before("v1", h))
                        for m in range(2):
                            for c in range(HC):
                                ins = pe.transpose(psum[:, 2 + m, c * P:(c + 1) * P],
                                                   vt[:, c * M + m * P:c * M + (m + 1) * P], ident[:, :])
                        ins.then_inc(E.sem, E.one("v"))
                        pe.wait_ge(A.sem, A.now("q3", h))
                        for t in range(TT):
                            if t % 2 == 0:
                                pe.wait_ge(A.sem, A.before(f"e{t + 1}", h))
                            for c in range(HC):
                                ins = pe.matmul(psum[:, 4 + t // 2, (t % 2) * M:(t % 2 + 1) * M],
                                                qh[:, c * T + t * P:c * T + (t + 1) * P], kh[:, c * M:(c + 1) * M],
                                                start=(c == 0), stop=(c == HC - 1))
                            if t % 2:
                                ins.then_inc(E.sem, E.one("s01" if t == 1 else "s23"))
                        pe.wait_ge(A.sem, A.before("p1", h))
                        for t in range(TT):
                            pe.wait_ge(V.sem, V.now(f"s{t}", h))
                            for m in range(2):
                                ins = pe.transpose(psum[:, 6 + m, t * P:(t + 1) * P],
                                                   pr[:, t * M + m * P:t * M + (m + 1) * P], ident[:, :])
                        ins.then_inc(E.sem, E.one("p"))
                        pe.wait_ge(A.sem, A.now("p1", h))
                        for c in range(HC):
                            if c >= 2:
                                pe.wait_ge(V.sem, V.now(f"lo{c - 2}", h))
                            for m in range(2):
                                ins = pe.matmul(psum[:, c % 2, :], vtok[:, m * HD + c * P:m * HD + (c + 1) * P], pt[:, m * T:(m + 1) * T],
                                                start=(m == 0), stop=(m == 1))
                            ins.then_inc(E.sem, E.one(f"o{c}"))

                @block.scalar
                def _(act):
                    act.sem_inc(A.sem, len(A.names))
                    with act.Fori(0, HEADS) as h:
                        for c in range(HC):
                            act.wait_ge(used, h * (2 * HC) + (BASE["att"] + 2 * c + 4))
                            if c == 0:
                                act.wait_ge(E.sem, E.before("s23", h))
                            act.activation(qh[:, c * T:(c + 1) * T], psum[:, c % 2, :], ACT.Copy)\
                               .then_inc(A.sem, A.one(f"q{c}"))
                        act.wait_ge(E.sem, E.now("v", h))
                        for m in range(2):
                            act.activation(vtok[:, m * HD:(m + 1) * HD], psum[:, 2 + m, :], ACT.Copy)\
                               .then_inc(A.sem, A.one(f"v{m}"))
                        for t in range(TT):
                            act.wait_ge(V.sem, V.now(f"n{t | 1}", h))
                            act.wait_ge(E.sem, E.before("p", h))
                            act.activation(pr[:, t * M:(t + 1) * M], psum[:, 4 + t // 2, (t % 2) * M:(t % 2 + 1) * M],
                                           ACT.Exp, bias=stat[:, TT + t:TT + t + 1], scale=HD ** -0.5,
                                           accum_out=stat[:, 2 * TT + t:2 * TT + t + 1])\
                               .then_inc(A.sem, A.one(f"e{t}"))
                        act.wait_ge(E.sem, E.now("p", h))
                        for m in range(2):
                            act.activation(pt[:, m * T:(m + 1) * T], psum[:, 6 + m, :], ACT.Copy)\
                               .then_inc(A.sem, A.one(f"p{m}"))
                        for c in range(HC):
                            hold(act, E.sem, E.now(f"o{c}", h))
                            act.activation(x_hi[:, bass.ds(h * (HC * T) + c * T, T)], psum[:, c % 2, :], ACT.Copy)\
                               .then_inc(A.sem, A.one(f"o{c}"))

                @block.vector
                def _(dve):
                    dve.sem_inc(V.sem, len(V.names))
                    with dve.Fori(0, HEADS) as h:
                        for t in range(TT):
                            dve.wait_ge(E.sem, E.now("s01" if t < 2 else "s23", h))
                            dve.tensor_reduce(stat[:, t:t + 1], psum[:, 4 + t // 2, (t % 2) * M:(t % 2 + 1) * M],
                                              AX_X, ALU.max).then_inc(V.sem, V.one(f"m{t}"))
                            dve.wait_ge(V.sem, V.now(f"m{t}", h))
                            dve.tensor_scalar(stat[:, TT + t:TT + t + 1], stat[:, t:t + 1], -HD ** -0.5, None,
                                              ALU.mult).then_inc(V.sem, V.one(f"n{t}"))
                        for t in range(TT):
                            dve.wait_ge(A.sem, A.now(f"e{t}", h))
                            dve.reciprocal(stat[:, 3 * TT + t:3 * TT + t + 1], stat[:, 2 * TT + t:2 * TT + t + 1])\
                               .then_inc(V.sem, V.one(f"r{t}"))
                            dve.wait_ge(V.sem, V.now(f"r{t}", h))
                            dve.tensor_scalar(pr[:, t * M:(t + 1) * M], pr[:, t * M:(t + 1) * M],
                                              stat[:, 3 * TT + t:3 * TT + t + 1], None, ALU.mult)\
                               .then_inc(V.sem, V.one(f"s{t}"))
                        for c in range(HC):
                            at = bass.ds(h * (HC * T) + c * T, T)
                            dve.wait_ge(A.sem, A.now(f"o{c}", h))
                            dve.tensor_tensor(x_lo[:, at], psum[:, c % 2, :], x_hi[:, at].bitcast(F32), ALU.subtract)\
                               .then_inc(V.sem, V.one(f"lo{c}"))
                    dve.wait_ge(V.sem, V.all(HEADS))

        project("xo", x_hi, x_lo, False)
        layer_norm("ln2", "g2", "be2", False, transposed=True)

        qt = tile_q = res[:, 0:PH * T]
        with ExitStack() as ctx:
            A = Steps(sem("pq_act", ctx), "q0 q1")
            with nc.Block() as block:
                @block.sync
                def _(sp):
                    loads(sp, "pq", PH)

                @block.gpsimd
                def _(pool):
                    splits(pool, "pq", PH)

                @block.tensor
                def _(pe):
                    with pe.Fori(0, PH // 2) as i:
                        for b in range(2):
                            pe.wait_ge(A.sem, A.before(f"q{b}", i))
                            gemm(pe, b, a_hi, a_lo, i * 4 + (BASE["pq"] + 2 * b))

                @block.scalar
                def _(act):
                    act.sem_inc(A.sem, 2)
                    with act.Fori(0, PH // 2) as i:
                        for b in range(2):
                            hold(act, used, i * 4 + (BASE["pq"] + 2 * b + 4))
                            act.activation(res[:, bass.ds(i * (2 * T) + b * T, T)], psum[:, b, :], ACT.Copy)\
                               .then_inc(A.sem, A.one(f"q{b}"))

        wctx.close()
        experts(nc, res, psum, sb, sem, hold, x2_d, keys_t, peer_u, peer_v, ln3, out)


def experts(nc, qt, psum, sb, sem, hold, x2_d, keys_t, peer_u, peer_v, ln3, out):
    wide = PH * TOPK * TOPK
    idx_all = qt[:, PH * T:PH * T + TT * HK].bitcast(U32)
    gate_all = qt[:, PH * T + TT * HK:PH * T + 2 * TT * HK]
    assert PH * T + 2 * TT * HK <= KC * T
    with ExitStack() as ctx:
        a0, a1, a2, a3 = (sb(f"route{k}", [P, n], ctx=ctx)[:, :] for k, n in enumerate((256 + PH * P, 8192, 4096, 2304)))
        keys = a0[:, 0:P]
        iota = a0[:, P:P + TOPK]
        qs = a0[:, 256:256 + PH * P]
        S, S2 = a1[:, 0:2048], a1[:, 2048:4096]
        cand, cand2 = a1[:, 4096:6144], a1[:, 6144:8192]
        eq, pr = a2[:, 0:wide], a2[:, wide:2 * wide]
        s16, i16 = a3[:, 0:256], a3[:, 256:512]
        i16u = a3[:, 512:768].bitcast(U32)
        best, posu = a3[:, 768:896], a3[:, 896:1024].bitcast(U32)
        hiu, lou = a3[:, 1024:1152].bitcast(U32), a3[:, 1152:1280].bitcast(U32)
        hif, lof = a3[:, 1280:1408], a3[:, 1408:1536]
        e1, e2 = a3[:, 1536:1664], a3[:, 1664:1792]
        sh, ex = a3[:, 1792:1920], a3[:, 1920:2048]
        tot, rec = a3[:, 2048:2056], a3[:, 2056:2064]
        iotau = a3[:, 2064:2080].bitcast(U32)

        def heads(t):
            return t.rearrange("p (h k) -> p h k", h=PH)

        keys_in, iota_done, setup = sem("keys_in", ctx), sem("iota_done", ctx), sem("route_setup", ctx)
        q_ready, s_ready, s_read = sem("route_q", ctx), sem("route_s", ctx), sem("route_read", ctx)
        soft, soft_ex = sem("route_soft", ctx), sem("route_exp", ctx)
        chain = sem("route_chain", ctx)
        with nc.Block() as block:
            @block.sync
            def _(sp):
                sp.dma_start(keys, keys_t).then_inc(keys_in, 16)

            @block.gpsimd
            def _(pool):
                pool.iota(iotau, [[1, TOPK]], base=0, channel_multiplier=0).then_inc(iota_done, 1)

            @block.scalar
            def _(act):
                act.sem_inc(q_ready, 1)
                with act.Fori(0, TT) as t:
                    hold(act, s_ready, t + 1)
                    act.activation(qs.rearrange("p (h n) -> p h n", h=PH),
                                   qt[:, 0:PH * T].rearrange("p (h n) -> p h n", h=PH)[:, :, bass.ts(t, P)], ACT.Copy)\
                       .then_inc(q_ready, 1)
                    act.wait_ge(soft, t + 1)
                    act.activation(ex, sh, ACT.Exp).then_inc(soft_ex, 1)

            @block.tensor
            def _(pe):
                pe.wait_ge(keys_in, 16)
                pe.sem_inc(s_ready, 1)
                with pe.Fori(0, TT) as t:
                    pe.wait_ge(q_ready, t + 2)
                    pe.wait_ge(s_read, t + 1)
                    for h in range(PH):
                        for j in range(2):
                            g = 2 * h + j
                            ins = pe.matmul(psum[:, 2 * j + h // 4, (h % 4) * P:(h % 4 + 1) * P],
                                            qs[j * 64:(j + 1) * 64, h * P:(h + 1) * P], keys[j * 64:(j + 1) * 64, :],
                                            start=True, stop=True)
                    ins.then_inc(s_ready, 1)

            @block.vector
            def _(dve):
                dve.sem_inc(s_read, 1)
                dve.wait_ge(iota_done, 1)
                dve.tensor_copy(iota, iotau).then_inc(setup, 1)
                dve.wait_ge(setup, 1)
                STEPS = 16 * 5 + 1 + 8 * 5 + 1 + 20

                with dve.Fori(0, TT) as t:
                    n = 0

                    def done(ins):
                        nonlocal n
                        n += 1
                        ins.then_inc(chain, 1)
                        hold(dve, chain, t * STEPS_N + n)

                    dve.wait_ge(s_ready, t + 2)
                    done(dve.tensor_copy(S.rearrange("p (b n) -> p b n", b=4), psum[:, 0:4, :]))
                    dve.sem_inc(s_read, 1)

                    def top16(v, v2, width, g, s_out, i_out):
                        a, b = v[:, g * width:(g + 1) * width], v2[:, g * width:(g + 1) * width]
                        s_lo, s_hi = (s_out[:, g * TOPK + 8 * k:g * TOPK + 8 * k + 8] for k in range(2))
                        i_lo, i_hi = (i_out[:, g * TOPK + 8 * k:g * TOPK + 8 * k + 8] for k in range(2))
                        done(dve.max(s_lo, a))
                        done(dve.max_index(i_lo, s_lo, a))
                        done(dve.match_replace(b, s_lo, a, -3.0e38))
                        done(dve.max(s_hi, b))
                        done(dve.max_index(i_hi, s_hi, b))

                    for g in range(2 * PH):
                        top16(S, S2, NK, g, s16, i16u)
                    done(dve.tensor_copy(i16, i16u))
                    for h in range(PH):
                        s1 = s16[:, h * TOPK:(h + 1) * TOPK]
                        s2 = s16[:, (PH + h) * TOPK:(PH + h + 1) * TOPK]
                        done(dve.tensor_tensor(
                            cand[:, h * 256:(h + 1) * 256].rearrange("p (i j) -> p i j", i=TOPK),
                            s1.unsqueeze(2).to_broadcast([P, TOPK, TOPK]), s2.unsqueeze(1).to_broadcast([P, TOPK, TOPK]),
                            ALU.add))
                    for h in range(PH):
                        top16(cand, cand2, 256, h, best, posu)
                    done(dve.tensor_scalar(hiu, posu, 4, None, ALU.logical_shift_right))
                    done(dve.tensor_scalar(lou, posu, 15, None, ALU.bitwise_and))
                    done(dve.tensor_copy(hif, hiu))
                    done(dve.tensor_copy(lof, lou))
                    for pos, lst, e in ((hif, i16[:, 0:HK], e1), (lof, i16[:, HK:2 * HK], e2)):
                        v4 = lambda a: a.rearrange("p (h k i) -> p h k i", h=PH, k=TOPK)
                        done(dve.tensor_tensor(
                            v4(eq), heads(pos).unsqueeze(3).to_broadcast([P, PH, TOPK, TOPK]),
                            iota.unsqueeze(1).unsqueeze(1).to_broadcast([P, PH, TOPK, TOPK]), ALU.is_equal))
                        done(dve.tensor_tensor(
                            v4(pr), v4(eq), heads(lst).unsqueeze(2).to_broadcast([P, PH, TOPK, TOPK]), ALU.mult))
                        done(dve.tensor_reduce(e, pr.rearrange("p (m i) -> p m i", i=TOPK), AX_X, ALU.add))
                    done(dve.scalar_tensor_tensor(e1, e1, float(NK), e2, ALU.mult, ALU.add))
                    done(dve.tensor_copy(idx_all[:, bass.ts(t, HK)], e1))
                    done(dve.tensor_tensor(heads(sh), heads(best), heads(best)[:, :, 0:1].to_broadcast([P, PH, TOPK]),
                                           ALU.subtract))
                    dve.sem_inc(soft, 1)
                    dve.wait_ge(soft_ex, t + 1)
                    done(dve.tensor_reduce(tot, heads(ex), AX_X, ALU.add))
                    done(dve.reciprocal(rec, tot))
                    done(dve.tensor_tensor(heads(gate_all[:, bass.ts(t, HK)]), heads(ex),
                                           rec.unsqueeze(2).to_broadcast([P, PH, TOPK]), ALU.mult))
                    assert n == STEPS_N, n

    with ExitStack() as ctx:
        rows = [sb(f"row{k}", [P, D], ctx=ctx)[:, :] for k in range(RING)]
        xt, acc, g3, b3, y = (sb(f"expert_{n}", [P, D], ctx=ctx)[:, :] for n in ("x", "sum", "gain", "shift", "y"))
        small = sb("expert_small", [P, 1024], ctx=ctx)
        dots, w, t1, t2 = (small[:, k * HK:(k + 1) * HK] for k in range(4))
        bn = small[:, 512:536]
        mv, rs = small[:, 544:546], small[:, 546:547]
        islot = [small[:, 560 + 4 * k:564 + 4 * k].bitcast(U32) for k in range(2)]
        HALFR = RING // 2

        arrived = [sem(f"row_arrived{s}", ctx) for s in range(RING)]
        taken = sem("row_taken", ctx)
        idx_ready = sem("index_ready", ctx)
        x_in, ln_in = sem("x2_in", ctx), sem("ln3_in", ctx)
        stored = sem("stored", ctx)
        tile_done = sem("tile_done", ctx)
        chain, g_a = sem("expert_chain", ctx), sem("expert_gelu", ctx)
        g_d = sem("expert_gelu_in", ctx)
        PASSES = HK // RING

        with nc.Block() as block:
            @block.sync
            def _(sp):
                sp.dma_start(g3, ln3[0:1, :].to_broadcast([P, D])).then_inc(ln_in, 16)
                sp.dma_start(b3, ln3[1:2, :].to_broadcast([P, D])).then_inc(ln_in, 16)
                with sp.Fori(0, TT) as t:
                    hold(sp, tile_done, t + 1)
                    sp.dma_start(xt, x2_d[bass.ds(t, 1)].rearrange("a p n -> (a p) n")).then_inc(x_in, 16)

            @block.gpsimd
            def _(pool):
                with pool.Fori(0, TT) as t:
                    for part, table in ((0, peer_u), (1, peer_v)):
                        with pool.Fori(0, PASSES) as i:
                            row = t * (2 * HK) + (i * RING + part * HK)
                            for half in range(2):
                                hold(pool, taken, row + (half * HALFR + HALFR))
                                pool.tensor_copy(islot[half], idx_all[:, bass.ds(t * HK + i * RING + half * HALFR, HALFR)])\
                                    .then_inc(idx_ready, 1)
                                hold(pool, idx_ready, t * (4 * PASSES) + (i * 2 + (2 * PASSES * part + half + 1)))
                                for s in range(HALFR):
                                    pool.indirect_dma_start(
                                        out=rows[half * HALFR + s], out_offset=None, in_=table,
                                        in_offset=bass.IndirectOffsetOnAxis(ap=islot[half][:, s:s + 1], axis=0))\
                                        .then_inc(arrived[half * HALFR + s], 16)

            @block.scalar
            def _(act):
                act.sem_inc(g_a, 1)
                with act.Fori(0, TT) as t:
                    act.wait_ge(g_d, t * 2 + 1)
                    act.activation(t2, t1, ACT.Tanh, scale=GELU_C).then_inc(g_a, 1)
                    act.wait_ge(g_d, t * 2 + 2)
                    act.activation(rs, mv[:, 1:2], ACT.Sqrt).then_inc(g_a, 1)
                    act.wait_ge(tile_done, t + 2)
                    act.dma_start(out[bass.ds(t, 1)].rearrange("a p n -> (a p) n"), y).then_inc(stored, 16)
                act.wait_ge(stored, (TT + 1) * 16)

            @block.vector
            def _(dve):
                dve.sem_inc(taken, RING)
                dve.sem_inc(tile_done, 1)
                dve.sem_inc(stored, 16)
                dve.wait_ge(ln_in, 32)
                with dve.Fori(0, TT) as t:
                    n = 0
                    CH = 19

                    def done(ins):
                        nonlocal n
                        n += 1
                        ins.then_inc(chain, 1)
                        hold(dve, chain, t * CH + n)

                    hold(dve, x_in, t * 16 + 16)
                    with dve.Fori(0, PASSES) as i:
                        for s in range(RING):
                            dve.wait_ge(arrived[s], (t * (2 * PASSES) + i) * 16 + 16)
                            dve.scalar_tensor_tensor(rows[s], rows[s], 1.0, xt, ALU.mult, ALU.mult,
                                                     accum_out=dots[:, bass.ds(i * RING + s, 1)]).then_inc(taken, 1)
                    dve.wait_ge(taken, t * (2 * HK) + (RING + HK))
                    gate = gate_all[:, bass.ts(t, HK)]
                    done(dve.tensor_tensor(t1, dots, dots, ALU.mult))
                    done(dve.tensor_scalar(t1, t1, 0.044715, 1.0, ALU.mult, ALU.add))
                    done(dve.tensor_tensor(t1, t1, dots, ALU.mult))
                    dve.sem_inc(g_d, 1)
                    dve.wait_ge(g_a, t * 2 + 2)
                    done(dve.scalar_tensor_tensor(w, t2, 1.0, dots, ALU.add, ALU.mult))
                    done(dve.scalar_tensor_tensor(w, w, 0.5, gate, ALU.mult, ALU.mult))
                    done(dve.tensor_scalar(acc, xt, ALPHA, None, ALU.mult))
                    with dve.Fori(0, PASSES) as i:
                        for s in range(RING):
                            dve.wait_ge(arrived[s], (t * (2 * PASSES) + i) * 16 + (PASSES + 1) * 16)
                            dve.wait_ge(taken, t * (2 * HK) + (i * RING + (HK + RING + s)))
                            dve.scalar_tensor_tensor(acc, rows[s], w[:, bass.ds(i * RING + s, 1)], acc, ALU.mult,
                                                     ALU.add).then_inc(taken, 1)
                    dve.wait_ge(taken, t * (2 * HK) + (2 * HK + RING))
                    for k in range(4):
                        done(dve.bn_stats(bn[:, 6 * k:6 * k + 6], acc[:, k * 512:(k + 1) * 512]))
                    done(dve.bn_aggr(mv, bn))
                    done(dve.tensor_scalar(mv[:, 1:2], mv[:, 1:2], EPS, None, ALU.add))
                    dve.sem_inc(g_d, 1)
                    dve.wait_ge(g_a, t * 2 + 3)
                    done(dve.reciprocal(rs, rs))
                    dve.wait_ge(stored, t * 16 + 16)
                    done(dve.tensor_scalar(acc, acc, mv[:, 0:1], rs, ALU.subtract, ALU.mult))
                    done(dve.tensor_tensor(acc, acc, g3, ALU.mult))
                    done(dve.tensor_tensor(y, acc, b3, ALU.add))
                    dve.sem_inc(tile_done, 1)
                    assert n <= CH, n
                    for _ in range(CH - n):
                        n += 1
                        dve.sem_inc(chain, 1)


STEPS_N = 1 + 16 * 5 + 1 + 8 + 8 * 5 + 4 + 6 + 2 + 1 + 3

_OUT = (1, T, D)


def kernel(**inputs):
    import numpy as np
    import concourse.bacc as bacc
    from concourse.bass_utils import run_bass_kernel_spmd as run

    a = {k: np.asarray(v) for k, v in inputs.items()}

    def chunks(w):
        n = w.shape[1] // P
        return w.reshape(2, HALF, P, n, P).transpose(3, 0, 2, 1, 4).reshape(n, 2, P, WH)

    def pairs(u, v):
        return np.stack([chunks(u), chunks(v)], axis=1).reshape(-1, 2, P, WH)

    w = a["w_in"][0]
    xr, gr, ca, cg, g_rnn, g_conf = (w[:, i * D:(i + 1) * D] for i in range(6))
    stream = np.concatenate([
        chunks(a["xa_w_k"][0]), chunks(a["xa_w_v"][0]), pairs(cg, ca), pairs(g_conf, a["w_conf_out"][0]),
        pairs(xr, gr), pairs(g_rnn, a["w_rnn_out"][0]), chunks(a["w_mix_out"][0]), chunks(a["xa_w_q"][0]),
        chunks(a["xa_w_o"][0]), chunks(a["peer_w_q"][0])]).reshape(-1, P, WH)

    def cols(v):
        return v.reshape(-1, P).T

    vecs = np.ascontiguousarray(np.concatenate([
        cols(a[n][0]) for n in ("b_in", "rnn_conv_w", "rnn_conv_b", "rnn_b_a", "rnn_b_x", "rnn_lambda", "conf_dw_w",
                                "conf_dw_b", "conf_ln_g", "conf_ln_b", "b_conf_out", "ln1_g", "ln1_b", "ln2_g",
                                "ln2_b")], axis=1))

    def turned(v):
        t = v.reshape(v.shape[0], KC, P)
        return np.ascontiguousarray(t.transpose(2, 1, 0)).reshape(P, -1)

    arrays = {
        "wstream": stream,
        "x_t": turned(a["x"][0]),
        "mem_t": turned(a["mem"][0]),
        "vecs": vecs,
        "gates_w": np.ascontiguousarray(np.concatenate([a["rnn_w_a"][0], a["rnn_w_x"][0]], axis=2)),
        "ident_d": np.eye(P, dtype=np.float32),
        "keys_t": np.ascontiguousarray(a["peer_sub_keys"][0].transpose(0, 2, 1)).reshape(P, NK),
        "peer_u": a["peer_u"][0],
        "peer_v": a["peer_v"][0],
        "ln3": np.stack([a["ln3_g"][0], a["ln3_b"][0]]),
    }
    nc = bacc.Bacc("TRN2", target_bir_lowering=False, num_devices=1)
    args = [nc.dram_tensor(n, v.shape, F32, kind="ExternalInput").ap() for n, v in arrays.items()]
    o = nc.dram_tensor("out", (TT, P, D), F32, kind="ExternalOutput").ap()
    build(nc, *args, o)
    r = run(nc, [arrays], core_ids=[0])
    return r.results[0]["out"].reshape(_OUT)
```

```python
from contextlib import ExitStack

import concourse.bass as bass
from concourse import mybir

F32 = mybir.dt.float32
F32R = mybir.dt.float32r
U32 = mybir.dt.uint32
ACT = mybir.ActivationFunctionType
ALU = mybir.AluOpType
AX_X = mybir.AxisListType.X

P = 128
D = 2048
T = 512
KC = D // P
HALF = KC // 2
WH = HALF * P
M = 256
RNN_K, CONF_K = 4, 31
HEADS, HD = 4, 512
HC = HD // P
PH, NK, TOPK, PKH = 8, 128, 16, 64
HK = PH * TOPK
N_EXPERTS = NK * NK
TT = T // P
GT = 64
ALPHA = 2.0 ** 0.25
EPS = 1e-5
GELU_C = 0.7978845608028654
EG = N_EXPERTS // D
ECH = N_EXPERTS // P

COLS = {}
_at = 0
for _name, _n in (("b_in", 6 * KC), ("rnn_w", RNN_K * KC), ("rnn_b", KC), ("b_a", KC), ("b_x", KC), ("lam", KC),
                  ("conf_w", CONF_K * KC), ("conf_b", KC), ("conf_g", KC), ("conf_be", KC), ("b_out", KC),
                  ("g1", KC), ("be1", KC), ("g2", KC), ("be2", KC), ("g3", KC), ("be3", KC)):
    COLS[_name] = _at
    _at += _n
NCOLS = _at

STAGE_CHUNKS = (("kv", 2 * KC), ("glu", 2 * KC), ("conf", 2 * KC), ("lru", 2 * KC), ("rnn", 2 * KC),
                ("mix", KC), ("att", KC), ("xo", KC), ("pq", PH), ("pick", ECH // 2), ("gates", ECH // 2), ("down", ECH))
BASE = {}
_at = 0
for _name, _n in STAGE_CHUNKS:
    BASE[_name] = 2 * _at
    _at += _n
HALVES = 2 * _at
AHEAD_LOAD, AHEAD_SPLIT = 4, 2


class Steps:

    def __init__(self, sem, names):
        self.sem, self.names, self.at = sem, names.split(), 0

    def one(self, name):
        assert self.names[self.at % len(self.names)] == name, (name, self.names[self.at % len(self.names)])
        self.at += 1
        return 1

    def now(self, name, i=0):
        return i * len(self.names) + (len(self.names) + self.names.index(name) + 1)

    def before(self, name, i=0):
        return i * len(self.names) + (self.names.index(name) + 1)

    def all(self, n):
        return (n + 1) * len(self.names)


def build(nc, wstream, x_t, mem_t, vecs, gates_w, ident_d, keys_t, out):
    top = ExitStack()
    with top:
        def sb(name, shape, dt=F32, ctx=top):
            return ctx.enter_context(nc.sbuf_tensor(name, shape, dt))

        def sem(name, ctx=top):
            return ctx.enter_context(nc.semaphore(name))

        psum = top.enter_context(nc.psum_tensor("psum", [P, 8, 512], F32))
        vec = sb("vec", [P, NCOLS])
        hb_in = sb("hb_in", [P, 6 * KC])
        hb_ax = sb("hb_ax", [P, 2 * KC])
        nsp = sb("nsp", [P, KC])
        hcw = sb("hcw", [P, CONF_K * KC])
        ident = sb("ident", [P, P])
        iota_k = sb("iota_k", [P, P])
        iota_u = sb("iota_u", [P, P], U32)
        ones = sb("ones", [P, P])
        zero = sb("zero", [P, 1])
        kv_d = nc.dram_tensor("kv_scratch", (2 * KC, P, M), F32).ap()
        conf_d = nc.dram_tensor("conf_scratch", (KC, P, T), F32).ap()
        act_d = nc.dram_tensor("expert_act_scratch", (ECH, P, T), F32).ap()
        gate_d = nc.dram_tensor("gate_scratch", (T // GT, P, ECH, GT), F32).ap()

        loaded = [sem(f"weights_loaded{i}") for i in range(4)]
        hi_made = sem("weights_hi_made")
        split = sem("weights_split")
        raw_free = sem("weights_raw_free")
        used = sem("weights_used")
        alone = sem("wait_passed")

        def hold(eng, s, value):
            eng.wait_ge(s, value)
            eng.sem_inc(alone, 1)

        res = sb("res", [P, KC * T])
        wctx = top.enter_context(ExitStack())
        w_raw = [sb(f"w_raw{i}", [P, WH], ctx=wctx) for i in range(2)]
        w_hi = [sb(f"w_hi{i}", [P, WH], F32R, ctx=wctx) for i in range(2)]
        w_lo = [sb(f"w_lo{i}", [P, WH], F32R, ctx=wctx) for i in range(2)]
        stream = wstream.rearrange("h p n -> h p n")

        def load_half(sp, g, s):
            hold(sp, raw_free, g + 1)
            sp.dma_start(w_raw[s % 2][:, :], stream[bass.ds(g, 1)].rearrange("a p n -> (a p) n")).then_inc(loaded[s], 16)

        def his(act, name, i, b):
            for s in range(2):
                ahead = BASE[name] + AHEAD_SPLIT + 2 * b + s
                slot = ahead % 4
                hold(act, loaded[slot], i * 16 + (ahead // 4 * 16 + 16))
                hold(act, used, i * 4 + (ahead + 1))
                act.activation(w_hi[slot % 2][:, :], w_raw[slot % 2][:, :], ACT.Copy).then_inc(hi_made, 1)

        def split_half(pool, g, round_, s, hi_by_act=False):
            if not hi_by_act:
                hold(pool, loaded[s], round_ * 16 + 16)
                hold(pool, used, g + 1)
                pool.tensor_tensor(w_hi[s % 2][:, :], w_raw[s % 2][:, :], zero[:, :].to_broadcast([P, WH]), ALU.add)\
                    .then_inc(hi_made, 1)
            pool.wait_ge(hi_made, g + 1)
            pool.tensor_tensor(w_lo[s % 2][:, :], w_raw[s % 2][:, :], w_hi[s % 2][:, :].bitcast(F32),
                               ALU.subtract).then_inc(split, 1)
            pool.wait_ge(split, g + 1)
            pool.sem_inc(raw_free, 1)

        def loads(sp, name, n_chunks):
            first, last = BASE[name] + AHEAD_LOAD, min(BASE[name] + 2 * n_chunks + AHEAD_LOAD, HALVES)
            with sp.Fori(0, (last - first) // 4) as i:
                for s in range(4):
                    load_half(sp, i * 4 + (first + s), s)

        def splits(pool, name, n_chunks, hi_by_act=False, each=None):
            first, last = BASE[name] + AHEAD_SPLIT, min(BASE[name] + 2 * n_chunks + AHEAD_SPLIT, HALVES)
            n = (last - first) // 4
            with pool.Fori(0, n) as i:
                for s in range(4):
                    slot = (AHEAD_SPLIT + s) % 4
                    split_half(pool, i * 4 + (first + s), i + (first + s) // 4, slot, hi_by_act)
                if each:
                    each(i)
            for g in range(first + 4 * n, last):
                split_half(pool, g, g // 4, g % 4, hi_by_act)

        def gemm(pe, bank, act_hi, act_lo, g, n=T, done=None):
            for half in range(2):
                pe.wait_ge(split, g + (half + 1))
                for k in range(HALF):
                    kk = half * HALF + k
                    wh, wl = (w[half][:, k * P:(k + 1) * P] for w in (w_hi, w_lo))
                    xh, xl = (a[:, kk * n:(kk + 1) * n] for a in (act_hi, act_lo))
                    pe.matmul(psum[:, bank, 0:n], wh, xh, start=(kk == 0), stop=False)
                    pe.matmul(psum[:, bank, 0:n], wh, xl, start=False, stop=False)
                    last = pe.matmul(psum[:, bank, 0:n], wl, xh, start=False, stop=(kk == KC - 1))
                last.then_inc(used, 1)

        def chunk(t, c, n=T):
            return t[:, bass.ts(c, n)]

        def col(name, c, k=0, t=None):
            return (vec if t is None else t)[:, bass.ds(c + ((COLS[name] if t is None else 0) + k), 1)]

        a_hi = sb("a_hi", [P, KC * T], F32R, ctx=wctx)
        a_lo = sb("a_lo", [P, KC * T], F32R, ctx=wctx)
        total = sb("total", [P, T], ctx=wctx)
        total2 = sb("total2", [P, T], ctx=wctx)
        work = sb("work", [P, 2 * T], ctx=wctx)
        tile_in, rstd = work[:, 0:T], work[:, T:2 * T]
        xctx = ExitStack()
        wctx.enter_context(xctx)
        x_hi = sb("x_hi", [P, KC * T], F32R, ctx=xctx)
        x_lo = sb("x_lo", [P, KC * T], F32R, ctx=xctx)
        tile = [res[:, k * T:(k + 1) * T] for k in range(KC)]

        const_in, c_d, c_a, c_p = sem("const_in"), sem("c_dve"), sem("c_act"), sem("c_pool")
        mem_in = sem("mem_in")
        with nc.Block() as block:
            @block.sync
            def _(sp):
                sp.dma_start(vec[:, :], vecs).then_inc(const_in, 16)
                sp.dma_start(ident[:, :], ident_d).then_inc(const_in, 16)
                sp.dma_start(res[:, 0:KC * M], mem_t).then_inc(mem_in, 16)
                sp.wait_ge(raw_free, 2)
                for g in range(2):
                    sp.dma_start(w_raw[g][:, :], stream[g]).then_inc(loaded[g], 16)
                for g in range(2, AHEAD_LOAD):
                    sp.wait_ge(raw_free, g + 1)
                    sp.dma_start(w_raw[g % 2][:, :], stream[g]).then_inc(loaded[g], 16)

            @block.gpsimd
            def _(pool):
                pool.sem_inc(raw_free, 2)
                pool.memset(zero[:, :], 0.0).then_inc(c_p, 1)
                pool.memset(ones[:, :], 1.0 / D).then_inc(c_p, 1)
                pool.iota(iota_u[:, :], [[1, P]], base=0, channel_multiplier=0).then_inc(c_p, 1)
                pool.wait_ge(c_p, 3)
                for g in range(AHEAD_SPLIT):
                    split_half(pool, g, 0, g)

            @block.tensor
            def _(pe):
                pe.sem_inc(used, 2)

            @block.scalar
            def _(act):
                act.wait_ge(c_d, 1)
                act.activation(tile[8][:, 0:KC], tile[9][:, 0:KC], ACT.Exp, scale=-1.0).then_inc(c_a, 1)
                act.wait_ge(c_d, 3)
                act.activation(tile[11][:, 0:KC], tile[10][:, 0:KC], ACT.Ln).then_inc(c_a, 1)
                act.wait_ge(mem_in, 16)
                act.activation(x_hi[:, 0:KC * M], res[:, 0:KC * M], ACT.Copy).then_inc(c_a, 1)

            @block.vector
            def _(dve):
                n = 0

                def done(ins):
                    nonlocal n
                    n += 1
                    ins.then_inc(c_d, 1)
                    dve.wait_ge(c_d, n)

                dve.wait_ge(const_in, 32)
                dve.wait_ge(c_p, 3)
                lam = vec[:, COLS["lam"]:COLS["lam"] + KC]
                e, ab, w, lw, t1 = (tile[k][:, 0:KC] for k in (8, 9, 10, 11, 12))
                t2, t3, t4 = (tile[k][:, 0:KC] for k in (13, 14, 15))
                done(dve.scalar_tensor_tensor(ab, lam, -1.0, lam, ALU.mult, ALU.max))
                dve.wait_ge(c_a, 1)
                done(dve.tensor_scalar(w, e, 1.0, None, ALU.add))
                done(dve.tensor_scalar(t1, w, -1.0, None, ALU.add))
                done(dve.tensor_scalar(t2, t1, 0.0, None, ALU.is_equal))
                done(dve.tensor_tensor(t1, t1, t2, ALU.add))
                done(dve.reciprocal(t3, t1))
                dve.wait_ge(c_a, 2)
                done(dve.tensor_tensor(lw, lw, t2, ALU.add))
                done(dve.tensor_tensor(lw, lw, t3, ALU.mult))
                done(dve.tensor_tensor(lw, lw, e, ALU.mult))
                done(dve.tensor_scalar(t4, lam, -1.0, 0.0, ALU.mult, ALU.max))
                done(dve.tensor_tensor(lw, lw, t4, ALU.add))
                done(dve.tensor_scalar(nsp[:, :], lw, -4.0, None, ALU.mult))
                done(dve.tensor_copy(iota_k[:, :], iota_u[:, :]))
                done(dve.tensor_scalar(hb_in[:, :], vec[:, 0:6 * KC], 0.5, None, ALU.mult))
                done(dve.tensor_scalar(hb_ax[:, :], vec[:, COLS["b_a"]:COLS["b_a"] + 2 * KC], 0.5, None, ALU.mult))
                done(dve.tensor_scalar(hcw[:, :], vec[:, COLS["conf_w"]:COLS["conf_w"] + CONF_K * KC], 0.5, None,
                                       ALU.mult))
                dve.wait_ge(c_a, 3)
                done(dve.tensor_tensor(x_lo[:, 0:KC * M], res[:, 0:KC * M], x_hi[:, 0:KC * M].bitcast(F32),
                                       ALU.subtract))

        with ExitStack() as ctx:
            kv_out = sem("kv_out", ctx)
            A = Steps(sem("kv_evacuated", ctx), "copy0 copy1")
            sent = [sem(f"kv_sent{i}", ctx) for i in range(2)]
            with nc.Block() as block:
                @block.sync
                def _(sp):
                    loads(sp, "kv", 2 * KC)

                @block.gpsimd
                def _(pool):
                    splits(pool, "kv", 2 * KC, hi_by_act=True)

                @block.tensor
                def _(pe):
                    with pe.Fori(0, KC) as i:
                        for b in range(2):
                            pe.wait_ge(A.sem, A.before(f"copy{b}", i))
                            gemm(pe, b, x_hi, x_lo, i * 4 + (BASE["kv"] + 2 * b), M)

                @block.scalar
                def _(act):
                    act.sem_inc(A.sem, 2)
                    for b in range(2):
                        act.sem_inc(sent[b], 16)
                    with act.Fori(0, KC) as i:
                        for b in range(2):
                            his(act, "kv", i, b)
                            hold(act, sent[b], i * 16 + 16)
                            act.wait_ge(used, i * 4 + (BASE["kv"] + 2 * b + 4))
                            act.activation(tile[8 + b][:, 0:M], psum[:, b, 0:M], ACT.Copy)\
                               .then_inc(A.sem, A.one(f"copy{b}"))
                            hold(act, A.sem, A.now(f"copy{b}", i))
                            act.dma_start(kv_d[bass.ds(i * 2 + b, 1)].rearrange("a p n -> (a p) n"),
                                          tile[8 + b][:, 0:M]).then_inc(sent[b], 16)
                    for b in range(2):
                        act.wait_ge(sent[b], (KC + 1) * 16)

        def split_x(read_scale, from_dram):
            with ExitStack() as ctx:
                arrived = sem("x_arrived", ctx)
                hi_done = sem("x_hi_done", ctx)
                lo_done = sem("x_lo_done", ctx)
                with nc.Block() as block:
                    @block.sync
                    def _(sp):
                        if from_dram:
                            sp.dma_start(res[:, :], x_t).then_inc(arrived, 16)

                    Q = KC * T // 4
                    @block.scalar
                    def _(act):
                        if from_dram:
                            act.wait_ge(arrived, 16)
                        for q in range(4):
                            act.activation(x_hi[:, q * Q:(q + 1) * Q], res[:, q * Q:(q + 1) * Q], ACT.Copy,
                                           scale=read_scale).then_inc(hi_done, 1)

                    @block.vector
                    def _(dve):
                        for q in range(4):
                            dve.wait_ge(hi_done, q + 1)
                            dve.scalar_tensor_tensor(x_lo[:, q * Q:(q + 1) * Q], res[:, q * Q:(q + 1) * Q],
                                                     read_scale, x_hi[:, q * Q:(q + 1) * Q].bitcast(F32),
                                                     ALU.mult, ALU.subtract).then_inc(lo_done, 1)
                        dve.wait_ge(lo_done, 4)

        split_x(1.0, True)

        PAD = CONF_K - 1
        with ExitStack() as ctx:
            th = rstd
            cab = sb("glu_ca", [P, T], ctx=ctx)
            xp = sb("glu_padded", [P, PAD + T], ctx=ctx)
            odd = sb("glu_odd", [P, T], ctx=ctx)
            A = Steps(sem("glu_act", ctx), "th ca")
            SQ = Steps(sem("glu_squared", ctx), "sq")
            V = Steps(sem("glu_dve", ctx), "glu " + " ".join(f"tap{k}" for k in range(CONF_K)))
            G = Steps(sem("glu_pool", ctx), "join total total2")
            padded, zeroed = sem("glu_pad_zeroed", ctx), sem("glu_totals_zeroed", ctx)
            with nc.Block() as block:
                @block.sync
                def _(sp):
                    loads(sp, "glu", 2 * KC)

                @block.gpsimd
                def _(pool):
                    def totals(c):
                        hold(pool, V.sem, V.now(f"tap{CONF_K - 1}", c - 1))
                        pool.tensor_tensor(chunk(res, c - 1), chunk(res, c - 1), odd[:, :], ALU.add)\
                            .then_inc(G.sem, G.one("join"))
                        hold(pool, G.sem, G.now("join", c - 1))
                        pool.tensor_tensor(total[:, :], total[:, :], chunk(res, c - 1), ALU.add)\
                            .then_inc(G.sem, G.one("total"))
                        pool.wait_ge(SQ.sem, SQ.now("sq", c - 1))
                        pool.tensor_tensor(total2[:, :], total2[:, :], tile_in[:, :], ALU.add)\
                            .then_inc(G.sem, G.one("total2"))

                    pool.sem_inc(G.sem, len(G.names))
                    pool.memset(total[:, :], 0.0).then_inc(zeroed, 1)
                    pool.memset(total2[:, :], 0.0).then_inc(zeroed, 1)
                    pool.wait_ge(zeroed, 2)
                    first = BASE["glu"] + AHEAD_SPLIT
                    for s in range(4):
                        split_half(pool, first + s, (first + s) // 4, (first + s) % 4, hi_by_act=True)
                    with pool.Fori(0, KC - 1) as c:
                        for s in range(4):
                            split_half(pool, c * 4 + (first + 4 + s), c, (first + s) % 4, hi_by_act=True)
                        totals(c + 1)
                    totals(KC)
                    pool.wait_ge(G.sem, G.all(KC))

                @block.tensor
                def _(pe):
                    with pe.Fori(0, KC) as c:
                        pe.wait_ge(A.sem, A.before("th", c))
                        gemm(pe, 0, x_hi, x_lo, c * 4 + BASE["glu"])
                        pe.wait_ge(A.sem, A.before("ca", c))
                        gemm(pe, 1, x_hi, x_lo, c * 4 + (BASE["glu"] + 2))

                @block.scalar
                def _(act):
                    act.sem_inc(A.sem, len(A.names))
                    act.sem_inc(SQ.sem, 1)

                    def square(c):
                        hold(act, G.sem, G.now("join", c))
                        act.activation(tile_in[:, :], chunk(res, c), ACT.Square).then_inc(SQ.sem, SQ.one("sq"))

                    def body(c, first):
                        his(act, "glu", c, 0)
                        hold(act, V.sem, V.before("glu", c))
                        hold(act, used, c * 4 + (BASE["glu"] + 4))
                        act.activation(th, psum[:, 0, :], ACT.Tanh, bias=col("", c, 3 * KC, hb_in),
                                       scale=0.5).then_inc(A.sem, A.one("th"))
                        his(act, "glu", c, 1)
                        hold(act, used, c * 4 + (BASE["glu"] + 6))
                        act.activation(cab[:, :], psum[:, 1, :], ACT.Identity, bias=col("b_in", c, 2 * KC))\
                           .then_inc(A.sem, A.one("ca"))
                        if not first:
                            square(c - 1)

                    body(0, True)
                    with act.Fori(0, KC - 1) as c:
                        body(c + 1, False)
                    square(KC - 1)

                @block.vector
                def _(dve):
                    dve.sem_inc(V.sem, len(V.names))
                    dve.memset(xp[:, 0:PAD], 0.0).then_inc(padded, 1)
                    dve.wait_ge(padded, 1)
                    with dve.Fori(0, KC) as c:
                        even = chunk(res, c)
                        dve.wait_ge(V.sem, V.before(f"tap{CONF_K - 1}", c))
                        dve.wait_ge(A.sem, A.now("ca", c))
                        dve.scalar_tensor_tensor(xp[:, PAD:PAD + T], th, 1.0, cab[:, :], ALU.add, ALU.mult)\
                           .then_inc(V.sem, V.one("glu"))
                        dve.wait_ge(V.sem, V.now("glu", c))
                        for k in range(CONF_K):
                            acc = odd[:, :] if k % 2 else even
                            tap = col("", c, k * KC, hcw)
                            if k == 0:
                                ins = dve.tensor_scalar(acc, xp[:, 0:T], tap, col("conf_b", c), ALU.mult, ALU.add)
                            elif k == 1:
                                dve.wait_ge(G.sem, G.before("join", c))
                                ins = dve.tensor_scalar(acc, xp[:, 1:1 + T], tap, None, ALU.mult)
                            else:
                                dve.wait_ge(V.sem, V.now(f"tap{k - 2}", c))
                                ins = dve.scalar_tensor_tensor(acc, xp[:, k:k + T], tap, acc, ALU.mult, ALU.add)
                            ins.then_inc(V.sem, V.one(f"tap{k}"))
                    dve.wait_ge(V.sem, V.all(KC))


        def layer_norm(name, g_name, b_name, silu=False, turned_out=None):
            B = 2 if silu else 4
            with ExitStack() as ctx:
                s = lambda n: sem(f"{name}_{n}", ctx)
                shift = sb(f"{name}_shift", [P, T], ctx=ctx)
                y = [sb(f"{name}_y{b}", [P, T], ctx=ctx) for b in range(B if silu or turned_out is not None else 0)]
                outs = [sb(f"{name}_out{b}", [P, T], ctx=ctx)[:, :] for b in range(B if turned_out is not None else 0)]
                pe_sem, sqrt_done, st = s("pe"), s("sqrt"), s("stats")
                each = lambda *names: " ".join(f"{n}{b}" for n in names for b in range(B))
                V = Steps(s("dve"), each("scale", "shift") + (" " + each("gate") if silu else "")
                          + ("" if turned_out is not None else " " + each("lo")))
                if silu:
                    A = Steps(s("act"), each("affine", "tanh", "hi"))
                elif turned_out is not None:
                    A = Steps(s("act"), each("affine", "out"))
                else:
                    A = Steps(s("act"), each("affine", "hi"))
                E = Steps(s("turn"), each("turn"))
                sent = [s(f"sent{b}") for b in range(B)]
                with nc.Block() as block:
                    @block.tensor
                    def _(pe):
                        pe.matmul(psum[:, 6, :], ones[:, :], total[:, :], start=True, stop=True).then_inc(pe_sem, 1)
                        pe.matmul(psum[:, 7, :], ones[:, :], total2[:, :], start=True, stop=True).then_inc(pe_sem, 1)
                        if turned_out is not None:
                            pe.sem_inc(E.sem, B)
                            with pe.Fori(0, KC // B) as i:
                                for b in range(B):
                                    pe.wait_ge(A.sem, A.now(f"affine{b}", i))
                                    pe.wait_ge(A.sem, A.before(f"out{b}", i))
                                    for t in range(TT):
                                        ins = pe.transpose(psum[:, b, t * P:(t + 1) * P],
                                                           y[b][:, t * P:(t + 1) * P],
                                                           ident[:, :])
                                    ins.then_inc(E.sem, E.one(f"turn{b}"))

                    @block.scalar
                    def _(act):
                        act.sem_inc(A.sem, len(A.names))
                        act.wait_ge(st, 4)
                        act.activation(rstd[:, :], rstd[:, :], ACT.Sqrt).then_inc(sqrt_done, 1)
                        if turned_out is not None:
                            for b in range(B):
                                act.sem_inc(sent[b], 16)
                        with act.Fori(0, KC // B) as i:
                            r = lambda b: res[:, bass.ds(i * (B * T) + b * T, T)]
                            c = i * B
                            for b in range(B):
                                hold(act, V.sem, V.now(f"shift{b}", i))
                                if silu:
                                    hold(act, V.sem, V.before(f"lo{b}", i))
                                if turned_out is not None:
                                    hold(act, E.sem, E.before(f"turn{b}", i))
                                act.activation(y[b][:, :] if y else r(b), r(b), ACT.Identity,
                                               scale=col(g_name, c, b), bias=col(b_name, c, b))\
                                   .then_inc(A.sem, A.one(f"affine{b}"))
                            if silu:
                                for b in range(B):
                                    hold(act, A.sem, A.now(f"affine{b}", i))
                                    act.activation(r(b), y[b][:, :], ACT.Tanh, scale=0.5)\
                                       .then_inc(A.sem, A.one(f"tanh{b}"))
                                for b in range(B):
                                    hold(act, V.sem, V.now(f"gate{b}", i))
                                    act.activation(a_hi[:, bass.ds(i * (B * T) + b * T, T)], y[b][:, :], ACT.Copy,
                                                   scale=0.5).then_inc(A.sem, A.one(f"hi{b}"))
                            elif turned_out is not None:
                                for b in range(B):
                                    hold(act, sent[b], i * 16 + 16)
                                    hold(act, E.sem, E.now(f"turn{b}", i))
                                    act.activation(outs[b], psum[:, b, :], ACT.Copy).then_inc(A.sem, A.one(f"out{b}"))
                                    hold(act, A.sem, A.now(f"out{b}", i))
                                    act.dma_start(turned_out[:, :, bass.ds(i * (B * P) + b * P, P)]
                                                  .rearrange("t p n -> p t n"),
                                                  outs[b].rearrange("p (t n) -> p t n", t=TT)).then_inc(sent[b], 16)
                            else:
                                for b in range(B):
                                    hold(act, A.sem, A.now(f"affine{b}", i))
                                    act.activation(a_hi[:, bass.ds(i * (B * T) + b * T, T)], r(b), ACT.Copy)\
                                       .then_inc(A.sem, A.one(f"hi{b}"))
                        if turned_out is not None:
                            for b in range(B):
                                act.wait_ge(sent[b], (KC // B + 1) * 16)

                    @block.vector
                    def _(dve):
                        dve.sem_inc(V.sem, len(V.names))
                        dve.wait_ge(pe_sem, 1)
                        dve.tensor_copy(shift[:, :], psum[:, 6, :]).then_inc(st, 1)
                        dve.wait_ge(st, 1)
                        dve.tensor_tensor(rstd[:, :], shift[:, :], shift[:, :], ALU.mult).then_inc(st, 1)
                        dve.wait_ge(pe_sem, 2)
                        dve.wait_ge(st, 2)
                        dve.tensor_tensor(rstd[:, :], psum[:, 7, :], rstd[:, :], ALU.subtract).then_inc(st, 1)
                        dve.wait_ge(st, 3)
                        dve.tensor_scalar(rstd[:, :], rstd[:, :], 0.0, EPS, ALU.max, ALU.add).then_inc(st, 1)
                        dve.wait_ge(sqrt_done, 1)
                        dve.reciprocal(rstd[:, :], rstd[:, :]).then_inc(st, 1)
                        dve.wait_ge(st, 5)
                        dve.tensor_tensor(shift[:, :], shift[:, :], rstd[:, :], ALU.mult).then_inc(st, 1)
                        dve.wait_ge(st, 6)
                        with dve.Fori(0, KC // B) as i:
                            r = lambda b: res[:, bass.ds(i * (B * T) + b * T, T)]
                            for b in range(B):
                                dve.tensor_tensor(r(b), r(b), rstd[:, :], ALU.mult).then_inc(V.sem, V.one(f"scale{b}"))
                            for b in range(B):
                                dve.wait_ge(V.sem, V.now(f"scale{b}", i))
                                dve.tensor_tensor(r(b), r(b), shift[:, :], ALU.subtract)\
                                   .then_inc(V.sem, V.one(f"shift{b}"))
                            if silu:
                                for b in range(B):
                                    dve.wait_ge(A.sem, A.now(f"tanh{b}", i))
                                    dve.scalar_tensor_tensor(y[b][:, :], r(b), 1.0, y[b][:, :], ALU.add, ALU.mult)\
                                       .then_inc(V.sem, V.one(f"gate{b}"))
                                    dve.wait_ge(V.sem, V.now(f"gate{b}", i))
                            if turned_out is None:
                                for b in range(B):
                                    at = bass.ds(i * (B * T) + b * T, T)
                                    dve.wait_ge(A.sem, A.now(f"hi{b}", i))
                                    dve.scalar_tensor_tensor(a_lo[:, at], y[b][:, :] if silu else r(b), 0.5 if silu else 1.0,
                                                             a_hi[:, at].bitcast(F32), ALU.mult, ALU.subtract)\
                                       .then_inc(V.sem, V.one(f"lo{b}"))
                        dve.wait_ge(V.sem, V.all(KC // B))

        layer_norm("conf_ln", "conf_g", "conf_be", silu=True)

        def gated_out(name, gate_col, add_conf):
            with ExitStack() as ctx:
                th = sb(f"{name}_th", [P, T], ctx=ctx)
                yb = sb(f"{name}_y", [P, T], ctx=ctx)
                A = Steps(sem(f"{name}_act", ctx), "th y")
                V = Steps(sem(f"{name}_dve", ctx), "gate join")
                moved = sem(f"{name}_moved", ctx)
                with nc.Block() as block:
                    @block.sync
                    def _(sp):
                        loads(sp, name, 2 * KC)

                    @block.gpsimd
                    def _(pool):
                        splits(pool, name, 2 * KC, hi_by_act=True)

                    @block.tensor
                    def _(pe):
                        with pe.Fori(0, KC) as c:
                            pe.wait_ge(A.sem, A.before("th", c))
                            gemm(pe, 0, x_hi, x_lo, c * 4 + BASE[name])
                            pe.wait_ge(A.sem, A.before("y", c))
                            gemm(pe, 1, a_hi, a_lo, c * 4 + (BASE[name] + 2))

                    @block.scalar
                    def _(act):
                        act.sem_inc(A.sem, 2)
                        if not add_conf:
                            act.sem_inc(moved, 16)
                        with act.Fori(0, KC) as c:
                            hold(act, V.sem, V.before("join", c))
                            if add_conf:
                                act.dma_start(tile_in[:, :], conf_d[bass.ds(c, 1)].rearrange("a p n -> (a p) n"))\
                                   .then_inc(moved, 16)
                            his(act, name, c, 0)
                            hold(act, used, c * 4 + (BASE[name] + 4))
                            act.activation(th[:, :], psum[:, 0, :], ACT.Tanh, bias=col("", c, gate_col * KC, hb_in),
                                           scale=0.5).then_inc(A.sem, A.one("th"))
                            his(act, name, c, 1)
                            hold(act, used, c * 4 + (BASE[name] + 6))
                            if add_conf:
                                act.activation(yb[:, :], psum[:, 1, :], ACT.Copy).then_inc(A.sem, A.one("y"))
                            else:
                                act.activation(yb[:, :], psum[:, 1, :], ACT.Identity, bias=col("b_out", c))\
                                   .then_inc(A.sem, A.one("y"))
                                hold(act, V.sem, V.now("join", c))
                                act.dma_start(conf_d[bass.ds(c, 1)].rearrange("a p n -> (a p) n"), tile_in[:, :])\
                                   .then_inc(moved, 16)
                        act.wait_ge(moved, (KC if add_conf else KC + 1) * 16)

                    @block.vector
                    def _(dve):
                        dve.sem_inc(V.sem, 2)
                        with dve.Fori(0, KC) as c:
                            dve.wait_ge(A.sem, A.now("y", c))
                            dve.wait_ge(moved, c * 16 + 16)
                            if add_conf:
                                dve.scalar_tensor_tensor(yb[:, :], th[:, :], 1.0, yb[:, :], ALU.add, ALU.mult)\
                                   .then_inc(V.sem, V.one("gate"))
                                dve.wait_ge(V.sem, V.now("gate", c))
                                dve.tensor_tensor(chunk(res, c), yb[:, :], tile_in[:, :], ALU.add)\
                                   .then_inc(V.sem, V.one("join"))
                            else:
                                dve.scalar_tensor_tensor(tile_in[:, :], th[:, :], 1.0, yb[:, :], ALU.add, ALU.mult)\
                                   .then_inc(V.sem, V.one("gate"))
                                dve.wait_ge(V.sem, V.now("gate", c))
                                dve.sem_inc(V.sem, V.one("join"))
                        dve.wait_ge(V.sem, V.all(KC))

        gated_out("conf", 5, False)

        with ExitStack() as ctx:
            (g, q, xc, tr, ti, la, av, tv, den, rden, m2, u, h, gt, r, sqv) = tile
            xp = sb("lru_padded", [P, RNN_K - 1 + T], ctx=ctx)
            gw = sb("lru_gates", [P, 2 * P], ctx=ctx)
            A = Steps(sem("lru_act", ctx), "xr gr thr thi exp tanh gelu sqrt hi")
            V = Steps(sem("lru_dve", ctx), "c0 c1 c2 c3 g2 g3 g4 la ix den rden m2 gate u h r lo")
            E = Steps(sem("lru_pe", ctx), "gates")
            gates_in = sem("lru_gates_in", ctx)
            setup = sem("lru_setup", ctx)
            with nc.Block() as block:
                @block.sync
                def _(sp):
                    first = BASE["lru"] + AHEAD_LOAD
                    with sp.Fori(0, KC) as c:
                        hold(sp, E.sem, c + 1)
                        sp.dma_start(gw[:, :], gates_w[bass.ds(c, 1)].rearrange("a p n -> (a p) n"))\
                          .then_inc(gates_in, 16)
                        for s in range(4):
                            load_half(sp, c * 4 + (first + s), s)

                @block.gpsimd
                def _(pool):
                    splits(pool, "lru", 2 * KC)

                @block.tensor
                def _(pe):
                    pe.sem_inc(E.sem, 1)
                    with pe.Fori(0, KC) as c:
                        pe.wait_ge(A.sem, A.before("xr", c))
                        gemm(pe, 0, x_hi, x_lo, c * 4 + BASE["lru"])
                        pe.wait_ge(A.sem, A.before("gr", c))
                        gemm(pe, 1, x_hi, x_lo, c * 4 + (BASE["lru"] + 2))
                        pe.wait_ge(gates_in, c * 16 + 16)
                        pe.wait_ge(V.sem, V.now("c3", c))
                        pe.wait_ge(A.sem, A.before("thi", c))
                        for j in range(2):
                            ins = pe.matmul(psum[:, 2 + j, :], gw[:, j * P:(j + 1) * P], xc, start=True, stop=True)
                        ins.then_inc(E.sem, E.one("gates"))

                @block.scalar
                def _(act):
                    act.sem_inc(A.sem, len(A.names))
                    with act.Fori(0, KC) as c:
                        hold(act, used, c * 4 + (BASE["lru"] + 4))
                        hold(act, V.sem, V.before("c3", c))
                        act.activation(xp[:, 3:3 + T], psum[:, 0, :], ACT.Identity, bias=col("b_in", c))\
                           .then_inc(A.sem, A.one("xr"))
                        hold(act, used, c * 4 + (BASE["lru"] + 6))
                        hold(act, V.sem, V.before("gate", c))
                        act.activation(g, psum[:, 1, :], ACT.Identity, bias=col("b_in", c, KC))\
                           .then_inc(A.sem, A.one("gr"))
                        hold(act, E.sem, c + 2)
                        hold(act, V.sem, V.before("lo", c))
                        act.activation(tr, psum[:, 2, :], ACT.Tanh, bias=col("", c, 0, hb_ax), scale=0.5)\
                           .then_inc(A.sem, A.one("thr"))
                        act.activation(ti, psum[:, 3, :], ACT.Tanh, bias=col("", c, KC, hb_ax), scale=0.5)\
                           .then_inc(A.sem, A.one("thi"))
                        act.wait_ge(V.sem, V.now("la", c))
                        act.activation(av, la, ACT.Exp).then_inc(A.sem, A.one("exp"))
                        act.activation(tv, la, ACT.Tanh).then_inc(A.sem, A.one("tanh"))
                        act.activation(gt, q, ACT.Tanh, scale=GELU_C).then_inc(A.sem, A.one("gelu"))
                        act.wait_ge(V.sem, V.now("m2", c))
                        act.activation(sqv, m2, ACT.Sqrt).then_inc(A.sem, A.one("sqrt"))
                        hold(act, V.sem, V.now("r", c))
                        act.activation(chunk(a_hi, c), r, ACT.Copy).then_inc(A.sem, A.one("hi"))

                @block.vector
                def _(dve):
                    dve.sem_inc(V.sem, len(V.names))
                    dve.memset(xp[:, 0:3], 0.0).then_inc(setup, 1)
                    dve.wait_ge(setup, 1)
                    with dve.Fori(0, KC) as c:
                        def after(name):
                            dve.wait_ge(V.sem, V.now(name, c))

                        def step(name, ins):
                            ins.then_inc(V.sem, V.one(name))

                        dve.wait_ge(A.sem, A.now("xr", c))
                        dve.wait_ge(V.sem, V.before("lo", c))
                        step("c0", dve.tensor_scalar(xc, xp[:, 0:T], col("rnn_w", c), col("rnn_b", c), ALU.mult, ALU.add))
                        for k in range(1, RNN_K):
                            after(f"c{k - 1}")
                            step(f"c{k}", dve.scalar_tensor_tensor(xc, xp[:, k:k + T], col("rnn_w", c, k * KC), xc,
                                                                   ALU.mult, ALU.add))
                        dve.wait_ge(A.sem, A.now("gr", c))
                        step("g2", dve.tensor_tensor(q, g, g, ALU.mult))
                        after("g2")
                        step("g3", dve.tensor_scalar(q, q, 0.044715, 1.0, ALU.mult, ALU.add))
                        after("g3")
                        step("g4", dve.tensor_tensor(q, q, g, ALU.mult))
                        dve.wait_ge(A.sem, A.now("thi", c))
                        step("la", dve.tensor_scalar(la, tr, 1.0, col("", c, 0, nsp), ALU.add, ALU.mult))
                        after("la")
                        step("ix", dve.scalar_tensor_tensor(tr, ti, 1.0, xc, ALU.add, ALU.mult))
                        dve.wait_ge(A.sem, A.now("tanh", c))
                        step("den", dve.tensor_scalar(den, tv, -1.0, 1.0, ALU.mult, ALU.add))
                        after("den")
                        step("rden", dve.reciprocal(rden, den))
                        after("rden")
                        step("m2", dve.scalar_tensor_tensor(m2, tv, -2.0, rden, ALU.mult, ALU.mult))
                        dve.wait_ge(A.sem, A.now("gelu", c))
                        step("gate", dve.scalar_tensor_tensor(gt, gt, 1.0, g, ALU.add, ALU.mult))
                        dve.wait_ge(A.sem, A.now("sqrt", c))
                        after("ix")
                        step("u", dve.scalar_tensor_tensor(u, tr, 0.5, sqv, ALU.mult, ALU.mult))
                        after("u")
                        step("h", dve.tensor_tensor_scan(h, av, u, 0.0, ALU.mult, ALU.add))
                        after("h")
                        after("gate")
                        step("r", dve.scalar_tensor_tensor(r, gt, 0.5, h, ALU.mult, ALU.mult))
                        dve.wait_ge(A.sem, A.now("hi", c))
                        after("r")
                        step("lo", dve.tensor_tensor(chunk(a_lo, c), r, chunk(a_hi, c).bitcast(F32), ALU.subtract))
                    dve.wait_ge(V.sem, V.all(KC))

        gated_out("rnn", 4, True)
        split_x(0.5, False)

        def project(name, act_hi, act_lo, from_x):
            with ExitStack() as ctx:
                xr = [sb(f"{name}_x{b}", [P, T], ctx=ctx) for b in range(2)]
                V = Steps(sem(f"{name}_dve", ctx), "res0 lo0 total0 square0 res1 lo1 total1 square1")
                A = Steps(sem(f"{name}_act", ctx), "sq0 sq1")
                sq = tile_in
                x_in = [sem(f"{name}_in{b}", ctx) for b in range(2)]
                setup = sem(f"{name}_setup", ctx)
                with nc.Block() as block:
                    @block.sync
                    def _(sp):
                        loads(sp, name, KC)

                    @block.gpsimd
                    def _(pool):
                        splits(pool, name, KC, hi_by_act=True)

                    @block.tensor
                    def _(pe):
                        with pe.Fori(0, KC // 2) as i:
                            for b in range(2):
                                pe.wait_ge(V.sem, V.before(f"res{b}", i))
                                gemm(pe, b, act_hi, act_lo, i * 4 + (BASE[name] + 2 * b))

                    @block.scalar
                    def _(act):
                        act.sem_inc(A.sem, 2)
                        with act.Fori(0, KC // 2) as i:
                            for b in range(2):
                                if from_x:
                                    hold(act, V.sem, V.before(f"res{b}", i))
                                    act.dma_start(xr[b][:, :], x_t[:, bass.ds(i * (2 * T) + b * T, T)])\
                                       .then_inc(x_in[b], 16)
                            for b in range(2):
                                his(act, name, i, b)
                                hold(act, V.sem, V.now(f"lo{b}", i))
                                hold(act, V.sem, V.now("square0", i) if b else V.before("square1", i))
                                act.activation(sq[:, :], res[:, bass.ds(i * (2 * T) + b * T, T)], ACT.Square)\
                                   .then_inc(A.sem, A.one(f"sq{b}"))

                    @block.vector
                    def _(dve):
                        dve.sem_inc(V.sem, len(V.names))
                        dve.memset(total[:, :], 0.0).then_inc(setup, 1)
                        dve.memset(total2[:, :], 0.0).then_inc(setup, 1)
                        dve.wait_ge(setup, 2)
                        with dve.Fori(0, KC // 2) as i:
                            for b in range(2):
                                at = bass.ds(i * (2 * T) + b * T, T)
                                dve.wait_ge(used, i * 4 + (BASE[name] + 2 * b + 4))
                                if from_x:
                                    dve.wait_ge(x_in[b], i * 16 + 16)
                                    src = xr[b][:, :]
                                else:
                                    src = a_hi[:, at].bitcast(F32)
                                dve.scalar_tensor_tensor(res[:, at], src, ALPHA, psum[:, b, :], ALU.mult, ALU.add)\
                                   .then_inc(V.sem, V.one(f"res{b}"))
                                dve.wait_ge(V.sem, V.now(f"res{b}", i))
                                if from_x:
                                    dve.sem_inc(V.sem, V.one(f"lo{b}"))
                                else:
                                    dve.scalar_tensor_tensor(res[:, at], a_lo[:, at].bitcast(F32), ALPHA, res[:, at],
                                                             ALU.mult, ALU.add).then_inc(V.sem, V.one(f"lo{b}"))
                                    dve.wait_ge(V.sem, V.now(f"lo{b}", i))
                                dve.tensor_tensor(total[:, :], total[:, :], res[:, at], ALU.add)\
                                   .then_inc(V.sem, V.one(f"total{b}"))
                                dve.wait_ge(A.sem, A.now(f"sq{b}", i))
                                dve.tensor_tensor(total2[:, :], total2[:, :], sq[:, :], ALU.add)\
                                   .then_inc(V.sem, V.one(f"square{b}"))
                                dve.wait_ge(V.sem, V.now(f"square{b}", i))

        project("mix", x_hi, x_lo, True)
        layer_norm("ln1", "g1", "be1")

        with ExitStack() as ctx:
            def part(at, n):
                return res[:, at:at + n]

            qh, kh, vt, pr, pt, vtok = (part(0, 2048), part(2048, 1024), part(3072, 1024), part(4096, 1024),
                                        part(5120, 1024), part(6144, 1024))
            stat = sb("att_stat", [P, 4 * TT], ctx=ctx)
            Q = Steps(sem("att_q", ctx), "q0 q1 q2 q3")
            A = Steps(sem("att_act", ctx), "v0 v1 e0 e1 e2 e3 p0 p1 o0 o1 o2 o3")
            V = Steps(sem("att_dve", ctx), "m0 n0 m1 n1 m2 n2 m3 n3 r0 s0 r1 s1 r2 s2 r3 s3 lo0 lo1 lo2 lo3")
            E = Steps(sem("att_pe", ctx), "v s01 s23 p o0 o1 o2 o3")
            kv_in = sem("att_kv_in", ctx)
            with nc.Block() as block:
                @block.sync
                def _(sp):
                    first = BASE["att"] + AHEAD_LOAD
                    with sp.Fori(0, HEADS) as h:
                        hold(sp, E.sem, E.before("s23", h))
                        sp.dma_start(kh.rearrange("p (c n) -> p c n", c=HC),
                                     kv_d[bass.ds(h * HC, HC)].rearrange("c p n -> p c n")).then_inc(kv_in, 16)
                        sp.dma_start(vt.rearrange("p (c n) -> p c n", c=HC),
                                     kv_d[bass.ds(h * HC + KC, HC)].rearrange("c p n -> p c n")).then_inc(kv_in, 16)
                        for s in range(2 * HC):
                            load_half(sp, h * (2 * HC) + (first + s), s % 4)

                @block.gpsimd
                def _(pool):
                    splits(pool, "att", KC)

                @block.tensor
                def _(pe):
                    pe.sem_inc(E.sem, len(E.names))

                    def queries(h, first=False):
                        for c in range(HC):
                            if c >= 2:
                                pe.wait_ge(Q.sem, Q.now(f"q{c - 2}", h))
                            elif not first:
                                pe.wait_ge(V.sem, V.before(f"lo{c + 2}", h - 1))
                            gemm(pe, c % 2, a_hi, a_lo, h * (2 * HC) + (BASE["att"] + 2 * c))

                    def scores(h):
                        pe.wait_ge(kv_in, h * 32 + 32)
                        pe.wait_ge(A.sem, A.before("v1", h))
                        for m in range(2):
                            for c in range(HC):
                                ins = pe.transpose(psum[:, 2 + m, c * P:(c + 1) * P],
                                                   vt[:, c * M + m * P:c * M + (m + 1) * P], ident[:, :])
                        ins.then_inc(E.sem, E.one("v"))
                        pe.wait_ge(Q.sem, Q.now("q3", h))
                        for t in range(TT):
                            if t % 2 == 0:
                                pe.wait_ge(A.sem, A.before(f"e{t + 1}", h))
                            for c in range(HC):
                                ins = pe.matmul(psum[:, 4 + t // 2, (t % 2) * M:(t % 2 + 1) * M],
                                                qh[:, c * T + t * P:c * T + (t + 1) * P], kh[:, c * M:(c + 1) * M],
                                                start=(c == 0), stop=(c == HC - 1))
                            if t % 2:
                                ins.then_inc(E.sem, E.one("s01" if t == 1 else "s23"))

                    def outputs(h, next_q):
                        pe.wait_ge(A.sem, A.before("p1", h))
                        for t in range(TT):
                            pe.wait_ge(V.sem, V.now(f"s{t}", h))
                            for m in range(2):
                                ins = pe.transpose(psum[:, 6 + m, t * P:(t + 1) * P],
                                                   pr[:, t * M + m * P:t * M + (m + 1) * P], ident[:, :])
                        ins.then_inc(E.sem, E.one("p"))
                        pe.wait_ge(A.sem, A.now("p1", h))
                        if next_q:
                            pe.wait_ge(Q.sem, Q.now("q3", h + 1))
                        for c in range(HC):
                            if c >= 2:
                                pe.wait_ge(V.sem, V.now(f"lo{c - 2}", h))
                            for m in range(2):
                                ins = pe.matmul(psum[:, c % 2, :], vtok[:, m * HD + c * P:m * HD + (c + 1) * P],
                                                pt[:, m * T:(m + 1) * T], start=(m == 0), stop=(m == 1))
                            ins.then_inc(E.sem, E.one(f"o{c}"))

                    queries(0, first=True)
                    with pe.Fori(0, HEADS - 1) as h:
                        scores(h)
                        queries(h + 1)
                        outputs(h, True)
                    scores(HEADS - 1)
                    outputs(HEADS - 1, False)

                @block.scalar
                def _(act):
                    act.sem_inc(A.sem, len(A.names))
                    act.sem_inc(Q.sem, len(Q.names))

                    def queries(h):
                        for c in range(HC):
                            hold(act, used, h * (2 * HC) + (BASE["att"] + 2 * c + 4))
                            act.activation(qh[:, c * T:(c + 1) * T], psum[:, c % 2, :], ACT.Copy)\
                               .then_inc(Q.sem, Q.one(f"q{c}"))

                    def head(h, last):
                        act.wait_ge(E.sem, E.now("v", h))
                        hold(act, E.sem, E.before("o3", h))
                        for m in range(2):
                            act.activation(vtok[:, m * HD:(m + 1) * HD], psum[:, 2 + m, :], ACT.Copy)\
                               .then_inc(A.sem, A.one(f"v{m}"))
                        for t in range(TT):
                            act.wait_ge(V.sem, V.now(f"n{t | 1}", h))
                            act.activation(pr[:, t * M:(t + 1) * M], psum[:, 4 + t // 2, (t % 2) * M:(t % 2 + 1) * M],
                                           ACT.Exp, bias=stat[:, TT + t:TT + t + 1], scale=HD ** -0.5,
                                           accum_out=stat[:, 2 * TT + t:2 * TT + t + 1])\
                               .then_inc(A.sem, A.one(f"e{t}"))
                        if not last:
                            hold(act, E.sem, E.now("s23", h))
                            queries(h + 1)
                        act.wait_ge(E.sem, E.now("p", h))
                        for m in range(2):
                            act.activation(pt[:, m * T:(m + 1) * T], psum[:, 6 + m, :], ACT.Copy)\
                               .then_inc(A.sem, A.one(f"p{m}"))
                        for c in range(HC):
                            hold(act, E.sem, E.now(f"o{c}", h))
                            act.activation(x_hi[:, bass.ds(h * (HC * T) + c * T, T)], psum[:, c % 2, :], ACT.Copy)\
                               .then_inc(A.sem, A.one(f"o{c}"))

                    queries(0)
                    with act.Fori(0, HEADS - 1) as h:
                        head(h, False)
                    head(HEADS - 1, True)

                @block.vector
                def _(dve):
                    dve.sem_inc(V.sem, len(V.names))
                    with dve.Fori(0, HEADS) as h:
                        for t in range(TT):
                            dve.wait_ge(E.sem, E.now("s01" if t < 2 else "s23", h))
                            dve.tensor_reduce(stat[:, t:t + 1], psum[:, 4 + t // 2, (t % 2) * M:(t % 2 + 1) * M],
                                              AX_X, ALU.max).then_inc(V.sem, V.one(f"m{t}"))
                            dve.wait_ge(V.sem, V.now(f"m{t}", h))
                            dve.tensor_scalar(stat[:, TT + t:TT + t + 1], stat[:, t:t + 1], -HD ** -0.5, None,
                                              ALU.mult).then_inc(V.sem, V.one(f"n{t}"))
                        for t in range(TT):
                            dve.wait_ge(A.sem, A.now(f"e{t}", h))
                            dve.reciprocal(stat[:, 3 * TT + t:3 * TT + t + 1], stat[:, 2 * TT + t:2 * TT + t + 1])\
                               .then_inc(V.sem, V.one(f"r{t}"))
                            dve.wait_ge(V.sem, V.now(f"r{t}", h))
                            dve.tensor_scalar(pr[:, t * M:(t + 1) * M], pr[:, t * M:(t + 1) * M],
                                              stat[:, 3 * TT + t:3 * TT + t + 1], None, ALU.mult)\
                               .then_inc(V.sem, V.one(f"s{t}"))
                        for c in range(HC):
                            at = bass.ds(h * (HC * T) + c * T, T)
                            dve.wait_ge(A.sem, A.now(f"o{c}", h))
                            dve.tensor_tensor(x_lo[:, at], psum[:, c % 2, :], x_hi[:, at].bitcast(F32), ALU.subtract)\
                               .then_inc(V.sem, V.one(f"lo{c}"))
                    dve.wait_ge(V.sem, V.all(HEADS))

        project("xo", x_hi, x_lo, False)
        layer_norm("ln2", "g2", "be2")

        xctx.close()
        pctx = wctx.enter_context(ExitStack())
        sums = sb("pick_sums", [P, TT * HK], ctx=pctx)
        key1 = sb("pick_key1", [P, TT * HK], ctx=pctx)
        key2 = sb("pick_key2", [P, TT * HK], ctx=pctx)
        sctx = ExitStack()
        scores = sb("scores", [P, TT * 2 * PH * NK], ctx=sctx)
        with ExitStack() as ctx:
            qt = sb("expert_q", [P, PH * T], ctx=ctx)
            keys = sb("sub_keys", [P, NK], ctx=ctx)
            A = Steps(sem("pq_act", ctx), "q0 q1")
            E = sem("pq_scores", ctx)
            S = sem("pq_scores_copied", ctx)
            keys_in = sem("keys_in", ctx)
            with nc.Block() as block:
                @block.sync
                def _(sp):
                    sp.dma_start(keys[:, :], keys_t).then_inc(keys_in, 16)
                    loads(sp, "pq", PH)

                @block.gpsimd
                def _(pool):
                    splits(pool, "pq", PH, hi_by_act=True)

                @block.tensor
                def _(pe):
                    with pe.Fori(0, PH // 2) as i:
                        for b in range(2):
                            pe.wait_ge(A.sem, A.before(f"q{b}", i))
                            gemm(pe, b, a_hi, a_lo, i * 4 + (BASE["pq"] + 2 * b))
                    pe.wait_ge(keys_in, 16)
                    pe.wait_ge(A.sem, A.all(PH // 2))
                    for t in range(TT):
                        if t:
                            pe.wait_ge(S, t)
                        for h in range(PH):
                            for j in range(2):
                                half = slice(j * PKH, (j + 1) * PKH)
                                ins = pe.matmul(psum[:, 2 + 2 * j + h // 4, (h % 4) * P:(h % 4 + 1) * P],
                                                qt[half, h * T + t * P:h * T + (t + 1) * P], keys[half, :],
                                                start=True, stop=True)
                        ins.then_inc(E, 1)

                @block.scalar
                def _(act):
                    act.sem_inc(A.sem, 2)
                    with act.Fori(0, PH // 2) as i:
                        for b in range(2):
                            his(act, "pq", i, b)
                            hold(act, used, i * 4 + (BASE["pq"] + 2 * b + 4))
                            act.activation(qt[:, bass.ds(i * (2 * T) + b * T, T)], psum[:, b, :], ACT.Copy)\
                               .then_inc(A.sem, A.one(f"q{b}"))

                @block.vector
                def _(dve):
                    for t in range(TT):
                        dve.wait_ge(E, t + 1)
                        dve.tensor_copy(scores[:, t * D:(t + 1) * D].rearrange("p (b n) -> p b n", b=4),
                                        psum[:, 2:6, :]).then_inc(S, 1)
                    dve.wait_ge(S, TT)

        class Up:

            def __init__(self, name, ctx):
                self.name = name
                self.h = [sb(f"{name}_h{b}", [P, T], ctx=ctx) for b in range(2)]
                self.q = [sb(f"{name}_q{b}", [P, T], ctx=ctx) for b in range(2)]
                self.A = Steps(sem(f"{name}_up_act", ctx), "h0 h1 th0 th1")
                self.V = Steps(sem(f"{name}_up_dve", ctx), "square0 square1 poly0 poly1 arg0 arg1 gelu0 gelu1")
                self.sent = [sem(f"{name}_sent{b}", ctx) for b in range(2)]

            def start_act(self, act):
                act.sem_inc(self.A.sem, len(self.A.names))
                for b in range(2):
                    act.sem_inc(self.sent[b], 16)

            def start_dve(self, dve):
                dve.sem_inc(self.V.sem, len(self.V.names))

            def dots(self, pe, b, i):
                pe.wait_ge(self.A.sem, self.A.before(f"h{b}", i))
                gemm(pe, b, a_hi, a_lo, i * 4 + (BASE[self.name] + 2 * b))

            def copy(self, act, b, i):
                hold(act, self.sent[b], i * 16 + 16)
                hold(act, used, i * 4 + (BASE[self.name] + 2 * b + 4))
                act.activation(self.h[b][:, :], psum[:, b, :], ACT.Copy).then_inc(self.A.sem, self.A.one(f"h{b}"))

            def tanh_and_store(self, act, i, first_chunk):
                for b in range(2):
                    act.wait_ge(self.V.sem, self.V.now(f"arg{b}", i))
                    act.activation(self.q[b][:, :], self.q[b][:, :], ACT.Tanh, scale=GELU_C)\
                       .then_inc(self.A.sem, self.A.one(f"th{b}"))
                for b in range(2):
                    hold(act, self.V.sem, self.V.now(f"gelu{b}", i))
                    act.dma_start(act_d[bass.ds(i * 2 + (first_chunk + b), 1)].rearrange("a p n -> (a p) n"),
                                  self.h[b][:, :]).then_inc(self.sent[b], 16)

            def gelu(self, dve, i):
                V, A = self.V, self.A
                for b in range(2):
                    dve.wait_ge(A.sem, A.now(f"h{b}", i))
                    dve.wait_ge(V.sem, V.before(f"gelu{b}", i))
                    dve.tensor_tensor(self.q[b][:, :], self.h[b][:, :], self.h[b][:, :], ALU.mult)\
                       .then_inc(V.sem, V.one(f"square{b}"))
                for b in range(2):
                    dve.wait_ge(V.sem, V.now(f"square{b}", i))
                    dve.tensor_scalar(self.q[b][:, :], self.q[b][:, :], 0.044715, 1.0, ALU.mult, ALU.add)\
                       .then_inc(V.sem, V.one(f"poly{b}"))
                for b in range(2):
                    dve.wait_ge(V.sem, V.now(f"poly{b}", i))
                    dve.tensor_tensor(self.q[b][:, :], self.q[b][:, :], self.h[b][:, :], ALU.mult)\
                       .then_inc(V.sem, V.one(f"arg{b}"))
                for b in range(2):
                    dve.wait_ge(A.sem, A.now(f"th{b}", i))
                    dve.wait_ge(V.sem, V.now(f"arg{b}", i))
                    dve.scalar_tensor_tensor(self.h[b][:, :], self.q[b][:, :], 1.0, self.h[b][:, :], ALU.add, ALU.mult)\
                       .then_inc(V.sem, V.one(f"gelu{b}"))

            def finish(self, act, n):
                for b in range(2):
                    act.wait_ge(self.sent[b], (n + 1) * 16)

        UP = ECH // 4
        N_GROUPS = 2 * PH + PH
        SLOTS = UP // TT
        with ExitStack() as ctx:
            up = Up("pick", ctx)
            wide = PH * TOPK * TOPK
            st = sb("pick_scores", [P, D], ctx=ctx)[:, :]
            cand = sb("pick_cand", [P, wide], ctx=ctx)[:, :]
            eq = st
            small = sb("pick_small", [P, 1600], ctx=ctx)
            s16, i16 = small[:, 0:256], small[:, 256:512]
            best, posf1, posf2 = small[:, 512:640], small[:, 640:768], small[:, 768:896]
            usmall = sb("pick_index", [P, 640], U32, ctx=ctx)
            i16u, posu = usmall[:, 0:256], usmall[:, 256:384]
            hiu, lou = usmall[:, 384:512], usmall[:, 512:640]
            chain = sem("pick_chain", ctx)
            p_iter = (PH * 3) // SLOTS
            assert SLOTS == 8 and p_iter == 3

            def heads(v):
                return v.rearrange("p (h k) -> p h k", h=PH)

            with nc.Block() as block:
                @block.sync
                def _(sp):
                    loads(sp, "pick", ECH // 2)

                @block.gpsimd
                def _(pool):
                    splits(pool, "pick", ECH // 2)

                @block.tensor
                def _(pe):
                    with pe.Fori(0, UP) as i:
                        for b in range(2):
                            up.dots(pe, b, i)

                @block.scalar
                def _(act):
                    up.start_act(act)
                    with act.Fori(0, UP) as i:
                        for b in range(2):
                            up.copy(act, b, i)
                        up.tanh_and_store(act, i, 0)
                    up.finish(act, UP)

                @block.vector
                def _(dve):
                    up.start_dve(dve)
                    with dve.Fori(0, TT) as t:
                        n = 0

                        def done(ins):
                            nonlocal n
                            n += 1
                            ins.then_inc(chain, 1)
                            hold(dve, chain, t * PICK_STEPS + n)

                        def top16(searches):
                            nonlocal n
                            for k in range(2):
                                for what in ("max", "index", "drop"):
                                    if k and what == "drop":
                                        continue
                                    for v, s_out, i_out in searches:
                                        s8, i8 = s_out[:, 8 * k:8 * k + 8], i_out[:, 8 * k:8 * k + 8]
                                        if what == "max":
                                            ins = dve.max(s8, v)
                                        elif what == "index":
                                            ins = dve.max_index(i8, s8, v)
                                        else:
                                            ins = dve.match_replace(v, s8, v, -3.0e38)
                                        ins.then_inc(chain, 1)
                                        n += 1
                                    hold(dve, chain, t * PICK_STEPS + n)

                        for k in range(SLOTS):
                            if k == 0:
                                done(dve.tensor_copy(st, scores[:, bass.ts(t, D)]))
                            if k < 5:
                                groups = range(k * 4 - (k // 5), min(k * 4 + 4, 2 * PH)) if k < 4 else ()
                                if groups:
                                    top16([(st[:, g * NK:(g + 1) * NK], s16[:, g * TOPK:(g + 1) * TOPK],
                                            i16u[:, g * TOPK:(g + 1) * TOPK]) for g in groups])
                            if k == 4:
                                done(dve.tensor_copy(i16, i16u))
                                for h in range(PH):
                                    s1 = s16[:, h * TOPK:(h + 1) * TOPK]
                                    s2 = s16[:, (PH + h) * TOPK:(PH + h + 1) * TOPK]
                                    done(dve.tensor_tensor(
                                        cand[:, h * 256:(h + 1) * 256].rearrange("p (i j) -> p i j", i=TOPK),
                                        s1.unsqueeze(2).to_broadcast([P, TOPK, TOPK]),
                                        s2.unsqueeze(1).to_broadcast([P, TOPK, TOPK]), ALU.add))
                            if k in (5, 6):
                                top16([(cand[:, h * 256:(h + 1) * 256], best[:, h * TOPK:(h + 1) * TOPK],
                                        posu[:, h * TOPK:(h + 1) * TOPK]) for h in range((k - 5) * 4, (k - 5) * 4 + 4)])
                            if k == 7:
                                done(dve.tensor_scalar(hiu, posu, 4, None, ALU.logical_shift_right))
                                done(dve.tensor_scalar(lou, posu, 15, None, ALU.bitwise_and))
                                done(dve.tensor_copy(posf1, hiu))
                                done(dve.tensor_copy(posf2, lou))
                                for pos, lst, key in ((posf1, i16[:, 0:HK], key1), (posf2, i16[:, HK:2 * HK], key2)):
                                    v4 = lambda v: v.rearrange("p (h k i) -> p h k i", h=PH, k=TOPK)
                                    done(dve.tensor_tensor(
                                        v4(eq), heads(pos).unsqueeze(3).to_broadcast([P, PH, TOPK, TOPK]),
                                        iota_k[:, 0:TOPK].unsqueeze(1).unsqueeze(1).to_broadcast([P, PH, TOPK, TOPK]),
                                        ALU.is_equal))
                                    done(dve.tensor_tensor(
                                        v4(eq), v4(eq), heads(lst).unsqueeze(2).to_broadcast([P, PH, TOPK, TOPK]),
                                        ALU.mult))
                                    done(dve.tensor_reduce(key[:, bass.ts(t, HK)],
                                                           eq.rearrange("p (m i) -> p m i", i=TOPK), AX_X, ALU.add))
                                done(dve.tensor_tensor(heads(sums[:, bass.ts(t, HK)]), heads(best),
                                                       heads(best)[:, :, 0:1].to_broadcast([P, PH, TOPK]), ALU.subtract))
                            up.gelu(dve, t * SLOTS + k)
                        assert n == PICK_STEPS, n
                    dve.wait_ge(up.V.sem, up.V.all(UP))

        sctx.close()
        tctx = wctx.enter_context(ExitStack())
        turned = [sb(f"turned_{n}", [P, T], ctx=tctx) for n in ("key1", "key2", "gate_hi", "gate_lo")]
        with ExitStack() as ctx:
            tot, rec = (sb(f"soft_{n}", [P, TT * PH], ctx=ctx) for n in ("tot", "rec"))
            s_exp, s_dve, s_pe, s_hi = (sem(f"soft_{n}", ctx) for n in ("exp", "dve", "turned", "copied"))
            with nc.Block() as block:
                @block.scalar
                def _(act):
                    act.activation(sums[:, :], sums[:, :], ACT.Exp).then_inc(s_exp, 1)
                    for k in range(2):
                        act.wait_ge(s_pe, k + 1)
                        act.activation(turned[k][:, :], psum[:, 2 + k, :], ACT.Copy).then_inc(s_hi, 1)
                    act.wait_ge(s_pe, 3)
                    act.activation(turned[2][:, :].bitcast(F32R), psum[:, 4, :], ACT.Copy).then_inc(s_hi, 1)

                @block.vector
                def _(dve):
                    dve.wait_ge(s_exp, 1)
                    v = sums[:, :].rearrange("p (m k) -> p m k", k=TOPK)
                    dve.tensor_reduce(tot[:, :], v, AX_X, ALU.add).then_inc(s_dve, 1)
                    dve.wait_ge(s_dve, 1)
                    dve.tensor_scalar(tot[:, :], tot[:, :], 2.0, None, ALU.mult).then_inc(s_dve, 1)
                    dve.wait_ge(s_dve, 2)
                    dve.reciprocal(rec[:, :], tot[:, :]).then_inc(s_dve, 1)
                    dve.wait_ge(s_dve, 3)
                    dve.tensor_tensor(v, v, rec[:, :].unsqueeze(2).to_broadcast([P, TT * PH, TOPK]), ALU.mult)\
                       .then_inc(s_dve, 1)
                    dve.wait_ge(s_hi, 3)
                    dve.tensor_tensor(turned[3][:, :], psum[:, 4, :], turned[2][:, :], ALU.subtract).then_inc(s_dve, 1)
                    dve.wait_ge(s_dve, 5)

                @block.tensor
                def _(pe):
                    for k, v in enumerate((key1, key2, sums)):
                        if k == 2:
                            pe.wait_ge(s_dve, 4)
                        for t in range(TT):
                            ins = pe.transpose(psum[:, 2 + k, t * P:(t + 1) * P], v[:, t * P:(t + 1) * P], ident[:, :])
                        ins.then_inc(s_pe, 1)

        NB = 8
        BLOCKS = T // GT
        PB = GT // (2 * NB)
        assert BLOCKS * PB == UP
        with ExitStack() as ctx:
            up = Up("gates", ctx)
            hot2, hot1h, hot1l = (sb(f"hot_{n}", [P, NB * P], F32R, ctx=ctx) for n in ("second", "first_hi", "first_lo"))
            hot1 = sb("hot_first", [P, NB * P], ctx=ctx)
            stage = sb("gate_stage", [P, ECH * GT], ctx=ctx)
            H = Steps(sem("hot_dve", ctx), "second0 first0 hi0 lo0 second1 first1 hi1 lo1")
            E = Steps(sem("hot_pe", ctx), "spread0 spread1")
            C = Steps(sem("hot_act", ctx), "c00 c01 c10 c11")
            gate_sent = sem("gate_sent", ctx)
            with nc.Block() as block:
                @block.sync
                def _(sp):
                    loads(sp, "gates", ECH // 2)

                @block.gpsimd
                def _(pool):
                    splits(pool, "gates", ECH // 2)

                @block.tensor
                def _(pe):
                    pe.sem_inc(E.sem, 2)
                    with pe.Fori(0, UP) as i:
                        for b in range(2):
                            up.dots(pe, b, i)
                            pe.wait_ge(H.sem, H.now(f"lo{b}", i))
                            pe.wait_ge(C.sem, C.before(f"c{b}1", i))
                            for j in range(NB):
                                at = slice(j * P, (j + 1) * P)
                                bank = psum[:, 2 + 2 * b + j // 4, (j % 4) * P:(j % 4 + 1) * P]
                                pe.matmul(bank, hot2[:, at], hot1h[:, at], start=True, stop=False)
                                ins = pe.matmul(bank, hot2[:, at], hot1l[:, at], start=False, stop=True)
                            ins.then_inc(E.sem, E.one(f"spread{b}"))

                @block.scalar
                def _(act):
                    up.start_act(act)
                    act.sem_inc(C.sem, 4)
                    act.sem_inc(gate_sent, 16)
                    with act.Fori(0, BLOCKS) as blk:
                        with act.Fori(0, PB) as k:
                            i = blk * PB + k
                            for b in range(2):
                                up.copy(act, b, i)
                                if b == 0:
                                    hold(act, gate_sent, blk * 16 + 16)
                                hold(act, E.sem, E.now(f"spread{b}", i))
                                for q in range(2):
                                    to = stage[:, :].rearrange("p (e t) -> p t e", t=GT)[
                                        :, bass.ds(k * (2 * NB) + (NB * b + 4 * q), 4), :]
                                    act.activation(to, psum[:, 2 + 2 * b + q, :].rearrange("p (t e) -> p t e", t=4),
                                                   ACT.Copy).then_inc(C.sem, C.one(f"c{b}{q}"))
                            up.tanh_and_store(act, i, ECH // 2)
                        hold(act, C.sem, blk * (4 * PB) + (4 * PB + 4))
                        act.dma_start(gate_d[bass.ds(blk, 1)].rearrange("a p e t -> (a p) (e t)"), stage[:, :])\
                           .then_inc(gate_sent, 16)
                    up.finish(act, UP)
                    act.wait_ge(gate_sent, (BLOCKS + 1) * 16)

                @block.vector
                def _(dve):
                    up.start_dve(dve)
                    dve.sem_inc(H.sem, len(H.names))
                    shape = [P, NB, P]
                    v3 = lambda v: v.rearrange("p (t e) -> p t e", e=P)
                    keys = iota_k[:, :].unsqueeze(1).to_broadcast(shape)
                    with dve.Fori(0, UP) as i:
                        for b in range(2):
                            def of(v):
                                return v[:, bass.ds(i * (2 * NB) + NB * b, NB)].unsqueeze(2).to_broadcast(shape)

                            k1, k2, g_hi, g_lo = turned
                            dve.wait_ge(E.sem, E.now("spread0", i) if b else E.before("spread1", i))
                            dve.tensor_tensor(v3(hot2[:, :]), keys, of(k2), ALU.is_equal)\
                               .then_inc(H.sem, H.one(f"second{b}"))
                            dve.wait_ge(H.sem, H.now("lo0", i) if b else H.before("lo1", i))
                            dve.tensor_tensor(v3(hot1[:, :]), keys, of(k1), ALU.is_equal)\
                               .then_inc(H.sem, H.one(f"first{b}"))
                            dve.wait_ge(H.sem, H.now(f"first{b}", i))
                            dve.tensor_tensor(v3(hot1h[:, :]), v3(hot1[:, :]), of(g_hi), ALU.mult)\
                               .then_inc(H.sem, H.one(f"hi{b}"))
                            dve.tensor_tensor(v3(hot1l[:, :]), v3(hot1[:, :]), of(g_lo), ALU.mult)\
                               .then_inc(H.sem, H.one(f"lo{b}"))
                        up.gelu(dve, i)
                    dve.wait_ge(up.V.sem, up.V.all(UP))
                    dve.wait_ge(H.sem, H.all(UP))

        tctx.close()
        pctx.close()

        with ExitStack() as ctx:
            NQ = KC // 4
            acts = [sb(f"first_acts{b}", [P, NQ * T], ctx=ctx) for b in range(4)]
            gates = [sb(f"first_gates{b}", [P, NQ * T], ctx=ctx) for b in range(4)]
            come = [sem(f"first_in{b}", ctx) for b in range(4)]
            mul, hi, lo = (sem(f"first_{n}", ctx) for n in ("mul", "hi", "lo"))
            with nc.Block() as block:
                @block.sync
                def _(sp):
                    for q in range(4):
                        sp.dma_start(acts[q][:, :].rearrange("p (a n) -> p a n", a=NQ),
                                     act_d[q * NQ:(q + 1) * NQ].rearrange("a p n -> p a n")).then_inc(come[q], 16)
                        sp.dma_start(gates[q][:, :].rearrange("p (k e t) -> p k e t", e=NQ, t=GT),
                                     gate_d[:, :, q * NQ:(q + 1) * NQ, :].rearrange("k p e t -> p k e t"))\
                          .then_inc(come[q], 16)

                @block.scalar
                def _(act):
                    for q in range(4):
                        act.wait_ge(mul, q + 1)
                        act.activation(a_hi[:, q * NQ * T:(q + 1) * NQ * T], acts[q][:, :], ACT.Copy).then_inc(hi, 1)

                @block.vector
                def _(dve):
                    def rest(q):
                        dve.wait_ge(hi, q + 1)
                        at = slice(q * NQ * T, (q + 1) * NQ * T)
                        dve.tensor_tensor(a_lo[:, at], acts[q][:, :], a_hi[:, at].bitcast(F32), ALU.subtract)\
                           .then_inc(lo, 1)

                    for q in range(4):
                        dve.wait_ge(come[q], 32)
                        v = acts[q][:, :].rearrange("p (e k t) -> p e k t", e=NQ, t=GT)
                        dve.tensor_tensor(v, v, gates[q][:, :].rearrange("p (k e t) -> p e k t", e=NQ, t=GT), ALU.mult)\
                           .then_inc(mul, 1)
                        if q:
                            rest(q - 1)
                    rest(3)
                    dve.wait_ge(lo, 4)

        with ExitStack() as ctx:
            b_hi = sb("b_hi", [P, KC * T], F32R, ctx=ctx)
            b_lo = sb("b_lo", [P, KC * T], F32R, ctx=ctx)
            ah, ag = sb("down_acts", [P, 2 * T], ctx=ctx), work
            V = Steps(sem("down_prep", ctx), "mul0 mul1 lo0 lo1")
            A = Steps(sem("down_hi", ctx), "hi0 hi1")
            S = Steps(sem("down_sum", ctx), "sum0 sum1")
            come = sem("down_in", ctx)
            setup = sem("down_setup", ctx)
            NP = KC // 2
            pair = [(a_hi, a_lo), (b_hi, b_lo)]

            def groups(body):
                def run(eng):
                    with eng.Fori(0, EG // 2 - 1) as gg:
                        for parity in range(2):
                            body(eng, gg * 2 + parity, parity, True)
                    body(eng, EG - 2, 0, True)
                    body(eng, EG - 1, 1, False)
                return run

            with nc.Block() as block:
                @block.sync
                def _(sp):
                    def fetch(sp, j):
                        hold(sp, V.sem, V.before("lo1", j))
                        sp.dma_start(ah[:, :].rearrange("p (b n) -> p b n", b=2),
                                     act_d[bass.ds(j * 2 + KC, 2)].rearrange("b p n -> p b n")).then_inc(come, 16)
                        sp.dma_start(ag[:, :].rearrange("p (k b t) -> p k b t", b=2, t=GT),
                                     gate_d[:, :, bass.ds(j * 2 + KC, 2), :].rearrange("k p b t -> p k b t"))\
                          .then_inc(come, 16)

                    def body(sp, g, parity, prepare):
                        def one(i, more):
                            for s in range(4):
                                load_half(sp, i * 4 + (BASE["down"] + AHEAD_LOAD + s), s)
                                if s == 1 and more:
                                    fetch(sp, i + 1)

                        if isinstance(g, int):
                            with sp.Fori(0, NP - 1) as k:
                                one(k + g * NP, prepare)
                            if prepare:
                                one((g + 1) * NP - 1, False)
                        else:
                            with sp.Fori(0, NP) as k:
                                one(g * NP + k, True)

                    fetch(sp, 0)
                    groups(body)(sp)

                @block.gpsimd
                def _(pool):
                    splits(pool, "down", ECH, hi_by_act=True)

                @block.tensor
                def _(pe):
                    def body(pe, g, parity, prepare):
                        hold(pe, V.sem, g * (NP * 4) + 4)
                        with pe.Fori(0, NP) as k:
                            i = g * NP + k
                            for b in range(2):
                                pe.wait_ge(S.sem, S.before(f"sum{b}", i))
                                gemm(pe, b, *pair[parity], i * 4 + (BASE["down"] + 2 * b))
                    groups(body)(pe)

                @block.scalar
                def _(act):
                    act.sem_inc(A.sem, 2)

                    def body(act, g, parity, prepare):
                        def one(i, k, last=False):
                            if prepare:
                                for b in range(2):
                                    hold(act, V.sem, V.now(f"mul{b}", i))
                                    act.activation(pair[1 - parity][0][:, bass.ds(k * (2 * T) + b * T, T)],
                                                   ah[:, b * T:(b + 1) * T], ACT.Copy).then_inc(A.sem, A.one(f"hi{b}"))
                            for b in range(1 if last else 2):
                                his(act, "down", i, b)

                        if prepare:
                            with act.Fori(0, NP) as k:
                                one(g * NP + k, k)
                        else:
                            with act.Fori(0, NP - 1) as k:
                                one(k + g * NP, k)
                            one(g * NP + NP - 1, NP - 1, last=True)
                    groups(body)(act)

                @block.vector
                def _(dve):
                    dve.sem_inc(V.sem, 4)
                    dve.sem_inc(S.sem, 2)
                    dve.tensor_scalar(res[:, :], res[:, :], ALPHA, None, ALU.mult).then_inc(setup, 1)
                    dve.memset(total[:, :], 0.0).then_inc(setup, 1)
                    dve.memset(total2[:, :], 0.0).then_inc(setup, 1)
                    dve.wait_ge(setup, 3)

                    def prep(i, k, to):
                        dve.wait_ge(come, i * 32 + 32)
                        for b in range(2):
                            a = ah[:, b * T:(b + 1) * T].rearrange("p (k t) -> p k t", t=GT)
                            gate = ag[:, :].rearrange("p (k b t) -> p b k t", b=2, t=GT)[:, b]
                            dve.tensor_tensor(a, a, gate, ALU.mult).then_inc(V.sem, V.one(f"mul{b}"))
                        for b in range(2):
                            at = bass.ds(k * (2 * T) + b * T, T)
                            dve.wait_ge(V.sem, V.now(f"mul{b}", i))
                            dve.wait_ge(A.sem, A.now(f"hi{b}", i))
                            dve.tensor_tensor(to[1][:, at], ah[:, b * T:(b + 1) * T], to[0][:, at].bitcast(F32),
                                              ALU.subtract).then_inc(V.sem, V.one(f"lo{b}"))

                    def body(dve, g, parity, prepare):
                        hold(dve, S.sem, g * (NP * 2) + 2)
                        with dve.Fori(0, NP) as k:
                            i = g * NP + k
                            if prepare:
                                prep(i, k, pair[1 - parity])
                            for b in range(2):
                                r = res[:, bass.ds(k * (2 * T) + b * T, T)]
                                dve.wait_ge(used, i * 4 + (BASE["down"] + 2 * b + 4))
                                dve.tensor_tensor(r, r, psum[:, b, :], ALU.add).then_inc(S.sem, S.one(f"sum{b}"))
                    groups(body)(dve)
                    dve.wait_ge(S.sem, S.all(EG * NP))

        with ExitStack() as ctx:
            sq = [sb(f"last_sq{b}", [P, T], ctx=ctx) for b in range(2)]
            A = Steps(sem("last_act", ctx), "sq0 sq1")
            V = Steps(sem("last_dve", ctx), "total0 square0 total1 square1")
            with nc.Block() as block:
                @block.scalar
                def _(act):
                    act.sem_inc(A.sem, 2)
                    with act.Fori(0, KC // 2) as i:
                        for b in range(2):
                            hold(act, V.sem, V.before(f"square{b}", i))
                            act.activation(sq[b][:, :], res[:, bass.ds(i * (2 * T) + b * T, T)], ACT.Square)\
                               .then_inc(A.sem, A.one(f"sq{b}"))

                @block.vector
                def _(dve):
                    dve.sem_inc(V.sem, len(V.names))
                    with dve.Fori(0, KC // 2) as i:
                        for b in range(2):
                            dve.wait_ge(V.sem, V.now("total0", i) if b else V.before("total1", i))
                            dve.tensor_tensor(total[:, :], total[:, :], res[:, bass.ds(i * (2 * T) + b * T, T)], ALU.add)\
                               .then_inc(V.sem, V.one(f"total{b}"))
                            dve.wait_ge(A.sem, A.now(f"sq{b}", i))
                            dve.wait_ge(V.sem, V.now("square0", i) if b else V.before("square1", i))
                            dve.tensor_tensor(total2[:, :], total2[:, :], sq[b][:, :], ALU.add)\
                               .then_inc(V.sem, V.one(f"square{b}"))
                    dve.wait_ge(V.sem, V.all(KC // 2))

        layer_norm("ln3", "g3", "be3", turned_out=out)


PICK_STEPS = 1 + 16 * 5 + 1 + 8 + 8 * 5 + 4 + 6 + 1


_OUT = (1, T, D)


def kernel(**inputs):
    import numpy as np
    import concourse.bacc as bacc
    from concourse.bass_utils import run_bass_kernel_spmd as run

    a = {k: np.asarray(v) for k, v in inputs.items()}

    def chunks(w):
        n = w.shape[1] // P
        return w.reshape(2, HALF, P, n, P).transpose(3, 0, 2, 1, 4).reshape(n, 2, P, WH)

    def pairs(u, v):
        return np.stack([chunks(u), chunks(v)], axis=1).reshape(-1, 2, P, WH)

    w = a["w_in"][0]
    xr, gr, ca, cg, g_rnn, g_conf = (w[:, i * D:(i + 1) * D] for i in range(6))
    stream = np.concatenate([
        chunks(a["xa_w_k"][0]), chunks(a["xa_w_v"][0]), pairs(cg, ca), pairs(g_conf, a["w_conf_out"][0]),
        pairs(xr, gr), pairs(g_rnn, a["w_rnn_out"][0]), chunks(a["w_mix_out"][0]), chunks(a["xa_w_q"][0]),
        chunks(a["xa_w_o"][0]), chunks(a["peer_w_q"][0]), chunks(a["peer_u"][0].T),
        *[chunks(a["peer_v"][0][g * D:(g + 1) * D]) for g in range(EG)]]).reshape(-1, P, WH)

    def cols(v):
        return v.reshape(-1, P).T

    vecs = np.ascontiguousarray(np.concatenate([
        cols(a[n][0]) for n in ("b_in", "rnn_conv_w", "rnn_conv_b", "rnn_b_a", "rnn_b_x", "rnn_lambda", "conf_dw_w",
                                "conf_dw_b", "conf_ln_g", "conf_ln_b", "b_conf_out", "ln1_g", "ln1_b", "ln2_g",
                                "ln2_b", "ln3_g", "ln3_b")], axis=1))

    def turned(v):
        t = v.reshape(v.shape[0], KC, P)
        return np.ascontiguousarray(t.transpose(2, 1, 0)).reshape(P, -1)

    arrays = {
        "wstream": stream,
        "x_t": turned(a["x"][0]),
        "mem_t": turned(a["mem"][0]),
        "vecs": vecs,
        "gates_w": np.ascontiguousarray(np.concatenate([a["rnn_w_a"][0], a["rnn_w_x"][0]], axis=2)),
        "ident_d": np.eye(P, dtype=np.float32),
        "keys_t": np.ascontiguousarray(a["peer_sub_keys"][0].transpose(0, 2, 1)).reshape(P, NK),
    }
    nc = bacc.Bacc("TRN2", target_bir_lowering=False, num_devices=1)
    args = [nc.dram_tensor(n, v.shape, F32, kind="ExternalInput").ap() for n, v in arrays.items()]
    o = nc.dram_tensor("out", (TT, P, D), F32, kind="ExternalOutput").ap()
    build(nc, *args, o)
    r = run(nc, [arrays], core_ids=[0])
    return r.results[0]["out"].reshape(_OUT)
```

```python
from contextlib import ExitStack

import concourse.bass as bass
from concourse import mybir

F32 = mybir.dt.float32
F32R = mybir.dt.float32r
U32 = mybir.dt.uint32
ACT = mybir.ActivationFunctionType
ALU = mybir.AluOpType
AX_X = mybir.AxisListType.X

P = 128
D = 2048
T = 512
KC = D // P
HALF = KC // 2
WH = HALF * P
M = 256
RNN_K, CONF_K = 4, 31
HEADS, HD = 4, 512
HC = HD // P
PH, NK, TOPK, PKH = 8, 128, 16, 64
HK = PH * TOPK
N_EXPERTS = NK * NK
TT = T // P
GT = 64
ALPHA = 2.0 ** 0.25
EPS = 1e-5
GELU_C = 0.7978845608028654
PICK_STEPS = 1 + 16 * 5 + 1 + 8 + 8 * 5 + 4 + 6 + 1
EG = N_EXPERTS // D
ECH = N_EXPERTS // P

COLS = {}
_at = 0
for _name, _n in (("b_in", 6 * KC), ("rnn_w", RNN_K * KC), ("rnn_b", KC), ("b_a", KC), ("b_x", KC), ("lam", KC),
                  ("conf_w", CONF_K * KC), ("conf_b", KC), ("conf_g", KC), ("conf_be", KC), ("b_out", KC),
                  ("g1", KC), ("be1", KC), ("g2", KC), ("be2", KC), ("g3", KC), ("be3", KC)):
    COLS[_name] = _at
    _at += _n
NCOLS = _at

STAGE_CHUNKS = (("glu", 2 * KC), ("gconf", KC), ("conf", KC), ("lru", 2 * KC), ("rnn", 2 * KC),
                ("mix", KC), ("kv", 2 * KC), ("att", KC), ("xo", KC), ("pq", PH), ("pick", ECH // 2),
                ("gates", ECH // 2), ("down", ECH))
BASE = {}
_at = 0
for _name, _n in STAGE_CHUNKS:
    BASE[_name] = 2 * _at
    _at += _n
HALVES = 2 * _at
AHEAD_LOAD, AHEAD_SPLIT = 4, 2


class Steps:

    def __init__(self, sem, names):
        self.sem, self.names, self.at = sem, names.split(), 0

    def one(self, name):
        assert self.names[self.at % len(self.names)] == name, (name, self.names[self.at % len(self.names)])
        self.at += 1
        return 1

    def now(self, name, i=0):
        return i * len(self.names) + (len(self.names) + self.names.index(name) + 1)

    def before(self, name, i=0):
        return i * len(self.names) + (self.names.index(name) + 1)

    def all(self, n):
        return (n + 1) * len(self.names)


def build(nc, wstream, x_t, mem_t, vecs, gates_w, ident_d, keys_t, out):
    top = ExitStack()
    with top:
        def sb(name, shape, dt=F32, ctx=top):
            return ctx.enter_context(nc.sbuf_tensor(name, shape, dt))

        def sem(name, ctx=top):
            return ctx.enter_context(nc.semaphore(name))

        psum = top.enter_context(nc.psum_tensor("psum", [P, 8, 512], F32))
        vec = sb("vec", [P, NCOLS])
        hb_in = sb("hb_in", [P, 6 * KC])
        hb_ax = sb("hb_ax", [P, 2 * KC])
        nsp = sb("nsp", [P, KC])
        hcw = sb("hcw", [P, CONF_K * KC])
        ident = sb("ident", [P, P])
        iota_k = sb("iota_k", [P, P])
        iota_u = sb("iota_u", [P, P], U32)
        ones = sb("ones", [P, P])
        zero = sb("zero", [P, 1])
        kv_d = nc.dram_tensor("kv_scratch", (2 * KC, P, M), F32).ap()
        th_d = nc.dram_tensor("conf_gate_scratch", (KC, P, T), F32).ap()
        conf_d = nc.dram_tensor("conf_scratch", (KC, P, T), F32).ap()
        act_d = nc.dram_tensor("expert_act_scratch", (ECH, P, T), F32).ap()
        gate_d = nc.dram_tensor("gate_scratch", (T // GT, P, ECH, GT), F32).ap()

        loaded = [sem(f"weights_loaded{i}") for i in range(4)]
        hi_made = sem("weights_hi_made")
        split = sem("weights_split")
        raw_free = sem("weights_raw_free")
        used = sem("weights_used")
        alone = sem("wait_passed")

        def hold(eng, s, value):
            eng.wait_ge(s, value)
            eng.sem_inc(alone, 1)

        res = sb("res", [P, KC * T])
        wctx = top.enter_context(ExitStack())
        w_raw = [sb(f"w_raw{i}", [P, WH], ctx=wctx) for i in range(2)]
        w_hi = [sb(f"w_hi{i}", [P, WH], F32R, ctx=wctx) for i in range(2)]
        w_lo = [sb(f"w_lo{i}", [P, WH], F32R, ctx=wctx) for i in range(2)]
        stream = wstream

        def load_half(sp, g, s):
            hold(sp, raw_free, g + 1)
            sp.dma_start(w_raw[s % 2][:, :], stream[bass.ds(g, 1)].rearrange("a p n -> (a p) n")).then_inc(loaded[s], 16)

        def his(act, name, i, b):
            for s in range(2):
                ahead = BASE[name] + AHEAD_SPLIT + 2 * b + s
                slot = ahead % 4
                hold(act, loaded[slot], i * 16 + (ahead // 4 * 16 + 16))
                hold(act, used, i * 4 + (ahead + 1))
                act.activation(w_hi[slot % 2][:, :], w_raw[slot % 2][:, :], ACT.Copy).then_inc(hi_made, 1)

        def split_half(eng, g, round_, s, hi_by_act=False):
            if not hi_by_act:
                hold(eng, loaded[s], round_ * 16 + 16)
                hold(eng, used, g + 1)
                eng.tensor_tensor(w_hi[s % 2][:, :], w_raw[s % 2][:, :], zero[:, :].to_broadcast([P, WH]), ALU.add)\
                    .then_inc(hi_made, 1)
            eng.wait_ge(hi_made, g + 1)
            eng.tensor_tensor(w_lo[s % 2][:, :], w_raw[s % 2][:, :], w_hi[s % 2][:, :].bitcast(F32),
                              ALU.subtract).then_inc(split, 1)
            eng.wait_ge(split, g + 1)
            eng.sem_inc(raw_free, 1)

        def loads(sp, name, n_chunks, skip=0):
            first, last = BASE[name] + 2 * skip + AHEAD_LOAD, min(BASE[name] + 2 * n_chunks + AHEAD_LOAD, HALVES)
            n = (last - first) // 4
            with sp.Fori(0, n) as i:
                for s in range(4):
                    load_half(sp, i * 4 + (first + s), (first + s) % 4)
            for g in range(first + 4 * n, last):
                load_half(sp, g, g % 4)

        def splits(eng, name, n_chunks, skip=0, hi_by_act=False):
            first, last = BASE[name] + 2 * skip + AHEAD_SPLIT, min(BASE[name] + 2 * n_chunks + AHEAD_SPLIT, HALVES)
            n = (last - first) // 4
            with eng.Fori(0, n) as i:
                for s in range(4):
                    split_half(eng, i * 4 + (first + s), i + (first + s) // 4, (first + s) % 4, hi_by_act)
            for g in range(first + 4 * n, last):
                split_half(eng, g, g // 4, g % 4, hi_by_act)

        def gemm(pe, bank, act_hi, act_lo, g, n=T):
            for half in range(2):
                pe.wait_ge(split, g + (half + 1))
                for k in range(HALF):
                    kk = half * HALF + k
                    wh, wl = (w[half][:, k * P:(k + 1) * P] for w in (w_hi, w_lo))
                    xh, xl = (a[:, kk * n:(kk + 1) * n] for a in (act_hi, act_lo))
                    pe.matmul(psum[:, bank, 0:n], wh, xh, start=(kk == 0), stop=False)
                    pe.matmul(psum[:, bank, 0:n], wh, xl, start=False, stop=False)
                    last = pe.matmul(psum[:, bank, 0:n], wl, xh, start=False, stop=(kk == KC - 1))
                last.then_inc(used, 1)

        def chunk(t, c, n=T):
            return t[:, bass.ts(c, n)]

        def col(name, c, k=0, t=None):
            return (vec if t is None else t)[:, bass.ds(c + ((COLS[name] if t is None else 0) + k), 1)]

        a_hi = sb("a_hi", [P, KC * T], F32R, ctx=wctx)
        a_lo = sb("a_lo", [P, KC * T], F32R, ctx=wctx)
        total = sb("total", [P, T], ctx=wctx)
        total2 = sb("total2", [P, T], ctx=wctx)
        work = sb("work", [P, 2 * T], ctx=wctx)
        tile_in, rstd = work[:, 0:T], work[:, T:2 * T]
        xctx = ExitStack()
        wctx.enter_context(xctx)
        x_hi = sb("x_hi", [P, KC * T], F32R, ctx=xctx)
        x_lo = sb("x_lo", [P, KC * T], F32R, ctx=xctx)
        tile = [res[:, k * T:(k + 1) * T] for k in range(KC)]
        const = [total[:, k * KC:(k + 1) * KC] for k in range(8)]

        const_in, c_d, c_a, c_p = sem("const_in"), sem("c_dve"), sem("c_act"), sem("c_pool")
        x_in, x_hi_made, x_lo_made = [sem(f"x_in{q}") for q in range(4)], sem("x_hi_made"), sem("x_lo_made")
        Q = KC * T // 4
        quarter = [slice(q * Q, (q + 1) * Q) for q in range(4)]
        with nc.Block() as block:
            @block.sync
            def _(sp):
                sp.dma_start(vec[:, :], vecs).then_inc(const_in, 16)
                sp.dma_start(ident[:, :], ident_d).then_inc(const_in, 16)
                sp.wait_ge(raw_free, 2)
                for g in range(2):
                    sp.dma_start(w_raw[g][:, :], stream[g]).then_inc(loaded[g], 16)
                for q in range(4):
                    sp.dma_start(res[:, quarter[q]], x_t[:, quarter[q]]).then_inc(x_in[q], 16)
                for g in range(2, AHEAD_LOAD):
                    sp.wait_ge(raw_free, g + 1)
                    sp.dma_start(w_raw[g % 2][:, :], stream[g]).then_inc(loaded[g], 16)

            @block.gpsimd
            def _(pool):
                pool.sem_inc(raw_free, 2)
                pool.memset(zero[:, :], 0.0).then_inc(c_p, 1)
                pool.memset(ones[:, :], 1.0 / D).then_inc(c_p, 1)
                pool.iota(iota_u[:, :], [[1, P]], base=0, channel_multiplier=0).then_inc(c_p, 1)
                pool.wait_ge(c_p, 3)
                for g in range(AHEAD_SPLIT):
                    split_half(pool, g, 0, g)

            @block.tensor
            def _(pe):
                pe.sem_inc(used, 2)

            @block.scalar
            def _(act):
                act.wait_ge(c_d, 1)
                act.activation(const[0], const[1], ACT.Exp, scale=-1.0).then_inc(c_a, 1)
                act.wait_ge(c_d, 3)
                act.activation(const[3], const[2], ACT.Ln).then_inc(c_a, 1)
                for q in range(4):
                    act.wait_ge(x_in[q], 16)
                    act.activation(x_hi[:, quarter[q]], res[:, quarter[q]], ACT.Copy).then_inc(x_hi_made, 1)

            @block.vector
            def _(dve):
                n = 0

                def done(ins):
                    nonlocal n
                    n += 1
                    ins.then_inc(c_d, 1)
                    dve.wait_ge(c_d, n)

                dve.wait_ge(const_in, 32)
                dve.wait_ge(c_p, 3)
                lam = vec[:, COLS["lam"]:COLS["lam"] + KC]
                e, ab, w, lw, t1, t2, t3, t4 = const
                done(dve.scalar_tensor_tensor(ab, lam, -1.0, lam, ALU.mult, ALU.max))
                dve.wait_ge(c_a, 1)
                done(dve.tensor_scalar(w, e, 1.0, None, ALU.add))
                done(dve.tensor_scalar(t1, w, -1.0, None, ALU.add))
                done(dve.tensor_scalar(t2, t1, 0.0, None, ALU.is_equal))
                done(dve.tensor_tensor(t1, t1, t2, ALU.add))
                done(dve.reciprocal(t3, t1))
                dve.wait_ge(c_a, 2)
                done(dve.tensor_tensor(lw, lw, t2, ALU.add))
                done(dve.tensor_tensor(lw, lw, t3, ALU.mult))
                done(dve.tensor_tensor(lw, lw, e, ALU.mult))
                done(dve.tensor_scalar(t4, lam, -1.0, 0.0, ALU.mult, ALU.max))
                done(dve.tensor_tensor(lw, lw, t4, ALU.add))
                done(dve.tensor_scalar(nsp[:, :], lw, -4.0, None, ALU.mult))
                done(dve.tensor_copy(iota_k[:, :], iota_u[:, :]))
                done(dve.tensor_scalar(hb_in[:, :], vec[:, 0:6 * KC], 0.5, None, ALU.mult))
                done(dve.tensor_scalar(hb_ax[:, :], vec[:, COLS["b_a"]:COLS["b_a"] + 2 * KC], 0.5, None, ALU.mult))
                done(dve.tensor_scalar(hcw[:, :], vec[:, COLS["conf_w"]:COLS["conf_w"] + CONF_K * KC], 0.5, None,
                                       ALU.mult))
                for q in range(4):
                    dve.wait_ge(x_hi_made, q + 1)
                    dve.tensor_tensor(x_lo[:, quarter[q]], res[:, quarter[q]], x_hi[:, quarter[q]].bitcast(F32),
                                      ALU.subtract).then_inc(x_lo_made, 1)
                dve.wait_ge(x_lo_made, 4)

        PAD = CONF_K - 1
        with ExitStack() as ctx:
            th = rstd
            cab = sb("glu_ca", [P, T], ctx=ctx)
            xp = sb("glu_padded", [P, PAD + T], ctx=ctx)
            odd = sb("glu_odd", [P, T], ctx=ctx)
            A = Steps(sem("glu_act", ctx), "th ca")
            SQ = Steps(sem("glu_squared", ctx), "sq")
            V = Steps(sem("glu_dve", ctx), "glu " + " ".join(f"tap{k}" for k in range(CONF_K)))
            G = Steps(sem("glu_pool", ctx), "join total total2")
            padded, zeroed = sem("glu_pad_zeroed", ctx), sem("glu_totals_zeroed", ctx)
            with nc.Block() as block:
                @block.sync
                def _(sp):
                    loads(sp, "glu", 2 * KC + 2)

                @block.gpsimd
                def _(pool):
                    def totals(c):
                        hold(pool, V.sem, V.now(f"tap{CONF_K - 1}", c - 1))
                        pool.tensor_tensor(chunk(res, c - 1), chunk(res, c - 1), odd[:, :], ALU.add)\
                            .then_inc(G.sem, G.one("join"))
                        hold(pool, G.sem, G.now("join", c - 1))
                        pool.tensor_tensor(total[:, :], total[:, :], chunk(res, c - 1), ALU.add)\
                            .then_inc(G.sem, G.one("total"))
                        pool.wait_ge(SQ.sem, SQ.now("sq", c - 1))
                        pool.tensor_tensor(total2[:, :], total2[:, :], tile_in[:, :], ALU.add)\
                            .then_inc(G.sem, G.one("total2"))

                    pool.sem_inc(G.sem, len(G.names))
                    pool.memset(total[:, :], 0.0).then_inc(zeroed, 1)
                    pool.memset(total2[:, :], 0.0).then_inc(zeroed, 1)
                    pool.wait_ge(zeroed, 2)
                    first = BASE["glu"] + AHEAD_SPLIT
                    for s in range(4):
                        split_half(pool, first + s, (first + s) // 4, (first + s) % 4, hi_by_act=True)
                    with pool.Fori(0, KC - 1) as c:
                        for s in range(4):
                            split_half(pool, c * 4 + (first + 4 + s), c, (first + s) % 4, hi_by_act=True)
                        totals(c + 1)
                    for s in range(4):
                        split_half(pool, first + 4 * KC + s, KC, (first + s) % 4, hi_by_act=True)
                    totals(KC)
                    pool.wait_ge(G.sem, G.all(KC))

                @block.tensor
                def _(pe):
                    with pe.Fori(0, KC) as c:
                        pe.wait_ge(A.sem, A.before("th", c))
                        gemm(pe, 0, x_hi, x_lo, c * 4 + BASE["glu"])
                        pe.wait_ge(A.sem, A.before("ca", c))
                        gemm(pe, 1, x_hi, x_lo, c * 4 + (BASE["glu"] + 2))
                    for b, name in enumerate(("th", "ca")):
                        pe.wait_ge(A.sem, A.before(name, KC))
                        gemm(pe, b, x_hi, x_lo, BASE["gconf"] + 2 * b)

                @block.scalar
                def _(act):
                    act.sem_inc(A.sem, len(A.names))
                    act.sem_inc(SQ.sem, 1)

                    def square(c):
                        hold(act, G.sem, G.now("join", c))
                        act.activation(tile_in[:, :], chunk(res, c), ACT.Square).then_inc(SQ.sem, SQ.one("sq"))

                    def body(c, first):
                        his(act, "glu", c, 0)
                        hold(act, V.sem, V.before("glu", c))
                        hold(act, used, c * 4 + (BASE["glu"] + 4))
                        act.activation(th, psum[:, 0, :], ACT.Tanh, bias=col("", c, 3 * KC, hb_in),
                                       scale=0.5).then_inc(A.sem, A.one("th"))
                        his(act, "glu", c, 1)
                        hold(act, used, c * 4 + (BASE["glu"] + 6))
                        act.activation(cab[:, :], psum[:, 1, :], ACT.Identity, bias=col("b_in", c, 2 * KC))\
                           .then_inc(A.sem, A.one("ca"))
                        if not first:
                            square(c - 1)

                    body(0, True)
                    with act.Fori(0, KC - 1) as c:
                        body(c + 1, False)
                    for b in range(2):
                        his(act, "glu", KC, b)
                    square(KC - 1)

                @block.vector
                def _(dve):
                    dve.sem_inc(V.sem, len(V.names))
                    dve.memset(xp[:, 0:PAD], 0.0).then_inc(padded, 1)
                    dve.wait_ge(padded, 1)
                    with dve.Fori(0, KC) as c:
                        even = chunk(res, c)
                        dve.wait_ge(V.sem, V.before(f"tap{CONF_K - 1}", c))
                        dve.wait_ge(A.sem, A.now("ca", c))
                        dve.scalar_tensor_tensor(xp[:, PAD:PAD + T], th, 1.0, cab[:, :], ALU.add, ALU.mult)\
                           .then_inc(V.sem, V.one("glu"))
                        dve.wait_ge(V.sem, V.now("glu", c))
                        for k in range(CONF_K):
                            acc = odd[:, :] if k % 2 else even
                            tap = col("", c, k * KC, hcw)
                            if k == 0:
                                ins = dve.tensor_scalar(acc, xp[:, 0:T], tap, col("conf_b", c), ALU.mult, ALU.add)
                            elif k == 1:
                                dve.wait_ge(G.sem, G.before("join", c))
                                ins = dve.tensor_scalar(acc, xp[:, 1:1 + T], tap, None, ALU.mult)
                            else:
                                dve.wait_ge(V.sem, V.now(f"tap{k - 2}", c))
                                ins = dve.scalar_tensor_tensor(acc, xp[:, k:k + T], tap, acc, ALU.mult, ALU.add)
                            ins.then_inc(V.sem, V.one(f"tap{k}"))
                    dve.wait_ge(V.sem, V.all(KC))


        class Stats:

            def __init__(self, name, ctx):
                self.mean = sb(f"{name}_mean", [P, T], ctx=ctx)
                self.means, self.rooted, self.st = (sem(f"{name}_{n}", ctx) for n in ("means", "sqrt", "stats"))

            def means_of(self, pe):
                for k, v in enumerate((total, total2)):
                    pe.matmul(psum[:, 6 + k, :], ones[:, :], v[:, :], start=True, stop=True).then_inc(self.means, 1)

            def sqrt(self, act):
                act.wait_ge(self.st, 4)
                act.activation(rstd, rstd, ACT.Sqrt).then_inc(self.rooted, 1)

            def rest(self, dve):
                self.variance(dve)
                self.inverse(dve)

            def variance(self, dve):
                mean, st = self.mean, self.st
                dve.wait_ge(self.means, 1)
                dve.tensor_copy(mean[:, :], psum[:, 6, :]).then_inc(st, 1)
                dve.wait_ge(st, 1)
                dve.tensor_tensor(rstd, mean[:, :], mean[:, :], ALU.mult).then_inc(st, 1)
                dve.wait_ge(self.means, 2)
                dve.wait_ge(st, 2)
                dve.tensor_tensor(rstd, psum[:, 7, :], rstd, ALU.subtract).then_inc(st, 1)
                dve.wait_ge(st, 3)
                dve.tensor_scalar(rstd, rstd, 0.0, EPS, ALU.max, ALU.add).then_inc(st, 1)

            def inverse(self, dve):
                dve.wait_ge(self.rooted, 1)
                dve.reciprocal(rstd, rstd).then_inc(self.st, 1)
                dve.wait_ge(self.st, 5)

        def layer_norm(name, g_name, b_name, turned_out=None):
            B = 4
            turn = turned_out is not None
            with ExitStack() as ctx:
                s = lambda n: sem(f"{name}_{n}", ctx)
                stats = Stats(name, ctx)
                outs = [sb(f"{name}_out{b}", [P, T], ctx=ctx)[:, :] for b in range(B if turn else 0)]
                each = lambda *names: " ".join(f"{n}{b}" for n in names for b in range(B))
                V = Steps(s("scaled"), each("scale"))
                L = Steps(s("lo_made"), each("lo"))
                G = Steps(s("pool"), each("shift"))
                A = Steps(s("act"), each("affine", "out" if turn else "hi"))
                E = Steps(s("turn"), each("turn"))
                sent = [s(f"sent{b}") for b in range(B)]
                at = lambda i, b: bass.ds(i * (B * T) + b * T, T)
                with nc.Block() as block:
                    @block.tensor
                    def _(pe):
                        stats.means_of(pe)
                        if turn:
                            pe.sem_inc(E.sem, B)
                            for i in range(KC // B):
                                for b in range(B):
                                    pe.wait_ge(A.sem, A.now(f"affine{b}", i))
                                    pe.wait_ge(A.sem, A.before(f"out{b}", i))
                                    for t in range(TT):
                                        start = (i * B + b) * T + t * P
                                        ins = pe.transpose(psum[:, b, t * P:(t + 1) * P], res[:, start:start + P],
                                                           ident[:, :])
                                    ins.then_inc(E.sem, E.one(f"turn{b}"))

                    @block.scalar
                    def _(act):
                        act.sem_inc(A.sem, len(A.names))
                        stats.sqrt(act)
                        if turn:
                            for b in range(B):
                                act.sem_inc(sent[b], 16)
                        with act.Fori(0, KC // B) as i:
                            for b in range(B):
                                hold(act, V.sem, V.now(f"scale{b}", i))
                                act.activation(res[:, at(i, b)], res[:, at(i, b)], ACT.Identity,
                                               scale=col(g_name, i * B, b), bias=col(b_name, i * B, b))\
                                   .then_inc(A.sem, A.one(f"affine{b}"))
                            for b in range(B):
                                if turn:
                                    hold(act, sent[b], i * 16 + 16)
                                    hold(act, E.sem, E.now(f"turn{b}", i))
                                    act.activation(outs[b], psum[:, b, :], ACT.Copy).then_inc(A.sem, A.one(f"out{b}"))
                                    hold(act, A.sem, A.now(f"out{b}", i))
                                    act.dma_start(turned_out[:, :, bass.ds(i * (B * P) + b * P, P)]
                                                  .rearrange("t p n -> p t n"),
                                                  outs[b].rearrange("p (t n) -> p t n", t=TT)).then_inc(sent[b], 16)
                                else:
                                    hold(act, A.sem, A.now(f"affine{b}", i))
                                    act.activation(a_hi[:, at(i, b)], res[:, at(i, b)], ACT.Copy)\
                                       .then_inc(A.sem, A.one(f"hi{b}"))
                        if turn:
                            for b in range(B):
                                act.wait_ge(sent[b], (KC // B + 1) * 16)

                    @block.gpsimd
                    def _(pool):
                        pool.sem_inc(G.sem, B)
                        pool.wait_ge(stats.st, 1)
                        with pool.Fori(0, KC // B) as i:
                            for b in range(B):
                                pool.tensor_tensor(res[:, at(i, b)], res[:, at(i, b)], stats.mean[:, :], ALU.subtract)\
                                    .then_inc(G.sem, G.one(f"shift{b}"))

                    @block.vector
                    def _(dve):
                        dve.sem_inc(V.sem, B)
                        dve.sem_inc(L.sem, B)
                        stats.rest(dve)

                        def scale(i):
                            for b in range(B):
                                dve.wait_ge(G.sem, G.now(f"shift{b}", i))
                                dve.tensor_tensor(res[:, at(i, b)], res[:, at(i, b)], rstd, ALU.mult)\
                                   .then_inc(V.sem, V.one(f"scale{b}"))

                        def lo(i):
                            for b in range(B):
                                dve.wait_ge(A.sem, A.now(f"hi{b}", i))
                                dve.tensor_tensor(a_lo[:, at(i, b)], res[:, at(i, b)], a_hi[:, at(i, b)].bitcast(F32),
                                                  ALU.subtract).then_inc(L.sem, L.one(f"lo{b}"))

                        scale(0)
                        with dve.Fori(0, KC // B - 1) as i:
                            scale(i + 1)
                            if not turn:
                                lo(i)
                        if not turn:
                            lo(KC // B - 1)
                            dve.wait_ge(L.sem, L.all(KC // B))
                        dve.wait_ge(V.sem, V.all(KC // B))

        with ExitStack() as ctx:
            stats = Stats("conf_ln", ctx)
            th = [sb(f"gconf_th{b}", [P, T], ctx=ctx) for b in range(2)]
            y = [tile_in, total]
            TH = Steps(sem("gconf_tanh", ctx), "th0 th1")
            A = Steps(sem("conf_ln_act", ctx), "affine0 tanh0 hi0 affine1 tanh1 hi1")
            V = Steps(sem("conf_ln_dve", ctx), "shift0 scale0 gate0 lo0 shift1 scale1 gate1 lo1")
            sent = [sem(f"gconf_sent{b}", ctx) for b in range(2)]
            NP = KC // 2
            at = lambda j, b: bass.ds(j * (2 * T) + b * T, T)
            with nc.Block() as block:
                @block.sync
                def _(sp):
                    loads(sp, "gconf", KC, skip=2)

                @block.gpsimd
                def _(pool):
                    splits(pool, "gconf", KC, skip=2, hi_by_act=True)

                @block.tensor
                def _(pe):
                    stats.means_of(pe)
                    with pe.Fori(0, NP - 1) as j:
                        for b in range(2):
                            pe.wait_ge(TH.sem, TH.now(f"th{b}", j))
                            gemm(pe, b, x_hi, x_lo, j * 4 + (BASE["gconf"] + 4 + 2 * b))

                @block.scalar
                def _(act):
                    act.sem_inc(TH.sem, 2)
                    act.sem_inc(A.sem, len(A.names))
                    for b in range(2):
                        act.sem_inc(sent[b], 16)

                    def gate(j, b):
                        hold(act, sent[b], j * 16 + 16)
                        hold(act, used, j * 4 + (BASE["gconf"] + 2 * b + 4))
                        act.activation(th[b][:, :], psum[:, b, :], ACT.Tanh, bias=col("", j * 2, 5 * KC + b, hb_in),
                                       scale=0.5).then_inc(TH.sem, TH.one(f"th{b}"))
                        hold(act, TH.sem, TH.now(f"th{b}", j))
                        act.dma_start(th_d[bass.ds(j * 2 + b, 1)].rearrange("a p n -> (a p) n"), th[b][:, :])\
                           .then_inc(sent[b], 16)

                    def norm(j, b):
                        hold(act, V.sem, V.now(f"scale{b}", j))
                        hold(act, V.sem, V.before(f"lo{b}", j))
                        act.activation(y[b][:, :], res[:, at(j, b)], ACT.Identity, scale=col("conf_g", j * 2, b),
                                       bias=col("conf_be", j * 2, b)).then_inc(A.sem, A.one(f"affine{b}"))
                        hold(act, A.sem, A.now(f"affine{b}", j))
                        act.activation(res[:, at(j, b)], y[b][:, :], ACT.Tanh, scale=0.5)\
                           .then_inc(A.sem, A.one(f"tanh{b}"))
                        hold(act, V.sem, V.now(f"gate{b}", j))
                        act.activation(a_hi[:, at(j, b)], y[b][:, :], ACT.Copy, scale=0.5)\
                           .then_inc(A.sem, A.one(f"hi{b}"))

                    for b in range(2):
                        gate(0, b)
                    stats.sqrt(act)
                    with act.Fori(0, NP - 1) as j:
                        for b in range(2):
                            his(act, "gconf", j + 1, b)
                            gate(j + 1, b)
                            norm(j, b)
                    for b in range(2):
                        norm(NP - 1, b)
                    for b in range(2):
                        act.wait_ge(sent[b], (NP + 1) * 16)

                @block.vector
                def _(dve):
                    dve.sem_inc(V.sem, len(V.names))
                    stats.rest(dve)
                    with dve.Fori(0, NP) as j:
                        for b in range(2):
                            r = res[:, at(j, b)]
                            dve.tensor_tensor(r, r, stats.mean[:, :], ALU.subtract).then_inc(V.sem, V.one(f"shift{b}"))
                            dve.wait_ge(V.sem, V.now(f"shift{b}", j))
                            dve.tensor_tensor(r, r, rstd, ALU.mult).then_inc(V.sem, V.one(f"scale{b}"))
                            dve.wait_ge(A.sem, A.now(f"tanh{b}", j))
                            dve.scalar_tensor_tensor(y[b][:, :], r, 1.0, y[b][:, :], ALU.add, ALU.mult)\
                               .then_inc(V.sem, V.one(f"gate{b}"))
                            dve.wait_ge(V.sem, V.now(f"gate{b}", j))
                            dve.wait_ge(A.sem, A.now(f"hi{b}", j))
                            dve.scalar_tensor_tensor(a_lo[:, at(j, b)], y[b][:, :], 0.5, a_hi[:, at(j, b)].bitcast(F32),
                                                     ALU.mult, ALU.subtract).then_inc(V.sem, V.one(f"lo{b}"))
                    dve.wait_ge(V.sem, V.all(NP))

        with ExitStack() as ctx:
            th = [tile_in, total]
            y = [sb(f"conf_y{b}", [P, T], ctx=ctx) for b in range(2)]
            A = Steps(sem("conf_act", ctx), "y0 y1")
            V = Steps(sem("conf_dve", ctx), "gate0 gate1")
            th_in = [sem(f"conf_th_in{b}", ctx) for b in range(2)]
            sent = [sem(f"conf_sent{b}", ctx) for b in range(2)]
            NP = KC // 2
            with nc.Block() as block:
                @block.sync
                def _(sp):
                    loads(sp, "conf", KC)

                @block.gpsimd
                def _(pool):
                    splits(pool, "conf", KC, hi_by_act=True)

                @block.tensor
                def _(pe):
                    with pe.Fori(0, NP) as i:
                        for b in range(2):
                            pe.wait_ge(A.sem, A.before(f"y{b}", i))
                            gemm(pe, b, a_hi, a_lo, i * 4 + (BASE["conf"] + 2 * b))

                @block.scalar
                def _(act):
                    act.sem_inc(A.sem, 2)
                    for b in range(2):
                        act.sem_inc(sent[b], 16)
                    with act.Fori(0, NP) as i:
                        for b in range(2):
                            hold(act, V.sem, V.before(f"gate{b}", i))
                            act.dma_start(th[b][:, :], th_d[bass.ds(i * 2 + b, 1)].rearrange("a p n -> (a p) n"))\
                               .then_inc(th_in[b], 16)
                        for b in range(2):
                            his(act, "conf", i, b)
                            hold(act, sent[b], i * 16 + 16)
                            hold(act, used, i * 4 + (BASE["conf"] + 2 * b + 4))
                            act.activation(y[b][:, :], psum[:, b, :], ACT.Identity, bias=col("b_out", i * 2, b))\
                               .then_inc(A.sem, A.one(f"y{b}"))
                            hold(act, V.sem, V.now(f"gate{b}", i))
                            act.dma_start(conf_d[bass.ds(i * 2 + b, 1)].rearrange("a p n -> (a p) n"), y[b][:, :])\
                               .then_inc(sent[b], 16)
                    for b in range(2):
                        act.wait_ge(sent[b], (NP + 1) * 16)

                @block.vector
                def _(dve):
                    dve.sem_inc(V.sem, 2)
                    with dve.Fori(0, NP) as i:
                        for b in range(2):
                            dve.wait_ge(A.sem, A.now(f"y{b}", i))
                            dve.wait_ge(th_in[b], i * 16 + 16)
                            dve.scalar_tensor_tensor(y[b][:, :], th[b][:, :], 1.0, y[b][:, :], ALU.add, ALU.mult)\
                               .then_inc(V.sem, V.one(f"gate{b}"))
                    dve.wait_ge(V.sem, V.all(NP))

        with ExitStack() as ctx:
            (g, q, xc, tr, ti, la, av, tv, den, rden, m2, u, h, gt, r, sqv) = tile
            xp = sb("lru_padded", [P, RNN_K - 1 + T], ctx=ctx)
            gw = sb("lru_gates", [P, 2 * P], ctx=ctx)
            A = Steps(sem("lru_act", ctx), "xr gr thr thi exp tanh gelu sqrt hi")
            V = Steps(sem("lru_dve", ctx), "c0 c1 c2 c3 g2 g3 g4 la ix den rden m2 gate u h r lo")
            E = Steps(sem("lru_pe", ctx), "gates")
            gates_in = sem("lru_gates_in", ctx)
            padded = sem("lru_pad_zeroed", ctx)
            with nc.Block() as block:
                @block.sync
                def _(sp):
                    first = BASE["lru"] + AHEAD_LOAD
                    with sp.Fori(0, KC) as c:
                        hold(sp, E.sem, c + 1)
                        sp.dma_start(gw[:, :], gates_w[bass.ds(c, 1)].rearrange("a p n -> (a p) n"))\
                          .then_inc(gates_in, 16)
                        for s in range(4):
                            load_half(sp, c * 4 + (first + s), s)
                    for g in range(first + 4 * KC, first + 4 * KC + 2):
                        load_half(sp, g, g % 4)

                @block.gpsimd
                def _(pool):
                    splits(pool, "lru", 2 * KC + 1)

                @block.tensor
                def _(pe):
                    pe.sem_inc(E.sem, 1)
                    with pe.Fori(0, KC) as c:
                        pe.wait_ge(A.sem, A.before("xr", c))
                        gemm(pe, 0, x_hi, x_lo, c * 4 + BASE["lru"])
                        pe.wait_ge(A.sem, A.before("gr", c))
                        gemm(pe, 1, x_hi, x_lo, c * 4 + (BASE["lru"] + 2))
                        pe.wait_ge(gates_in, c * 16 + 16)
                        pe.wait_ge(V.sem, V.now("c3", c))
                        pe.wait_ge(A.sem, A.before("thi", c))
                        for j in range(2):
                            ins = pe.matmul(psum[:, 2 + j, :], gw[:, j * P:(j + 1) * P], xc, start=True, stop=True)
                        ins.then_inc(E.sem, E.one("gates"))
                    pe.wait_ge(A.sem, A.before("xr", KC))
                    gemm(pe, 0, x_hi, x_lo, BASE["rnn"])

                @block.scalar
                def _(act):
                    act.sem_inc(A.sem, len(A.names))
                    with act.Fori(0, KC) as c:
                        hold(act, used, c * 4 + (BASE["lru"] + 4))
                        hold(act, V.sem, V.before("c3", c))
                        act.activation(xp[:, 3:3 + T], psum[:, 0, :], ACT.Identity, bias=col("b_in", c))\
                           .then_inc(A.sem, A.one("xr"))
                        hold(act, used, c * 4 + (BASE["lru"] + 6))
                        hold(act, V.sem, V.before("gate", c))
                        act.activation(g, psum[:, 1, :], ACT.Identity, bias=col("b_in", c, KC))\
                           .then_inc(A.sem, A.one("gr"))
                        hold(act, E.sem, c + 2)
                        hold(act, V.sem, V.before("lo", c))
                        act.activation(tr, psum[:, 2, :], ACT.Tanh, bias=col("", c, 0, hb_ax), scale=0.5)\
                           .then_inc(A.sem, A.one("thr"))
                        act.activation(ti, psum[:, 3, :], ACT.Tanh, bias=col("", c, KC, hb_ax), scale=0.5)\
                           .then_inc(A.sem, A.one("thi"))
                        act.wait_ge(V.sem, V.now("la", c))
                        act.activation(av, la, ACT.Exp).then_inc(A.sem, A.one("exp"))
                        act.activation(tv, la, ACT.Tanh).then_inc(A.sem, A.one("tanh"))
                        act.activation(gt, q, ACT.Tanh, scale=GELU_C).then_inc(A.sem, A.one("gelu"))
                        act.wait_ge(V.sem, V.now("m2", c))
                        act.activation(sqv, m2, ACT.Sqrt).then_inc(A.sem, A.one("sqrt"))
                        hold(act, V.sem, V.now("r", c))
                        act.activation(chunk(a_hi, c), r, ACT.Copy).then_inc(A.sem, A.one("hi"))

                @block.vector
                def _(dve):
                    dve.sem_inc(V.sem, len(V.names))
                    dve.memset(xp[:, 0:3], 0.0).then_inc(padded, 1)
                    dve.wait_ge(padded, 1)
                    with dve.Fori(0, KC) as c:
                        def after(name):
                            dve.wait_ge(V.sem, V.now(name, c))

                        def step(name, ins):
                            ins.then_inc(V.sem, V.one(name))

                        dve.wait_ge(A.sem, A.now("xr", c))
                        dve.wait_ge(V.sem, V.before("lo", c))
                        step("c0", dve.tensor_scalar(xc, xp[:, 0:T], col("rnn_w", c), col("rnn_b", c), ALU.mult, ALU.add))
                        for k in range(1, RNN_K):
                            after(f"c{k - 1}")
                            step(f"c{k}", dve.scalar_tensor_tensor(xc, xp[:, k:k + T], col("rnn_w", c, k * KC), xc,
                                                                   ALU.mult, ALU.add))
                        dve.wait_ge(A.sem, A.now("gr", c))
                        step("g2", dve.tensor_tensor(q, g, g, ALU.mult))
                        after("g2")
                        step("g3", dve.tensor_scalar(q, q, 0.044715, 1.0, ALU.mult, ALU.add))
                        after("g3")
                        step("g4", dve.tensor_tensor(q, q, g, ALU.mult))
                        dve.wait_ge(A.sem, A.now("thi", c))
                        step("la", dve.tensor_scalar(la, tr, 1.0, col("", c, 0, nsp), ALU.add, ALU.mult))
                        after("la")
                        step("ix", dve.scalar_tensor_tensor(tr, ti, 1.0, xc, ALU.add, ALU.mult))
                        dve.wait_ge(A.sem, A.now("tanh", c))
                        step("den", dve.tensor_scalar(den, tv, -1.0, 1.0, ALU.mult, ALU.add))
                        after("den")
                        step("rden", dve.reciprocal(rden, den))
                        after("rden")
                        step("m2", dve.scalar_tensor_tensor(m2, tv, -2.0, rden, ALU.mult, ALU.mult))
                        dve.wait_ge(A.sem, A.now("gelu", c))
                        step("gate", dve.scalar_tensor_tensor(gt, gt, 1.0, g, ALU.add, ALU.mult))
                        dve.wait_ge(A.sem, A.now("sqrt", c))
                        after("ix")
                        step("u", dve.scalar_tensor_tensor(u, tr, 0.5, sqv, ALU.mult, ALU.mult))
                        after("u")
                        step("h", dve.tensor_tensor_scan(h, av, u, 0.0, ALU.mult, ALU.add))
                        after("h")
                        after("gate")
                        step("r", dve.scalar_tensor_tensor(r, gt, 0.5, h, ALU.mult, ALU.mult))
                        dve.wait_ge(A.sem, A.now("hi", c))
                        after("r")
                        step("lo", dve.tensor_tensor(chunk(a_lo, c), r, chunk(a_hi, c).bitcast(F32), ALU.subtract))
                    dve.wait_ge(V.sem, V.all(KC))

        with ExitStack() as ctx:
            th = sb("rnn_th", [P, T], ctx=ctx)
            y = sb("rnn_y", [P, T], ctx=ctx)
            TH = Steps(sem("rnn_tanh", ctx), "th")
            Y = Steps(sem("rnn_copied", ctx), "y")
            V = Steps(sem("rnn_dve", ctx), "gate join")
            conf_in, hi_done, lo_done = (sem(n, ctx) for n in ("rnn_conf_in", "merged_hi", "merged_lo"))
            pieces = quarter[:3] + [slice(3 * Q, KC * T - T), slice(KC * T - T, KC * T)]
            with nc.Block() as block:
                @block.sync
                def _(sp):
                    loads(sp, "rnn", 2 * KC, skip=1)

                @block.gpsimd
                def _(pool):
                    splits(pool, "rnn", 2 * KC, skip=1, hi_by_act=True)

                @block.tensor
                def _(pe):
                    def outputs(c):
                        pe.wait_ge(Y.sem, Y.before("y", c))
                        gemm(pe, 1, a_hi, a_lo, c * 4 + (BASE["rnn"] + 2))

                    with pe.Fori(0, KC - 1) as c:
                        outputs(c)
                        pe.wait_ge(TH.sem, TH.now("th", c))
                        gemm(pe, 0, x_hi, x_lo, c * 4 + (BASE["rnn"] + 4))
                    outputs(KC - 1)

                @block.scalar
                def _(act):
                    act.sem_inc(TH.sem, 1)
                    act.sem_inc(Y.sem, 1)

                    def fetch(c):
                        hold(act, V.sem, V.before("join", c))
                        act.dma_start(tile_in, conf_d[bass.ds(c, 1)].rearrange("a p n -> (a p) n"))\
                           .then_inc(conf_in, 16)

                    def tanh(c):
                        hold(act, used, c * 4 + (BASE["rnn"] + 4))
                        act.activation(th[:, :], psum[:, 0, :], ACT.Tanh, bias=col("", c, 4 * KC, hb_in),
                                       scale=0.5).then_inc(TH.sem, TH.one("th"))

                    def copy(c):
                        his(act, "rnn", c, 1)
                        hold(act, V.sem, V.before("join", c))
                        hold(act, used, c * 4 + (BASE["rnn"] + 6))
                        act.activation(y[:, :], psum[:, 1, :], ACT.Copy).then_inc(Y.sem, Y.one("y"))

                    def hi(q):
                        act.activation(x_hi[:, q], res[:, q], ACT.Copy, scale=0.5).then_inc(hi_done, 1)

                    tanh(0)
                    with act.Fori(0, KC - 1) as c:
                        fetch(c)
                        copy(c)
                        his(act, "rnn", c + 1, 0)
                        hold(act, V.sem, V.now("gate", c))
                        tanh(c + 1)
                    fetch(KC - 1)
                    for q in pieces[:-1]:
                        hi(q)
                    copy(KC - 1)
                    hold(act, V.sem, V.now("join", KC - 1))
                    hi(pieces[-1])

                @block.vector
                def _(dve):
                    dve.sem_inc(V.sem, 2)

                    def join(c):
                        dve.wait_ge(Y.sem, Y.now("y", c))
                        dve.scalar_tensor_tensor(y[:, :], th[:, :], 1.0, y[:, :], ALU.add, ALU.mult)\
                           .then_inc(V.sem, V.one("gate"))
                        dve.wait_ge(conf_in, c * 16 + 16)
                        dve.wait_ge(V.sem, V.now("gate", c))
                        dve.tensor_tensor(chunk(res, c), y[:, :], tile_in, ALU.add).then_inc(V.sem, V.one("join"))

                    def lo(n):
                        q = pieces[n]
                        dve.wait_ge(hi_done, n + 1)
                        dve.scalar_tensor_tensor(x_lo[:, q], res[:, q], 0.5, x_hi[:, q].bitcast(F32), ALU.mult,
                                                 ALU.subtract).then_inc(lo_done, 1)

                    with dve.Fori(0, KC - 1) as c:
                        join(c)
                    for n in range(len(pieces) - 1):
                        lo(n)
                    join(KC - 1)
                    lo(len(pieces) - 1)
                    dve.wait_ge(V.sem, V.all(KC))
                    dve.wait_ge(lo_done, len(pieces))

        def project(name, act_hi, act_lo, src_hi=None, src_lo=None):
            from_x = src_hi is None
            with ExitStack() as ctx:
                xr = [sb(f"{name}_x{b}", [P, T], ctx=ctx) for b in range(2)]
                V = Steps(sem(f"{name}_dve", ctx), "res0 lo0 total0 square0 res1 lo1 total1 square1")
                A = Steps(sem(f"{name}_act", ctx), "sq0 sq1")
                sq = tile_in
                x_in = [sem(f"{name}_in{b}", ctx) for b in range(2)]
                if from_x:
                    piece = sb("mem_piece", [P, T], ctx=ctx)
                    mem_in, mem_hi, mem_lo = (sem(f"mem_{n}", ctx) for n in ("in", "hi_made", "lo_made"))
                setup = sem(f"{name}_setup", ctx)
                with nc.Block() as block:
                    @block.sync
                    def _(sp):
                        loads(sp, name, KC)

                    @block.gpsimd
                    def _(pool):
                        splits(pool, name, KC, hi_by_act=True)

                    @block.tensor
                    def _(pe):
                        with pe.Fori(0, KC // 2) as i:
                            for b in range(2):
                                pe.wait_ge(V.sem, V.before(f"res{b}", i))
                                gemm(pe, b, act_hi, act_lo, i * 4 + (BASE[name] + 2 * b))

                    @block.scalar
                    def _(act):
                        act.sem_inc(A.sem, 2)
                        with act.Fori(0, KC // 2) as i:
                            if from_x:
                                hold(act, mem_lo, i + 1)
                                act.dma_start(piece[:, :], mem_t[:, bass.ts(i, T)]).then_inc(mem_in, 16)
                            for b in range(2):
                                if from_x:
                                    hold(act, V.sem, V.before(f"res{b}", i))
                                    act.dma_start(xr[b][:, :], x_t[:, bass.ds(i * (2 * T) + b * T, T)])\
                                       .then_inc(x_in[b], 16)
                            for b in range(2):
                                his(act, name, i, b)
                                hold(act, V.sem, V.now(f"lo{b}", i))
                                hold(act, V.sem, V.now("square0", i) if b else V.before("square1", i))
                                act.activation(sq[:, :], res[:, bass.ds(i * (2 * T) + b * T, T)], ACT.Square)\
                                   .then_inc(A.sem, A.one(f"sq{b}"))
                            if from_x:
                                hold(act, mem_in, i * 16 + 16)
                                act.activation(a_hi[:, bass.ts(i, T)], piece[:, :], ACT.Copy).then_inc(mem_hi, 1)

                    @block.vector
                    def _(dve):
                        dve.sem_inc(V.sem, len(V.names))
                        if from_x:
                            dve.sem_inc(mem_lo, 1)
                        dve.memset(total[:, :], 0.0).then_inc(setup, 1)
                        dve.memset(total2[:, :], 0.0).then_inc(setup, 1)
                        dve.wait_ge(setup, 2)
                        with dve.Fori(0, KC // 2) as i:
                            for b in range(2):
                                at = bass.ds(i * (2 * T) + b * T, T)
                                dve.wait_ge(used, i * 4 + (BASE[name] + 2 * b + 4))
                                if from_x:
                                    dve.wait_ge(x_in[b], i * 16 + 16)
                                    src = xr[b][:, :]
                                else:
                                    src = src_hi[:, at].bitcast(F32)
                                dve.scalar_tensor_tensor(res[:, at], src, ALPHA, psum[:, b, :], ALU.mult, ALU.add)\
                                   .then_inc(V.sem, V.one(f"res{b}"))
                                dve.wait_ge(V.sem, V.now(f"res{b}", i))
                                if from_x:
                                    dve.sem_inc(V.sem, V.one(f"lo{b}"))
                                else:
                                    dve.scalar_tensor_tensor(res[:, at], src_lo[:, at].bitcast(F32), ALPHA, res[:, at],
                                                             ALU.mult, ALU.add).then_inc(V.sem, V.one(f"lo{b}"))
                                    dve.wait_ge(V.sem, V.now(f"lo{b}", i))
                                dve.tensor_tensor(total[:, :], total[:, :], res[:, at], ALU.add)\
                                   .then_inc(V.sem, V.one(f"total{b}"))
                                dve.wait_ge(A.sem, A.now(f"sq{b}", i))
                                dve.tensor_tensor(total2[:, :], total2[:, :], sq[:, :], ALU.add)\
                                   .then_inc(V.sem, V.one(f"square{b}"))
                                dve.wait_ge(V.sem, V.now(f"square{b}", i))
                            if from_x:
                                dve.wait_ge(mem_hi, i + 1)
                                dve.tensor_tensor(a_lo[:, bass.ts(i, T)], piece[:, :], a_hi[:, bass.ts(i, T)].bitcast(F32),
                                                  ALU.subtract).then_inc(mem_lo, 1)
                        if from_x:
                            dve.wait_ge(mem_lo, KC // 2 + 1)

        project("mix", x_hi, x_lo)

        with ExitStack() as ctx:
            stats = Stats("ln1", ctx)
            kv = [sb(f"kv_tile{b}", [P, M], ctx=ctx) for b in range(2)]
            sent = [sem(f"kv_sent{b}", ctx) for b in range(2)]
            KV = Steps(sem("kv_copied", ctx), "copy0 copy1")
            A = Steps(sem("ln1_act", ctx), "affine hi")
            V = Steps(sem("ln1_scaled", ctx), "scale")
            L = Steps(sem("ln1_lo_made", ctx), "lo")
            G = Steps(sem("ln1_pool", ctx), "shift")
            with nc.Block() as block:
                @block.sync
                def _(sp):
                    loads(sp, "kv", 2 * KC)

                @block.gpsimd
                def _(pool):
                    pool.sem_inc(G.sem, 1)
                    pool.wait_ge(stats.st, 1)
                    with pool.Fori(0, KC) as c:
                        pool.tensor_tensor(chunk(res, c), chunk(res, c), stats.mean[:, :], ALU.subtract)\
                            .then_inc(G.sem, G.one("shift"))

                @block.tensor
                def _(pe):
                    stats.means_of(pe)
                    with pe.Fori(0, KC) as i:
                        for b in range(2):
                            pe.wait_ge(KV.sem, KV.before(f"copy{b}", i))
                            gemm(pe, b, a_hi, a_lo, i * 4 + (BASE["kv"] + 2 * b), M)

                @block.scalar
                def _(act):
                    act.sem_inc(KV.sem, 2)
                    act.sem_inc(A.sem, 2)
                    for b in range(2):
                        act.sem_inc(sent[b], 16)

                    def copies(i):
                        for b in range(2):
                            his(act, "kv", i, b)
                            hold(act, sent[b], i * 16 + 16)
                            act.wait_ge(used, i * 4 + (BASE["kv"] + 2 * b + 4))
                            act.activation(kv[b][:, :], psum[:, b, 0:M], ACT.Copy).then_inc(KV.sem, KV.one(f"copy{b}"))
                            hold(act, KV.sem, KV.now(f"copy{b}", i))
                            act.dma_start(kv_d[bass.ds(i * 2 + b, 1)].rearrange("a p n -> (a p) n"), kv[b][:, :])\
                               .then_inc(sent[b], 16)

                    def norm(c):
                        hold(act, V.sem, V.now("scale", c))
                        act.activation(chunk(res, c), chunk(res, c), ACT.Identity, scale=col("g1", c), bias=col("be1", c))\
                           .then_inc(A.sem, A.one("affine"))
                        hold(act, A.sem, A.now("affine", c))
                        act.activation(chunk(x_hi, c), chunk(res, c), ACT.Copy).then_inc(A.sem, A.one("hi"))

                    copies(0)
                    stats.sqrt(act)
                    with act.Fori(0, KC - 1) as c:
                        copies(c + 1)
                        norm(c)
                    norm(KC - 1)
                    for b in range(2):
                        act.wait_ge(sent[b], (KC + 1) * 16)

                @block.vector
                def _(dve):
                    dve.sem_inc(V.sem, 1)
                    dve.sem_inc(L.sem, 1)

                    def split_pass(i):
                        for s in range(4):
                            first = BASE["kv"] + AHEAD_SPLIT + s
                            split_half(dve, i * 4 + first, 0, first % 4, hi_by_act=True)

                    def scale(c):
                        dve.wait_ge(G.sem, G.now("shift", c))
                        dve.tensor_tensor(chunk(res, c), chunk(res, c), rstd, ALU.mult).then_inc(V.sem, V.one("scale"))

                    def lo(c):
                        dve.wait_ge(A.sem, A.now("hi", c))
                        dve.tensor_tensor(chunk(x_lo, c), chunk(res, c), chunk(x_hi, c).bitcast(F32), ALU.subtract)\
                           .then_inc(L.sem, L.one("lo"))

                    stats.variance(dve)
                    split_pass(0)
                    stats.inverse(dve)
                    scale(0)
                    with dve.Fori(0, KC - 1) as c:
                        split_pass(c + 1)
                        lo(c)
                        scale(c + 1)
                    lo(KC - 1)
                    dve.wait_ge(L.sem, L.all(KC))

        with ExitStack() as ctx:
            def part(at, n):
                return res[:, at:at + n]

            qh, kh, vt, pr, pt, vtok = (part(0, 2048), part(2048, 1024), part(3072, 1024), part(4096, 1024),
                                        part(5120, 1024), part(6144, 1024))
            stat = sb("att_stat", [P, 4 * TT], ctx=ctx)
            Q = Steps(sem("att_q", ctx), "q0 q1 q2 q3")
            A = Steps(sem("att_act", ctx), "v0 v1 e0 e1 e2 e3 p0 p1 o0 o1 o2 o3")
            V = Steps(sem("att_dve", ctx), "m0 n0 m1 n1 m2 n2 m3 n3 r0 s0 r1 s1 r2 s2 r3 s3 lo0 lo1 lo2 lo3")
            E = Steps(sem("att_pe", ctx), "v s01 s23 p o0 o1 o2 o3")
            kv_in = sem("att_kv_in", ctx)
            with nc.Block() as block:
                @block.sync
                def _(sp):
                    first = BASE["att"] + AHEAD_LOAD
                    with sp.Fori(0, HEADS) as h:
                        hold(sp, E.sem, E.before("s23", h))
                        sp.dma_start(kh.rearrange("p (c n) -> p c n", c=HC),
                                     kv_d[bass.ds(h * HC, HC)].rearrange("c p n -> p c n")).then_inc(kv_in, 16)
                        sp.dma_start(vt.rearrange("p (c n) -> p c n", c=HC),
                                     kv_d[bass.ds(h * HC + KC, HC)].rearrange("c p n -> p c n")).then_inc(kv_in, 16)
                        for s in range(2 * HC):
                            load_half(sp, h * (2 * HC) + (first + s), s % 4)

                @block.gpsimd
                def _(pool):
                    splits(pool, "att", KC)

                @block.tensor
                def _(pe):
                    pe.sem_inc(E.sem, len(E.names))

                    def queries(h, first=False):
                        for c in range(HC):
                            if c >= 2:
                                pe.wait_ge(Q.sem, Q.now(f"q{c - 2}", h))
                            elif not first:
                                pe.wait_ge(V.sem, V.before(f"lo{c + 2}", h - 1))
                            gemm(pe, c % 2, x_hi, x_lo, h * (2 * HC) + (BASE["att"] + 2 * c))

                    def scores(h):
                        pe.wait_ge(kv_in, h * 32 + 32)
                        pe.wait_ge(A.sem, A.before("v1", h))
                        for m in range(2):
                            for c in range(HC):
                                ins = pe.transpose(psum[:, 2 + m, c * P:(c + 1) * P],
                                                   vt[:, c * M + m * P:c * M + (m + 1) * P], ident[:, :])
                        ins.then_inc(E.sem, E.one("v"))
                        pe.wait_ge(Q.sem, Q.now("q3", h))
                        for t in range(TT):
                            if t % 2 == 0:
                                pe.wait_ge(A.sem, A.before(f"e{t + 1}", h))
                            for c in range(HC):
                                ins = pe.matmul(psum[:, 4 + t // 2, (t % 2) * M:(t % 2 + 1) * M],
                                                qh[:, c * T + t * P:c * T + (t + 1) * P], kh[:, c * M:(c + 1) * M],
                                                start=(c == 0), stop=(c == HC - 1))
                            if t % 2:
                                ins.then_inc(E.sem, E.one("s01" if t == 1 else "s23"))

                    def outputs(h, next_q):
                        pe.wait_ge(A.sem, A.before("p1", h))
                        for t in range(TT):
                            pe.wait_ge(V.sem, V.now(f"s{t}", h))
                            for m in range(2):
                                ins = pe.transpose(psum[:, 6 + m, t * P:(t + 1) * P],
                                                   pr[:, t * M + m * P:t * M + (m + 1) * P], ident[:, :])
                        ins.then_inc(E.sem, E.one("p"))
                        pe.wait_ge(A.sem, A.now("p1", h))
                        if next_q:
                            pe.wait_ge(Q.sem, Q.now("q3", h + 1))
                        for c in range(HC):
                            if c >= 2:
                                pe.wait_ge(V.sem, V.now(f"lo{c - 2}", h))
                            for m in range(2):
                                ins = pe.matmul(psum[:, c % 2, :], vtok[:, m * HD + c * P:m * HD + (c + 1) * P],
                                                pt[:, m * T:(m + 1) * T], start=(m == 0), stop=(m == 1))
                            ins.then_inc(E.sem, E.one(f"o{c}"))

                    queries(0, first=True)
                    with pe.Fori(0, HEADS - 1) as h:
                        scores(h)
                        queries(h + 1)
                        outputs(h, True)
                    scores(HEADS - 1)
                    outputs(HEADS - 1, False)

                @block.scalar
                def _(act):
                    act.sem_inc(A.sem, len(A.names))
                    act.sem_inc(Q.sem, len(Q.names))

                    def queries(h):
                        for c in range(HC):
                            hold(act, used, h * (2 * HC) + (BASE["att"] + 2 * c + 4))
                            act.activation(qh[:, c * T:(c + 1) * T], psum[:, c % 2, :], ACT.Copy)\
                               .then_inc(Q.sem, Q.one(f"q{c}"))

                    def head(h, last):
                        act.wait_ge(E.sem, E.now("v", h))
                        hold(act, E.sem, E.before("o3", h))
                        for m in range(2):
                            act.activation(vtok[:, m * HD:(m + 1) * HD], psum[:, 2 + m, :], ACT.Copy)\
                               .then_inc(A.sem, A.one(f"v{m}"))
                        for t in range(TT):
                            act.wait_ge(V.sem, V.now(f"n{t | 1}", h))
                            act.activation(pr[:, t * M:(t + 1) * M], psum[:, 4 + t // 2, (t % 2) * M:(t % 2 + 1) * M],
                                           ACT.Exp, bias=stat[:, TT + t:TT + t + 1], scale=HD ** -0.5,
                                           accum_out=stat[:, 2 * TT + t:2 * TT + t + 1])\
                               .then_inc(A.sem, A.one(f"e{t}"))
                        if not last:
                            hold(act, E.sem, E.now("s23", h))
                            queries(h + 1)
                        act.wait_ge(E.sem, E.now("p", h))
                        for m in range(2):
                            act.activation(pt[:, m * T:(m + 1) * T], psum[:, 6 + m, :], ACT.Copy)\
                               .then_inc(A.sem, A.one(f"p{m}"))
                        for c in range(HC):
                            hold(act, E.sem, E.now(f"o{c}", h))
                            act.activation(a_hi[:, bass.ds(h * (HC * T) + c * T, T)], psum[:, c % 2, :], ACT.Copy)\
                               .then_inc(A.sem, A.one(f"o{c}"))

                    queries(0)
                    with act.Fori(0, HEADS - 1) as h:
                        head(h, False)
                    head(HEADS - 1, True)

                @block.vector
                def _(dve):
                    dve.sem_inc(V.sem, len(V.names))
                    with dve.Fori(0, HEADS) as h:
                        for t in range(TT):
                            dve.wait_ge(E.sem, E.now("s01" if t < 2 else "s23", h))
                            dve.tensor_reduce(stat[:, t:t + 1], psum[:, 4 + t // 2, (t % 2) * M:(t % 2 + 1) * M],
                                              AX_X, ALU.max).then_inc(V.sem, V.one(f"m{t}"))
                            dve.wait_ge(V.sem, V.now(f"m{t}", h))
                            dve.tensor_scalar(stat[:, TT + t:TT + t + 1], stat[:, t:t + 1], -HD ** -0.5, None,
                                              ALU.mult).then_inc(V.sem, V.one(f"n{t}"))
                        for t in range(TT):
                            dve.wait_ge(A.sem, A.now(f"e{t}", h))
                            dve.reciprocal(stat[:, 3 * TT + t:3 * TT + t + 1], stat[:, 2 * TT + t:2 * TT + t + 1])\
                               .then_inc(V.sem, V.one(f"r{t}"))
                            dve.wait_ge(V.sem, V.now(f"r{t}", h))
                            dve.tensor_scalar(pr[:, t * M:(t + 1) * M], pr[:, t * M:(t + 1) * M],
                                              stat[:, 3 * TT + t:3 * TT + t + 1], None, ALU.mult)\
                               .then_inc(V.sem, V.one(f"s{t}"))
                        for c in range(HC):
                            at = bass.ds(h * (HC * T) + c * T, T)
                            dve.wait_ge(A.sem, A.now(f"o{c}", h))
                            dve.tensor_tensor(a_lo[:, at], psum[:, c % 2, :], a_hi[:, at].bitcast(F32), ALU.subtract)\
                               .then_inc(V.sem, V.one(f"lo{c}"))
                    dve.wait_ge(V.sem, V.all(HEADS))

        project("xo", a_hi, a_lo, x_hi, x_lo)
        layer_norm("ln2", "g2", "be2")

        xctx.close()
        pctx = wctx.enter_context(ExitStack())
        sums = sb("pick_sums", [P, TT * HK], ctx=pctx)
        key1 = sb("pick_key1", [P, TT * HK], ctx=pctx)
        key2 = sb("pick_key2", [P, TT * HK], ctx=pctx)
        sctx = ExitStack()
        scores = sb("scores", [P, TT * 2 * PH * NK], ctx=sctx)
        with ExitStack() as ctx:
            qt = sb("expert_q", [P, PH * T], ctx=ctx)
            keys = sb("sub_keys", [P, NK], ctx=ctx)
            A = Steps(sem("pq_act", ctx), "q0 q1")
            E = sem("pq_scores", ctx)
            S = sem("pq_scores_copied", ctx)
            keys_in = sem("keys_in", ctx)
            with nc.Block() as block:
                @block.sync
                def _(sp):
                    sp.dma_start(keys[:, :], keys_t).then_inc(keys_in, 16)
                    loads(sp, "pq", PH)

                @block.gpsimd
                def _(pool):
                    splits(pool, "pq", PH, hi_by_act=True)

                @block.tensor
                def _(pe):
                    with pe.Fori(0, PH // 2) as i:
                        for b in range(2):
                            pe.wait_ge(A.sem, A.before(f"q{b}", i))
                            gemm(pe, b, a_hi, a_lo, i * 4 + (BASE["pq"] + 2 * b))
                    pe.wait_ge(keys_in, 16)
                    pe.wait_ge(A.sem, A.all(PH // 2))
                    for t in range(TT):
                        if t:
                            pe.wait_ge(S, t)
                        for h in range(PH):
                            for j in range(2):
                                half = slice(j * PKH, (j + 1) * PKH)
                                ins = pe.matmul(psum[:, 2 + 2 * j + h // 4, (h % 4) * P:(h % 4 + 1) * P],
                                                qt[half, h * T + t * P:h * T + (t + 1) * P], keys[half, :],
                                                start=True, stop=True)
                        ins.then_inc(E, 1)

                @block.scalar
                def _(act):
                    act.sem_inc(A.sem, 2)
                    with act.Fori(0, PH // 2) as i:
                        for b in range(2):
                            his(act, "pq", i, b)
                            hold(act, used, i * 4 + (BASE["pq"] + 2 * b + 4))
                            act.activation(qt[:, bass.ds(i * (2 * T) + b * T, T)], psum[:, b, :], ACT.Copy)\
                               .then_inc(A.sem, A.one(f"q{b}"))

                @block.vector
                def _(dve):
                    for t in range(TT):
                        dve.wait_ge(E, t + 1)
                        dve.tensor_copy(scores[:, t * D:(t + 1) * D].rearrange("p (b n) -> p b n", b=4),
                                        psum[:, 2:6, :]).then_inc(S, 1)
                    dve.wait_ge(S, TT)

        class Up:

            def __init__(self, name, ctx):
                self.name = name
                self.h = [sb(f"{name}_h{b}", [P, T], ctx=ctx) for b in range(2)]
                self.q = [sb(f"{name}_q{b}", [P, T], ctx=ctx) for b in range(2)]
                self.A = Steps(sem(f"{name}_up_act", ctx), "h0 h1 th0 th1")
                self.V = Steps(sem(f"{name}_up_dve", ctx), "square0 square1 poly0 poly1 arg0 arg1 gelu0 gelu1")
                self.sent = [sem(f"{name}_sent{b}", ctx) for b in range(2)]

            def start_act(self, act):
                act.sem_inc(self.A.sem, len(self.A.names))
                for b in range(2):
                    act.sem_inc(self.sent[b], 16)

            def start_dve(self, dve):
                dve.sem_inc(self.V.sem, len(self.V.names))

            def dots(self, pe, b, i):
                pe.wait_ge(self.A.sem, self.A.before(f"h{b}", i))
                gemm(pe, b, a_hi, a_lo, i * 4 + (BASE[self.name] + 2 * b))

            def copy(self, act, b, i):
                hold(act, self.sent[b], i * 16 + 16)
                hold(act, used, i * 4 + (BASE[self.name] + 2 * b + 4))
                act.activation(self.h[b][:, :], psum[:, b, :], ACT.Copy).then_inc(self.A.sem, self.A.one(f"h{b}"))

            def tanh_and_store(self, act, i, first_chunk):
                for b in range(2):
                    act.wait_ge(self.V.sem, self.V.now(f"arg{b}", i))
                    act.activation(self.q[b][:, :], self.q[b][:, :], ACT.Tanh, scale=GELU_C)\
                       .then_inc(self.A.sem, self.A.one(f"th{b}"))
                for b in range(2):
                    hold(act, self.V.sem, self.V.now(f"gelu{b}", i))
                    act.dma_start(act_d[bass.ds(i * 2 + (first_chunk + b), 1)].rearrange("a p n -> (a p) n"),
                                  self.h[b][:, :]).then_inc(self.sent[b], 16)

            def gelu(self, dve, i):
                V, A = self.V, self.A
                for b in range(2):
                    dve.wait_ge(A.sem, A.now(f"h{b}", i))
                    dve.wait_ge(V.sem, V.before(f"gelu{b}", i))
                    dve.tensor_tensor(self.q[b][:, :], self.h[b][:, :], self.h[b][:, :], ALU.mult)\
                       .then_inc(V.sem, V.one(f"square{b}"))
                for b in range(2):
                    dve.wait_ge(V.sem, V.now(f"square{b}", i))
                    dve.tensor_scalar(self.q[b][:, :], self.q[b][:, :], 0.044715, 1.0, ALU.mult, ALU.add)\
                       .then_inc(V.sem, V.one(f"poly{b}"))
                for b in range(2):
                    dve.wait_ge(V.sem, V.now(f"poly{b}", i))
                    dve.tensor_tensor(self.q[b][:, :], self.q[b][:, :], self.h[b][:, :], ALU.mult)\
                       .then_inc(V.sem, V.one(f"arg{b}"))
                for b in range(2):
                    dve.wait_ge(A.sem, A.now(f"th{b}", i))
                    dve.wait_ge(V.sem, V.now(f"arg{b}", i))
                    dve.scalar_tensor_tensor(self.h[b][:, :], self.q[b][:, :], 1.0, self.h[b][:, :], ALU.add, ALU.mult)\
                       .then_inc(V.sem, V.one(f"gelu{b}"))

            def finish(self, act, n):
                for b in range(2):
                    act.wait_ge(self.sent[b], (n + 1) * 16)

        UP = ECH // 4
        SLOTS = UP // TT
        with ExitStack() as ctx:
            up = Up("pick", ctx)
            wide = PH * TOPK * TOPK
            st = sb("pick_scores", [P, D], ctx=ctx)[:, :]
            cand = sb("pick_cand", [P, wide], ctx=ctx)[:, :]
            eq = st
            small = sb("pick_small", [P, 1600], ctx=ctx)
            s16, i16 = small[:, 0:256], small[:, 256:512]
            best, posf1, posf2 = small[:, 512:640], small[:, 640:768], small[:, 768:896]
            usmall = sb("pick_index", [P, 640], U32, ctx=ctx)
            i16u, posu = usmall[:, 0:256], usmall[:, 256:384]
            hiu, lou = usmall[:, 384:512], usmall[:, 512:640]
            chain = sem("pick_chain", ctx)
            assert SLOTS == 8

            def heads(v):
                return v.rearrange("p (h k) -> p h k", h=PH)

            with nc.Block() as block:
                @block.sync
                def _(sp):
                    loads(sp, "pick", ECH // 2)

                @block.gpsimd
                def _(pool):
                    splits(pool, "pick", ECH // 2)

                @block.tensor
                def _(pe):
                    with pe.Fori(0, UP) as i:
                        for b in range(2):
                            up.dots(pe, b, i)

                @block.scalar
                def _(act):
                    up.start_act(act)
                    with act.Fori(0, UP) as i:
                        for b in range(2):
                            up.copy(act, b, i)
                        up.tanh_and_store(act, i, 0)
                    up.finish(act, UP)

                @block.vector
                def _(dve):
                    up.start_dve(dve)
                    with dve.Fori(0, TT) as t:
                        n = 0

                        def done(ins):
                            nonlocal n
                            n += 1
                            ins.then_inc(chain, 1)
                            hold(dve, chain, t * PICK_STEPS + n)

                        def top16(searches):
                            nonlocal n
                            for k in range(2):
                                for what in ("max", "index", "drop"):
                                    if k and what == "drop":
                                        continue
                                    for v, s_out, i_out in searches:
                                        s8, i8 = s_out[:, 8 * k:8 * k + 8], i_out[:, 8 * k:8 * k + 8]
                                        if what == "max":
                                            ins = dve.max(s8, v)
                                        elif what == "index":
                                            ins = dve.max_index(i8, s8, v)
                                        else:
                                            ins = dve.match_replace(v, s8, v, -3.0e38)
                                        ins.then_inc(chain, 1)
                                        n += 1
                                    hold(dve, chain, t * PICK_STEPS + n)

                        for k in range(SLOTS):
                            if k == 0:
                                done(dve.tensor_copy(st, scores[:, bass.ts(t, D)]))
                            if k < 4:
                                top16([(st[:, g * NK:(g + 1) * NK], s16[:, g * TOPK:(g + 1) * TOPK],
                                        i16u[:, g * TOPK:(g + 1) * TOPK]) for g in range(4 * k, 4 * k + 4)])
                            if k == 4:
                                done(dve.tensor_copy(i16, i16u))
                                for h in range(PH):
                                    s1 = s16[:, h * TOPK:(h + 1) * TOPK]
                                    s2 = s16[:, (PH + h) * TOPK:(PH + h + 1) * TOPK]
                                    done(dve.tensor_tensor(
                                        cand[:, h * 256:(h + 1) * 256].rearrange("p (i j) -> p i j", i=TOPK),
                                        s1.unsqueeze(2).to_broadcast([P, TOPK, TOPK]),
                                        s2.unsqueeze(1).to_broadcast([P, TOPK, TOPK]), ALU.add))
                            if k in (5, 6):
                                top16([(cand[:, h * 256:(h + 1) * 256], best[:, h * TOPK:(h + 1) * TOPK],
                                        posu[:, h * TOPK:(h + 1) * TOPK]) for h in range((k - 5) * 4, (k - 5) * 4 + 4)])
                            if k == 7:
                                done(dve.tensor_scalar(hiu, posu, 4, None, ALU.logical_shift_right))
                                done(dve.tensor_scalar(lou, posu, 15, None, ALU.bitwise_and))
                                done(dve.tensor_copy(posf1, hiu))
                                done(dve.tensor_copy(posf2, lou))
                                for pos, lst, key in ((posf1, i16[:, 0:HK], key1), (posf2, i16[:, HK:2 * HK], key2)):
                                    v4 = lambda v: v.rearrange("p (h k i) -> p h k i", h=PH, k=TOPK)
                                    done(dve.tensor_tensor(
                                        v4(eq), heads(pos).unsqueeze(3).to_broadcast([P, PH, TOPK, TOPK]),
                                        iota_k[:, 0:TOPK].unsqueeze(1).unsqueeze(1).to_broadcast([P, PH, TOPK, TOPK]),
                                        ALU.is_equal))
                                    done(dve.tensor_tensor(
                                        v4(eq), v4(eq), heads(lst).unsqueeze(2).to_broadcast([P, PH, TOPK, TOPK]),
                                        ALU.mult))
                                    done(dve.tensor_reduce(key[:, bass.ts(t, HK)],
                                                           eq.rearrange("p (m i) -> p m i", i=TOPK), AX_X, ALU.add))
                                done(dve.tensor_tensor(heads(sums[:, bass.ts(t, HK)]), heads(best),
                                                       heads(best)[:, :, 0:1].to_broadcast([P, PH, TOPK]), ALU.subtract))
                            up.gelu(dve, t * SLOTS + k)
                        assert n == PICK_STEPS, n
                    dve.wait_ge(up.V.sem, up.V.all(UP))

        sctx.close()
        tctx = wctx.enter_context(ExitStack())
        turned = [sb(f"turned_{n}", [P, T], ctx=tctx) for n in ("key1", "key2", "gate_hi", "gate_lo")]
        with ExitStack() as ctx:
            tot, rec = (sb(f"soft_{n}", [P, TT * PH], ctx=ctx) for n in ("tot", "rec"))
            s_exp, s_dve, s_pe, s_hi = (sem(f"soft_{n}", ctx) for n in ("exp", "dve", "turned", "copied"))
            with nc.Block() as block:
                @block.scalar
                def _(act):
                    act.activation(sums[:, :], sums[:, :], ACT.Exp).then_inc(s_exp, 1)
                    for k in range(2):
                        act.wait_ge(s_pe, k + 1)
                        act.activation(turned[k][:, :], psum[:, 2 + k, :], ACT.Copy).then_inc(s_hi, 1)
                    act.wait_ge(s_pe, 3)
                    act.activation(turned[2][:, :].bitcast(F32R), psum[:, 4, :], ACT.Copy).then_inc(s_hi, 1)

                @block.vector
                def _(dve):
                    dve.wait_ge(s_exp, 1)
                    v = sums[:, :].rearrange("p (m k) -> p m k", k=TOPK)
                    dve.tensor_reduce(tot[:, :], v, AX_X, ALU.add).then_inc(s_dve, 1)
                    dve.wait_ge(s_dve, 1)
                    dve.tensor_scalar(tot[:, :], tot[:, :], 2.0, None, ALU.mult).then_inc(s_dve, 1)
                    dve.wait_ge(s_dve, 2)
                    dve.reciprocal(rec[:, :], tot[:, :]).then_inc(s_dve, 1)
                    dve.wait_ge(s_dve, 3)
                    dve.tensor_tensor(v, v, rec[:, :].unsqueeze(2).to_broadcast([P, TT * PH, TOPK]), ALU.mult)\
                       .then_inc(s_dve, 1)
                    dve.wait_ge(s_hi, 3)
                    dve.tensor_tensor(turned[3][:, :], psum[:, 4, :], turned[2][:, :], ALU.subtract).then_inc(s_dve, 1)
                    dve.wait_ge(s_dve, 5)

                @block.tensor
                def _(pe):
                    for k, v in enumerate((key1, key2, sums)):
                        if k == 2:
                            pe.wait_ge(s_dve, 4)
                        for t in range(TT):
                            ins = pe.transpose(psum[:, 2 + k, t * P:(t + 1) * P], v[:, t * P:(t + 1) * P], ident[:, :])
                        ins.then_inc(s_pe, 1)

        NB = 8
        BLOCKS = T // GT
        PB = GT // (2 * NB)
        assert BLOCKS * PB == UP
        with ExitStack() as ctx:
            up = Up("gates", ctx)
            hot2 = sb("hot_second", [P, NB * P], F32R, ctx=ctx)
            hot1g = sb("hot_first_gated", [P, 2 * NB * P], F32R, ctx=ctx)
            hot1 = sb("hot_first", [P, NB * P], ctx=ctx)
            stage = sb("gate_stage", [P, ECH * GT], ctx=ctx)
            H = Steps(sem("hot_dve", ctx), "second0 first0 hi0 lo0 second1 first1 hi1 lo1")
            E = Steps(sem("hot_pe", ctx), "spread0 spread1")
            C = Steps(sem("hot_hi_copied", ctx), "copy0 copy1")
            J = Steps(sem("hot_lo_added", ctx), "add0 add1")
            spread = psum[:, 2:6, :].rearrange("p k (t h e) -> p (k t) h e", h=2, e=P)

            def staged(k, b):
                return stage[:, :].rearrange("p (e t) -> p t e", t=GT)[:, bass.ds(k * (2 * NB) + NB * b, NB), :]

            gate_sent = sem("gate_sent", ctx)
            with nc.Block() as block:
                @block.sync
                def _(sp):
                    loads(sp, "gates", ECH // 2)

                @block.gpsimd
                def _(pool):
                    splits(pool, "gates", ECH // 2)

                @block.tensor
                def _(pe):
                    pe.sem_inc(E.sem, 2)
                    with pe.Fori(0, UP) as i:
                        for b in range(2):
                            up.dots(pe, b, i)
                            pe.wait_ge(H.sem, H.now(f"lo{b}", i))
                            pe.wait_ge(J.sem, J.now("add0", i) if b else J.before("add1", i))
                            for j in range(NB):
                                ins = pe.matmul(psum[:, 2 + j // 2, (j % 2) * 2 * P:(j % 2 + 1) * 2 * P],
                                                hot2[:, j * P:(j + 1) * P], hot1g[:, j * 2 * P:(j + 1) * 2 * P],
                                                start=True, stop=True)
                            ins.then_inc(E.sem, E.one(f"spread{b}"))

                @block.scalar
                def _(act):
                    up.start_act(act)
                    act.sem_inc(C.sem, 2)
                    act.sem_inc(gate_sent, 16)
                    with act.Fori(0, BLOCKS) as blk:
                        with act.Fori(0, PB) as k:
                            i = blk * PB + k
                            for b in range(2):
                                up.copy(act, b, i)
                                if b == 0:
                                    hold(act, gate_sent, blk * 16 + 16)
                                hold(act, E.sem, E.now(f"spread{b}", i))
                                act.activation(staged(k, b), spread[:, :, 0, :], ACT.Copy)\
                                   .then_inc(C.sem, C.one(f"copy{b}"))
                            up.tanh_and_store(act, i, ECH // 2)
                        hold(act, J.sem, blk * (2 * PB) + (2 * PB + 2))
                        act.dma_start(gate_d[bass.ds(blk, 1)].rearrange("a p e t -> (a p) (e t)"), stage[:, :])\
                           .then_inc(gate_sent, 16)
                    up.finish(act, UP)
                    act.wait_ge(gate_sent, (BLOCKS + 1) * 16)

                @block.vector
                def _(dve):
                    up.start_dve(dve)
                    dve.sem_inc(H.sem, len(H.names))
                    shape = [P, NB, P]
                    v3 = lambda v: v.rearrange("p (t e) -> p t e", e=P)
                    keys = iota_k[:, :].unsqueeze(1).to_broadcast(shape)
                    dve.sem_inc(J.sem, 2)
                    gated = hot1g[:, :].rearrange("p (t h e) -> p t h e", h=2, e=P)
                    with dve.Fori(0, BLOCKS) as blk:
                        with dve.Fori(0, PB) as k:
                            i = blk * PB + k

                            def add(b):
                                dve.wait_ge(C.sem, C.now(f"copy{b}", i))
                                dve.tensor_tensor(staged(k, b), staged(k, b), spread[:, :, 1, :], ALU.add)\
                                   .then_inc(J.sem, J.one(f"add{b}"))

                            for b in range(2):
                                def of(v):
                                    return v[:, bass.ds(i * (2 * NB) + NB * b, NB)].unsqueeze(2).to_broadcast(shape)

                                k1, k2, g_hi, g_lo = turned
                                dve.wait_ge(E.sem, E.now("spread0", i) if b else E.before("spread1", i))
                                dve.tensor_tensor(v3(hot2[:, :]), keys, of(k2), ALU.is_equal)\
                                   .then_inc(H.sem, H.one(f"second{b}"))
                                dve.wait_ge(H.sem, H.now("lo0", i) if b else H.before("lo1", i))
                                dve.tensor_tensor(v3(hot1[:, :]), keys, of(k1), ALU.is_equal)\
                                   .then_inc(H.sem, H.one(f"first{b}"))
                                dve.wait_ge(H.sem, H.now(f"first{b}", i))
                                dve.tensor_tensor(gated[:, :, 0, :], v3(hot1[:, :]), of(g_hi), ALU.mult)\
                                   .then_inc(H.sem, H.one(f"hi{b}"))
                                dve.tensor_tensor(gated[:, :, 1, :], v3(hot1[:, :]), of(g_lo), ALU.mult)\
                                   .then_inc(H.sem, H.one(f"lo{b}"))
                            add(0)
                            up.gelu(dve, i)
                            add(1)
                    dve.wait_ge(up.V.sem, up.V.all(UP))
                    dve.wait_ge(H.sem, H.all(UP))
                    dve.wait_ge(J.sem, J.all(UP))

        tctx.close()
        pctx.close()

        with ExitStack() as ctx:
            NQ = KC // 4
            acts = [sb(f"first_acts{b}", [P, NQ * T], ctx=ctx) for b in range(4)]
            gates = [sb(f"first_gates{b}", [P, NQ * T], ctx=ctx) for b in range(4)]
            come = [sem(f"first_in{b}", ctx) for b in range(4)]
            mul, hi, lo = (sem(f"first_{n}", ctx) for n in ("mul", "hi", "lo"))
            with nc.Block() as block:
                @block.sync
                def _(sp):
                    for q in range(4):
                        sp.dma_start(acts[q][:, :].rearrange("p (a n) -> p a n", a=NQ),
                                     act_d[q * NQ:(q + 1) * NQ].rearrange("a p n -> p a n")).then_inc(come[q], 16)
                        sp.dma_start(gates[q][:, :].rearrange("p (k e t) -> p k e t", e=NQ, t=GT),
                                     gate_d[:, :, q * NQ:(q + 1) * NQ, :].rearrange("k p e t -> p k e t"))\
                          .then_inc(come[q], 16)

                @block.scalar
                def _(act):
                    for q in range(4):
                        act.wait_ge(mul, q + 1)
                        act.activation(a_hi[:, q * NQ * T:(q + 1) * NQ * T], acts[q][:, :], ACT.Copy).then_inc(hi, 1)

                @block.vector
                def _(dve):
                    def rest(q):
                        dve.wait_ge(hi, q + 1)
                        at = slice(q * NQ * T, (q + 1) * NQ * T)
                        dve.tensor_tensor(a_lo[:, at], acts[q][:, :], a_hi[:, at].bitcast(F32), ALU.subtract)\
                           .then_inc(lo, 1)

                    for q in range(4):
                        dve.wait_ge(come[q], 32)
                        v = acts[q][:, :].rearrange("p (e k t) -> p e k t", e=NQ, t=GT)
                        dve.tensor_tensor(v, v, gates[q][:, :].rearrange("p (k e t) -> p e k t", e=NQ, t=GT), ALU.mult)\
                           .then_inc(mul, 1)
                        if q:
                            rest(q - 1)
                    rest(3)
                    dve.wait_ge(lo, 4)

        with ExitStack() as ctx:
            b_hi = sb("b_hi", [P, KC * T], F32R, ctx=ctx)
            b_lo = sb("b_lo", [P, KC * T], F32R, ctx=ctx)
            ah, ag = sb("down_acts", [P, 2 * T], ctx=ctx), work
            V = Steps(sem("down_prep", ctx), "mul0 mul1 lo0 lo1")
            A = Steps(sem("down_hi", ctx), "hi0 hi1")
            S = Steps(sem("down_sum", ctx), "sum0 sum1")
            SQ = Steps(sem("last_squared", ctx), "sq0 sq1")
            TO = Steps(sem("last_totals", ctx), "total0 square0 total1 square1")
            come = sem("down_in", ctx)
            setup = sem("down_setup", ctx)
            NP = KC // 2
            pair = [(a_hi, a_lo), (b_hi, b_lo)]

            def groups(body):
                def run(eng):
                    with eng.Fori(0, EG // 2 - 1) as gg:
                        for parity in range(2):
                            body(eng, gg * 2 + parity, parity, True)
                    body(eng, EG - 2, 0, True)
                    body(eng, EG - 1, 1, False)
                return run

            with nc.Block() as block:
                @block.sync
                def _(sp):
                    def fetch(sp, j):
                        hold(sp, V.sem, V.before("lo1", j))
                        sp.dma_start(ah[:, :].rearrange("p (b n) -> p b n", b=2),
                                     act_d[bass.ds(j * 2 + KC, 2)].rearrange("b p n -> p b n")).then_inc(come, 16)
                        sp.dma_start(ag[:, :].rearrange("p (k b t) -> p k b t", b=2, t=GT),
                                     gate_d[:, :, bass.ds(j * 2 + KC, 2), :].rearrange("k p b t -> p k b t"))\
                          .then_inc(come, 16)

                    def body(sp, g, parity, prepare):
                        def one(i, more):
                            for s in range(4):
                                load_half(sp, i * 4 + (BASE["down"] + AHEAD_LOAD + s), s)
                                if s == 1 and more:
                                    fetch(sp, i + 1)

                        if isinstance(g, int):
                            with sp.Fori(0, NP - 1) as k:
                                one(k + g * NP, prepare)
                            if prepare:
                                one((g + 1) * NP - 1, False)
                        else:
                            with sp.Fori(0, NP) as k:
                                one(g * NP + k, True)

                    fetch(sp, 0)
                    groups(body)(sp)

                @block.gpsimd
                def _(pool):
                    splits(pool, "down", ECH, hi_by_act=True)

                @block.tensor
                def _(pe):
                    def body(pe, g, parity, prepare):
                        hold(pe, V.sem, g * (NP * 4) + 4)
                        with pe.Fori(0, NP) as k:
                            i = g * NP + k
                            for b in range(2):
                                pe.wait_ge(S.sem, S.before(f"sum{b}", i))
                                gemm(pe, b, *pair[parity], i * 4 + (BASE["down"] + 2 * b))
                    groups(body)(pe)

                @block.scalar
                def _(act):
                    act.sem_inc(A.sem, 2)
                    act.sem_inc(SQ.sem, 2)

                    def body(act, g, parity, prepare):
                        def square(k, b):
                            hold(act, TO.sem, TO.before(f"square{b}", k))
                            hold(act, S.sem, k * 2 + ((EG - 1) * NP * 2 + 2 + b + 1))
                            act.activation(ah[:, b * T:(b + 1) * T], res[:, bass.ds(k * (2 * T) + b * T, T)], ACT.Square)\
                               .then_inc(SQ.sem, SQ.one(f"sq{b}"))

                        def one(i, k, last=False):
                            if prepare:
                                for b in range(2):
                                    hold(act, V.sem, V.now(f"mul{b}", i))
                                    act.activation(pair[1 - parity][0][:, bass.ds(k * (2 * T) + b * T, T)],
                                                   ah[:, b * T:(b + 1) * T], ACT.Copy).then_inc(A.sem, A.one(f"hi{b}"))
                            for b in range(2):
                                if not (last and b):
                                    his(act, "down", i, b)
                                if not prepare:
                                    square(k, b)

                        if prepare:
                            with act.Fori(0, NP) as k:
                                one(g * NP + k, k)
                        else:
                            with act.Fori(0, NP - 1) as k:
                                one(k + g * NP, k)
                            one(g * NP + NP - 1, NP - 1, last=True)
                    groups(body)(act)

                @block.vector
                def _(dve):
                    dve.sem_inc(V.sem, 4)
                    dve.sem_inc(S.sem, 2)
                    dve.sem_inc(TO.sem, 4)
                    dve.tensor_scalar(res[:, :], res[:, :], ALPHA, None, ALU.mult).then_inc(setup, 1)
                    dve.memset(total[:, :], 0.0).then_inc(setup, 1)
                    dve.memset(total2[:, :], 0.0).then_inc(setup, 1)
                    dve.wait_ge(setup, 3)

                    def prep(i, k, to):
                        dve.wait_ge(come, i * 32 + 32)
                        for b in range(2):
                            a = ah[:, b * T:(b + 1) * T].rearrange("p (k t) -> p k t", t=GT)
                            gate = ag[:, :].rearrange("p (k b t) -> p b k t", b=2, t=GT)[:, b]
                            dve.tensor_tensor(a, a, gate, ALU.mult).then_inc(V.sem, V.one(f"mul{b}"))
                        for b in range(2):
                            at = bass.ds(k * (2 * T) + b * T, T)
                            dve.wait_ge(V.sem, V.now(f"mul{b}", i))
                            dve.wait_ge(A.sem, A.now(f"hi{b}", i))
                            dve.tensor_tensor(to[1][:, at], ah[:, b * T:(b + 1) * T], to[0][:, at].bitcast(F32),
                                              ALU.subtract).then_inc(V.sem, V.one(f"lo{b}"))

                    def body(dve, g, parity, prepare):
                        hold(dve, S.sem, g * (NP * 2) + 2)
                        with dve.Fori(0, NP) as k:
                            i = g * NP + k
                            if prepare:
                                prep(i, k, pair[1 - parity])
                            for b in range(2):
                                r = res[:, bass.ds(k * (2 * T) + b * T, T)]
                                dve.wait_ge(used, i * 4 + (BASE["down"] + 2 * b + 4))
                                dve.tensor_tensor(r, r, psum[:, b, :], ALU.add).then_inc(S.sem, S.one(f"sum{b}"))
                                if not prepare:
                                    dve.wait_ge(S.sem, S.now(f"sum{b}", i))
                                    dve.wait_ge(TO.sem, TO.now("total0", k) if b else TO.before("total1", k))
                                    dve.tensor_tensor(total[:, :], total[:, :], r, ALU.add)\
                                       .then_inc(TO.sem, TO.one(f"total{b}"))
                                    dve.wait_ge(SQ.sem, SQ.now(f"sq{b}", k))
                                    dve.wait_ge(TO.sem, TO.now("square0", k) if b else TO.before("square1", k))
                                    dve.tensor_tensor(total2[:, :], total2[:, :], ah[:, b * T:(b + 1) * T], ALU.add)\
                                       .then_inc(TO.sem, TO.one(f"square{b}"))
                    groups(body)(dve)
                    dve.wait_ge(TO.sem, TO.all(NP))
                    dve.wait_ge(S.sem, S.all(EG * NP))

        layer_norm("ln3", "g3", "be3", turned_out=out)




_OUT = (1, T, D)


def kernel(**inputs):
    import numpy as np
    import concourse.bacc as bacc
    from concourse.bass_utils import run_bass_kernel_spmd as run

    a = {k: np.asarray(v) for k, v in inputs.items()}

    def chunks(w):
        n = w.shape[1] // P
        return w.reshape(2, HALF, P, n, P).transpose(3, 0, 2, 1, 4).reshape(n, 2, P, WH)

    def pairs(u, v):
        return np.stack([chunks(u), chunks(v)], axis=1).reshape(-1, 2, P, WH)

    w = a["w_in"][0]
    xr, gr, ca, cg, g_rnn, g_conf = (w[:, i * D:(i + 1) * D] for i in range(6))
    stream = np.concatenate([
        pairs(cg, ca), chunks(g_conf), chunks(a["w_conf_out"][0]),
        pairs(xr, gr), pairs(g_rnn, a["w_rnn_out"][0]), chunks(a["w_mix_out"][0]), chunks(a["xa_w_k"][0]),
        chunks(a["xa_w_v"][0]), chunks(a["xa_w_q"][0]), chunks(a["xa_w_o"][0]), chunks(a["peer_w_q"][0]),
        chunks(a["peer_u"][0].T),
        *[chunks(a["peer_v"][0][g * D:(g + 1) * D]) for g in range(EG)]]).reshape(-1, P, WH)

    def cols(v):
        return v.reshape(-1, P).T

    vecs = np.ascontiguousarray(np.concatenate([
        cols(a[n][0]) for n in ("b_in", "rnn_conv_w", "rnn_conv_b", "rnn_b_a", "rnn_b_x", "rnn_lambda", "conf_dw_w",
                                "conf_dw_b", "conf_ln_g", "conf_ln_b", "b_conf_out", "ln1_g", "ln1_b", "ln2_g",
                                "ln2_b", "ln3_g", "ln3_b")], axis=1))

    def turned(v):
        t = v.reshape(v.shape[0], KC, P)
        return np.ascontiguousarray(t.transpose(2, 1, 0)).reshape(P, -1)

    arrays = {
        "wstream": stream,
        "x_t": turned(a["x"][0]),
        "mem_t": turned(a["mem"][0]),
        "vecs": vecs,
        "gates_w": np.ascontiguousarray(np.concatenate([a["rnn_w_a"][0], a["rnn_w_x"][0]], axis=2)),
        "ident_d": np.eye(P, dtype=np.float32),
        "keys_t": np.ascontiguousarray(a["peer_sub_keys"][0].transpose(0, 2, 1)).reshape(P, NK),
    }
    nc = bacc.Bacc("TRN2", target_bir_lowering=False, num_devices=1)
    args = [nc.dram_tensor(n, v.shape, F32, kind="ExternalInput").ap() for n, v in arrays.items()]
    o = nc.dram_tensor("out", (TT, P, D), F32, kind="ExternalOutput").ap()
    build(nc, *args, o)
    r = run(nc, [arrays], core_ids=[0])
    return r.results[0]["out"].reshape(_OUT)
```
